# Optimizing a Trainium2 kernel written in Bass

```python
import math
import jax, jax.numpy as jnp
from jax import lax
import numpy as np
import jax
import jax.numpy as jnp

D_MODEL = 1024
BATCH = 1
SEQ = 512
DEPTH = 2

N_A = DEPTH // 2
N_B = DEPTH - N_A
POOL_WINDOWS = (2, 4, 8, 16)
N_POOL_GROUPS = len(POOL_WINDOWS)
GROUP_CH = D_MODEL // N_POOL_GROUPS
HEAD_DIM = 64
N_Q_HEADS = D_MODEL // HEAD_DIM
N_KV_HEADS = 4
Q_PER_KV = N_Q_HEADS // N_KV_HEADS
WINDOW = 128
BLOCK = 128
ROPE_THETA = 10000.0
ATTN_SCALE = 1.0 / math.sqrt(HEAD_DIM)
NEG_INF = -1e30
D_FF = 2816
CONV_WIDTH = 3
RMS_EPS = 1e-6


def rms_norm(x, g):
    xf = x.astype(jnp.float32)
    y = xf * lax.rsqrt(jnp.mean(xf * xf, axis=-1, keepdims=True) + RMS_EPS)
    return (y * g.astype(jnp.float32)).astype(x.dtype)

def pool_mixer(h, w_pool, scale):
    B, S, D = h.shape
    hf = h.astype(jnp.float32)
    csum = jnp.concatenate([jnp.zeros((B, 1, D), jnp.float32), jnp.cumsum(hf, axis=1)], axis=1)
    t = jnp.arange(1, S + 1)
    diffs = []
    for gi, w in enumerate(POOL_WINDOWS):
        sl = slice(gi * GROUP_CH, (gi + 1) * GROUP_CH)
        lo = jnp.maximum(t - w, 0)
        cnt = jnp.minimum(t, w).astype(jnp.float32)
        mean = (csum[:, 1:, sl] - csum[:, lo, sl]) / cnt[None, :, None]
        diffs.append(mean - hf[..., sl])
    d = jnp.stack(diffs, axis=2).astype(h.dtype)
    y = jnp.einsum('bsgc,gcd->bsgd', d, w_pool).reshape(B, S, D)
    return y * scale

def conv_glu_ffn(h, w_in, conv_w, conv_b, w_out):
    S = h.shape[1]
    u = h @ w_in
    up = jnp.pad(u, ((0, 0), (CONV_WIDTH - 1, 0), (0, 0)))
    u = sum(conv_w[k] * up[:, k:k + S] for k in range(CONV_WIDTH)) + conv_b
    gate, val = jnp.split(u, 2, axis=-1)
    return (jax.nn.gelu(gate, approximate=True) * val) @ w_out

def rope(x, cos, sin):
    xf = x.astype(jnp.float32)
    x1, x2 = jnp.split(xf, 2, axis=-1)
    return jnp.concatenate([x1 * cos - x2 * sin, x2 * cos + x1 * sin], axis=-1).astype(x.dtype)

def rope_tables(positions):
    inv_freq = 1.0 / (ROPE_THETA ** (jnp.arange(0, HEAD_DIM, 2, dtype=jnp.float32) / HEAD_DIM))
    ang = positions.astype(jnp.float32)[..., None] * inv_freq
    return jnp.cos(ang)[:, :, None, :], jnp.sin(ang)[:, :, None, :]

def band_blocks(t):
    B, S = t.shape[:2]
    nb = S // BLOCK
    tb = t.reshape(B, nb, BLOCK, N_KV_HEADS, HEAD_DIM)
    prev = jnp.pad(tb, ((0, 0), (1, 0), (0, 0), (0, 0), (0, 0)))[:, :-1]
    return jnp.concatenate([prev, tb], axis=2).astype(jnp.float32)

def swa_sink_attention(q, kk, vv, sinks):
    B, S = q.shape[:2]
    nb = S // BLOCK
    qb = q.reshape(B, nb, BLOCK, N_KV_HEADS, Q_PER_KV, HEAD_DIM).astype(jnp.float32) * ATTN_SCALE
    s = jnp.einsum('bnqhgd,bnkhd->bnhgqk', qb, kk)
    qi = jnp.arange(BLOCK)[:, None]
    kj = jnp.arange(2 * BLOCK)[None, :]
    rel = BLOCK + qi - kj
    blk = jnp.arange(nb)[:, None, None]
    valid = (rel >= 0) & (rel < WINDOW) & (blk * BLOCK + kj - BLOCK >= 0)
    s = jnp.where(valid[None, :, None, None], s, NEG_INF)
    sink = sinks.astype(jnp.float32).reshape(N_KV_HEADS, Q_PER_KV)[None, None, :, :, None, None]
    m = jnp.maximum(jnp.max(s, axis=-1, keepdims=True), sink)
    p = jnp.exp(s - m)
    denom = jnp.sum(p, axis=-1) + jnp.exp(sink - m)[..., 0]
    o = jnp.einsum('bnhgqk,bnkhd->bnhgqd', p, vv) / denom[..., None]
    o = o.transpose(0, 1, 4, 2, 3, 5).reshape(B, S, N_Q_HEADS * HEAD_DIM)
    return o.astype(q.dtype)

def first_inputs(seed: int = 0) -> dict:
    key = jax.random.key(seed)
    ks = jax.random.split(key, 20)
    f32 = jnp.float32
    D, F = D_MODEL, D_FF
    HQD, HKVD = N_Q_HEADS * HEAD_DIM, N_KV_HEADS * HEAD_DIM

    def gain(k, shape):
        return 1.0 + 0.05 * jax.random.normal(k, shape, f32)

    x = jax.random.normal(ks[0], (BATCH, SEQ, D), f32)
    positions = jnp.broadcast_to(jnp.arange(SEQ, dtype=jnp.int32)[None, :], (BATCH, SEQ))
    return {
        "x": x,
        "positions": positions,
        "mix_pre_g": gain(ks[1], (DEPTH, D)),
        "mix_post_g": gain(ks[2], (DEPTH, D)),
        "pool_w": jax.random.normal(ks[3], (N_A, N_POOL_GROUPS, GROUP_CH, GROUP_CH), f32) * GROUP_CH ** -0.5,
        "pool_scale": 1.0 + 0.1 * jax.random.normal(ks[4], (N_A, D), f32),
        "kv_norm_g": gain(ks[5], (D,)),
        "w_kv": jax.random.normal(ks[6], (D, 2 * HKVD), f32) * D ** -0.5,
        "w_q": jax.random.normal(ks[7], (N_B, D, HQD), f32) * D ** -0.5,
        "w_o": jax.random.normal(ks[8], (N_B, HQD, D), f32) * HQD ** -0.5,
        "sinks": jax.random.normal(ks[9], (N_B, N_Q_HEADS), f32),
        "ffn_pre_g": gain(ks[10], (DEPTH, D)),
        "ffn_post_g": gain(ks[11], (DEPTH, D)),
        "ffn_w_in": jax.random.normal(ks[12], (DEPTH, D, 2 * F), f32) * D ** -0.5,
        "ffn_conv_w": jax.random.normal(ks[13], (DEPTH, CONV_WIDTH, 2 * F), f32) * CONV_WIDTH ** -0.5,
        "ffn_conv_b": 0.01 * jax.random.normal(ks[14], (DEPTH, 2 * F), f32),
        "ffn_w_out": jax.random.normal(ks[15], (DEPTH, F, D), f32) * F ** -0.5,
    }

def first_block(x, positions, mix_pre_g, mix_post_g, pool_w, pool_scale, kv_norm_g, w_kv,
              w_q, w_o, sinks, ffn_pre_g, ffn_post_g, ffn_w_in, ffn_conv_w, ffn_conv_b, ffn_w_out):
    B, S, D = x.shape
    cos, sin = rope_tables(positions)
    kk = vv = None
    for layer in range(DEPTH):
        h = rms_norm(x, mix_pre_g[layer])
        if layer < N_A:
            m = pool_mixer(h, pool_w[layer], pool_scale[layer])
        else:
            if layer == N_A:
                hkv = rms_norm(x, kv_norm_g)
                kv = (hkv @ w_kv).reshape(B, S, 2, N_KV_HEADS, HEAD_DIM)
                k_shared = rope(kv[:, :, 0], cos, sin)
                kk, vv = band_blocks(k_shared), band_blocks(kv[:, :, 1])
            j = layer - N_A
            q = rope((h @ w_q[j]).reshape(B, S, N_Q_HEADS, HEAD_DIM), cos, sin)
            m = swa_sink_attention(q, kk, vv, sinks[j]) @ w_o[j]
        x = x + rms_norm(m, mix_post_g[layer])
        f = conv_glu_ffn(rms_norm(x, ffn_pre_g[layer]), ffn_w_in[layer], ffn_conv_w[layer],
                         ffn_conv_b[layer], ffn_w_out[layer])
        x = x + rms_norm(f, ffn_post_g[layer])
    return x


N_MIXERS = 2
N_A_LAYERS = (DEPTH + 1) // 2
N_B_LAYERS = DEPTH // 2
NORM_EPS = 1e-5
D_FF_2 = 4 * D_MODEL
N_MOD = 6

S5_WIDTH = D_MODEL
S5_GROUP = 16
S5_GROUPS = S5_WIDTH // S5_GROUP
S5_STATE = 64
S5_CHUNK = 128
S5_DT_MIN = 0.001
S5_DT_MAX = 0.1

M2_D_INNER = 2 * D_MODEL
M2_HEADDIM = 64
M2_HEADS = M2_D_INNER // M2_HEADDIM
M2_GROUPS = 4
M2_HPG = M2_HEADS // M2_GROUPS
M2_STATE = 128
M2_CONV = 4
M2_CHUNK = 128
M2_CONV_DIM = M2_D_INNER + 2 * M2_GROUPS * M2_STATE
M2_IN_DIM = M2_D_INNER + M2_CONV_DIM + M2_HEADS
M2_DT_MIN = 0.001
M2_DT_MAX = 0.1


def _rmsnorm(x, g):
    xf = x.astype(jnp.float32)
    y = xf * lax.rsqrt(jnp.mean(xf * xf, axis=-1, keepdims=True) + NORM_EPS)
    return (y * g.astype(jnp.float32)).astype(x.dtype)

def _modulate(h, shift, scale):
    return h * (1 + scale) + shift

def _sq_relu_mlp(h, w1, w2):
    a = jax.nn.relu(h @ w1)
    return (a * a) @ w2

def _s5_combine(e1, e2):
    a1, b1 = e1
    a2, b2 = e2
    return a2 * a1, a2 * b1 + b2

def _s5_mixer(h, w_in, lam_re, lam_im, log_dt, b_re, b_im, c_re, c_im, d, w_glu, b_glu):
    f32 = jnp.float32
    bsz, L, _ = h.shape
    nc = L // S5_CHUNK
    u = (h @ w_in).astype(f32)
    lam = lax.complex(lam_re.astype(f32), lam_im.astype(f32))
    dt = jnp.exp(log_dt.astype(f32))[:, None]
    lam_dt = lam * dt
    lam_bar = jnp.exp(lam_dt)
    b_bar = ((lam_bar - 1) / lam)[..., None] * lax.complex(b_re.astype(f32), b_im.astype(f32))
    c_mat = lax.complex(c_re.astype(f32), c_im.astype(f32))
    steps = jnp.arange(1, S5_CHUNK + 1, dtype=f32)[:, None, None]
    a_pow = jnp.exp(lam_dt[None] * steps)
    a_elems = jnp.broadcast_to(lam_bar, (bsz, S5_CHUNK, S5_GROUPS, S5_STATE))
    u_blocks = u.reshape(bsz, nc, S5_CHUNK, S5_GROUPS, S5_GROUP).transpose(1, 0, 2, 3, 4)

    def block_step(carry, u_blk):
        bu = jnp.einsum('btgh,gph->btgp', u_blk.astype(jnp.complex64), b_bar)
        _, hs = lax.associative_scan(_s5_combine, (a_elems, bu), axis=1)
        hs = hs + a_pow[None] * carry[:, None]
        y = jnp.einsum('btgp,ghp->btgh', hs, c_mat).real
        return hs[:, -1], y

    carry0 = jnp.zeros((bsz, S5_GROUPS, S5_STATE), jnp.complex64)
    _, ys = lax.scan(block_step, carry0, u_blocks)
    y = ys.transpose(1, 0, 2, 3, 4).reshape(bsz, L, S5_WIDTH) + d.astype(f32) * u
    g = jax.nn.gelu(y)
    ab = g @ w_glu.astype(f32) + b_glu.astype(f32)
    val, gate = jnp.split(ab, 2, axis=-1)
    return (val * jax.nn.sigmoid(gate)).astype(h.dtype)

def _causal_dwconv(u, w):
    return lax.conv_general_dilated(u, w[:, None, :].astype(u.dtype), (1,), [(M2_CONV - 1, 0)],
                                    dimension_numbers=('NWC', 'WIO', 'NWC'),
                                    feature_group_count=u.shape[-1])

def _segsum(a):
    t = a.shape[-1]
    cs = jnp.cumsum(a, axis=-1)
    diff = cs[..., :, None] - cs[..., None, :]
    mask = jnp.tril(jnp.ones((t, t), dtype=bool))
    return jnp.where(mask, diff, -jnp.inf)

def _ssd_mixer(h, w_in, conv_w, conv_b, dt_bias, a_log, d, norm_g, w_out):
    f32 = jnp.float32
    bsz, L, _ = h.shape
    nc = L // M2_CHUNK
    G, R, P, N, Q = M2_GROUPS, M2_HPG, M2_HEADDIM, M2_STATE, M2_CHUNK
    zxbcdt = h @ w_in
    z, xbc, dt_raw = jnp.split(zxbcdt, [M2_D_INNER, M2_D_INNER + M2_CONV_DIM], axis=-1)
    xbc = jax.nn.silu(_causal_dwconv(xbc, conv_w) + conv_b)
    xs, b_in, c_in = jnp.split(xbc, [M2_D_INNER, M2_D_INNER + G * N], axis=-1)
    dt = jax.nn.softplus(dt_raw.astype(f32) + dt_bias.astype(f32))
    a = -jnp.exp(a_log.astype(f32)).reshape(G, R)
    xs = xs.astype(f32).reshape(bsz, nc, Q, G, R, P)
    b_in = b_in.astype(f32).reshape(bsz, nc, Q, G, N)
    c_in = c_in.astype(f32).reshape(bsz, nc, Q, G, N)
    dt = dt.reshape(bsz, nc, Q, G, R)
    xdt = xs * dt[..., None]
    a_dt = jnp.transpose(dt * a, (0, 3, 4, 1, 2))
    a_cs = jnp.cumsum(a_dt, axis=-1)
    l_mat = jnp.exp(_segsum(a_dt))
    cb = jnp.einsum('bclgn,bcsgn->bcgls', c_in, b_in)
    y_diag = jnp.einsum('bcgls,bgrcls,bcsgrp->bclgrp', cb, l_mat, xdt)
    decay_states = jnp.exp(a_cs[..., -1:] - a_cs)
    states = jnp.einsum('bclgn,bgrcl,bclgrp->bcgrpn', b_in, decay_states, xdt)
    chunk_decay = jnp.exp(a_cs[..., -1])

    def carry_step(carry, inp):
        st, dec = inp
        return dec[..., None, None] * carry + st, carry

    _, prev = lax.scan(carry_step, jnp.zeros((bsz, G, R, P, N), f32),
                       (jnp.moveaxis(states, 1, 0), jnp.moveaxis(chunk_decay, -1, 0)))
    prev = jnp.moveaxis(prev, 0, 1)
    y_off = jnp.einsum('bclgn,bcgrpn,bgrcl->bclgrp', c_in, prev, jnp.exp(a_cs))
    y = y_diag + y_off + xs * d.astype(f32).reshape(G, R, 1)
    y = y.reshape(bsz, L, M2_D_INNER) * jax.nn.silu(z.astype(f32))
    yg = y.reshape(bsz, L, G, M2_D_INNER // G)
    yg = yg * lax.rsqrt(jnp.mean(yg * yg, axis=-1, keepdims=True) + NORM_EPS)
    y = yg.reshape(bsz, L, M2_D_INNER) * norm_g.astype(f32)
    return y.astype(h.dtype) @ w_out

def second_inputs(seed: int = 0) -> dict:
    f32 = jnp.float32
    key = jax.random.key(seed)
    it = iter(jax.random.split(key, 28))

    def nrm(shape, scale):
        return scale * jax.random.normal(next(it), shape, f32)

    D, F = D_MODEL, D_FF_2
    NA, NB = N_A_LAYERS, N_B_LAYERS
    G, P, H = S5_GROUPS, S5_STATE, S5_GROUP
    x = nrm((BATCH, SEQ, D), 1.0)
    c = nrm((BATCH, D), 1.0)
    ada_w = nrm((DEPTH, D, N_MOD * D), 0.5 * D ** -0.5)
    ada_b = nrm((DEPTH, N_MOD * D), 0.02)
    norm_mix_g = 1.0 + nrm((DEPTH, D), 0.05)
    norm_mlp_g = 1.0 + nrm((DEPTH, D), 0.05)
    mlp_w1 = nrm((DEPTH, D, F), D ** -0.5)
    mlp_w2 = nrm((DEPTH, F, D), F ** -0.5)
    s5_w_in = nrm((NA, D, S5_WIDTH), D ** -0.5)
    s5_lambda_re = -0.5 + nrm((NA, G, P), 0.01)
    s5_lambda_im = math.pi * jnp.arange(P, dtype=f32) + nrm((NA, G, P), 0.01)
    s5_log_dt = jax.random.uniform(next(it), (NA, G), f32, minval=math.log(S5_DT_MIN), maxval=math.log(S5_DT_MAX))
    s5_b_re = nrm((NA, G, P, H), (2 * H) ** -0.5)
    s5_b_im = nrm((NA, G, P, H), (2 * H) ** -0.5)
    s5_c_re = nrm((NA, G, H, P), (2 * P) ** -0.5)
    s5_c_im = nrm((NA, G, H, P), (2 * P) ** -0.5)
    s5_d = nrm((NA, S5_WIDTH), 1.0)
    s5_w_glu = nrm((NA, S5_WIDTH, 2 * D), S5_WIDTH ** -0.5)
    s5_b_glu = nrm((NA, 2 * D), 0.02)
    m2_w_in = nrm((NB, D, M2_IN_DIM), D ** -0.5)
    m2_conv_w = nrm((NB, M2_CONV, M2_CONV_DIM), M2_CONV ** -0.5)
    m2_conv_b = nrm((NB, M2_CONV_DIM), 0.02)
    dt0 = jnp.exp(jax.random.uniform(next(it), (NB, M2_HEADS), f32, minval=math.log(M2_DT_MIN), maxval=math.log(M2_DT_MAX)))
    m2_dt_bias = dt0 + jnp.log(-jnp.expm1(-dt0))
    m2_a_log = jnp.log(jax.random.uniform(next(it), (NB, M2_HEADS), f32, minval=1.0, maxval=16.0))
    m2_d = 1.0 + nrm((NB, M2_HEADS), 0.1)
    m2_norm_g = 1.0 + nrm((NB, M2_D_INNER), 0.05)
    m2_w_out = nrm((NB, M2_D_INNER, D), M2_D_INNER ** -0.5)
    final_norm_g = 1.0 + nrm((D,), 0.05)
    return {'x': x, 'c': c, 'ada_w': ada_w, 'ada_b': ada_b,
            'norm_mix_g': norm_mix_g, 'norm_mlp_g': norm_mlp_g,
            'mlp_w1': mlp_w1, 'mlp_w2': mlp_w2,
            's5_w_in': s5_w_in, 's5_lambda_re': s5_lambda_re, 's5_lambda_im': s5_lambda_im,
            's5_log_dt': s5_log_dt, 's5_b_re': s5_b_re, 's5_b_im': s5_b_im,
            's5_c_re': s5_c_re, 's5_c_im': s5_c_im, 's5_d': s5_d,
            's5_w_glu': s5_w_glu, 's5_b_glu': s5_b_glu,
            'm2_w_in': m2_w_in, 'm2_conv_w': m2_conv_w, 'm2_conv_b': m2_conv_b,
            'm2_dt_bias': m2_dt_bias, 'm2_a_log': m2_a_log, 'm2_d': m2_d,
            'm2_norm_g': m2_norm_g, 'm2_w_out': m2_w_out,
            'final_norm_g': final_norm_g}

def second_block(x, c, ada_w, ada_b, norm_mix_g, norm_mlp_g, mlp_w1, mlp_w2,
              s5_w_in, s5_lambda_re, s5_lambda_im, s5_log_dt, s5_b_re, s5_b_im,
              s5_c_re, s5_c_im, s5_d, s5_w_glu, s5_b_glu,
              m2_w_in, m2_conv_w, m2_conv_b, m2_dt_bias, m2_a_log, m2_d,
              m2_norm_g, m2_w_out, final_norm_g):
    cond = jax.nn.silu(c)
    for i in range(DEPTH):
        mod = cond @ ada_w[i] + ada_b[i]
        sh1, sc1, g1, sh2, sc2, g2 = jnp.split(mod[:, None, :], N_MOD, axis=-1)
        h = _modulate(_rmsnorm(x, norm_mix_g[i]), sh1, sc1)
        j = i // N_MIXERS
        if i % N_MIXERS == 0:
            y = _s5_mixer(h, s5_w_in[j], s5_lambda_re[j], s5_lambda_im[j], s5_log_dt[j],
                          s5_b_re[j], s5_b_im[j], s5_c_re[j], s5_c_im[j], s5_d[j],
                          s5_w_glu[j], s5_b_glu[j])
        else:
            y = _ssd_mixer(h, m2_w_in[j], m2_conv_w[j], m2_conv_b[j], m2_dt_bias[j],
                           m2_a_log[j], m2_d[j], m2_norm_g[j], m2_w_out[j])
        x = x + g1 * y
        h = _modulate(_rmsnorm(x, norm_mlp_g[i]), sh2, sc2)
        x = x + g2 * _sq_relu_mlp(h, mlp_w1[i], mlp_w2[i])
    return _rmsnorm(x, final_norm_g)


def setup_inputs(seed=0):
    out = dict(first_inputs(seed))
    for name, value in second_inputs(seed + 1).items():
        if name != "x":
            out[name + "_2"] = value
    return out


def reference(
    x, positions, mix_pre_g, mix_post_g, pool_w, pool_scale, kv_norm_g, w_kv, w_q, w_o, sinks,
    ffn_pre_g, ffn_post_g, ffn_w_in, ffn_conv_w, ffn_conv_b, ffn_w_out, c_2, ada_w_2, ada_b_2,
    norm_mix_g_2, norm_mlp_g_2, mlp_w1_2, mlp_w2_2, s5_w_in_2, s5_lambda_re_2, s5_lambda_im_2,
    s5_log_dt_2, s5_b_re_2, s5_b_im_2, s5_c_re_2, s5_c_im_2, s5_d_2, s5_w_glu_2, s5_b_glu_2,
    m2_w_in_2, m2_conv_w_2, m2_conv_b_2, m2_dt_bias_2, m2_a_log_2, m2_d_2, m2_norm_g_2,
    m2_w_out_2, final_norm_g_2,
):
    x = first_block(
        x, positions, mix_pre_g, mix_post_g, pool_w, pool_scale, kv_norm_g, w_kv, w_q, w_o,
        sinks, ffn_pre_g, ffn_post_g, ffn_w_in, ffn_conv_w, ffn_conv_b, ffn_w_out,
    )
    return second_block(
        x, c_2, ada_w_2, ada_b_2, norm_mix_g_2, norm_mlp_g_2, mlp_w1_2, mlp_w2_2, s5_w_in_2,
        s5_lambda_re_2, s5_lambda_im_2, s5_log_dt_2, s5_b_re_2, s5_b_im_2, s5_c_re_2, s5_c_im_2,
        s5_d_2, s5_w_glu_2, s5_b_glu_2, m2_w_in_2, m2_conv_w_2, m2_conv_b_2, m2_dt_bias_2,
        m2_a_log_2, m2_d_2, m2_norm_g_2, m2_w_out_2, final_norm_g_2,
    )


_drawn_inputs = setup_inputs


def setup_inputs(seed=0):
    import zlib

    import numpy as np

    out = dict(_drawn_inputs(seed))
    spreads = {}
    factors = {'ffn_conv_b': 3.481,
     'norm_mix_g_2': 5.718,
     'norm_mlp_g_2': 3.869,
     's5_lambda_re_2': 64.0,
     's5_lambda_im_2': 64.0,
     's5_log_dt_2': 64.0,
     's5_b_re_2': 64.0,
     's5_b_im_2': 64.0,
     's5_c_re_2': 64.0,
     's5_c_im_2': 64.0,
     's5_b_glu_2': 8.0,
     'm2_conv_b_2': 43.194,
     'm2_d_2': 52.16,
     'm2_norm_g_2': 25.917}
    for name, (base, spread) in spreads.items():
        noise = np.random.default_rng([zlib.crc32(name.encode()), seed]).standard_normal(out[name].shape)
        drawn = base * np.exp(spread * noise) if base else spread * noise
        out[name] = jnp.asarray(drawn.astype(out[name].dtype))
    for name, factor in factors.items():
        out[name] = (out[name] * factor).astype(out[name].dtype)
    return out
```

```python
from contextlib import ExitStack, contextmanager

import numpy as np

import concourse.bass as bass
from concourse import mybir

P = 128
T = 512
D = 1024
DC = D // P
FF = 2816
FC = FF // P
FH = FC // 2
MC = 4 * D // P
MH = MC // 2
DI = 2 * D
ZC = DI // P
XC = (DI + 2 * 4 * P) // P
NH2 = DI // 64
NB = T // P
TILE = 16 * P
HALF = FH * P
EPS_A, EPS_B = 1e-6, 1e-5
NEG = -1e30
ADA = 48
ADA_TILES = 2 * ADA // 2

PHASES = [
    ("pool", 1, TILE, None),
    ("ffn0_in_a", FH, TILE, "dve"), ("ffn0_out_a", 8, HALF, "act"),
    ("ffn0_in_b", FH, TILE, "dve"), ("ffn0_out_b", 8, HALF, "dve"),
    ("kproj", 1, TILE, None), ("vproj", 1, TILE, None),
    ("qproj", 4, TILE, None), ("oproj", 4, TILE, "act"),
    ("ffn1_in_a", FH, TILE, "dve"), ("ffn1_out_a", 8, HALF, "act"),
    ("ffn1_in_b", FH, TILE, "dve"), ("ffn1_out_b", 8, HALF, "dve"),
    ("s5_in", 4, TILE, "act"), ("s5_glu", 8, TILE, "dve"),
    ("mlp0_in_a", 8, TILE, "act"), ("mlp0_out_a", 8, TILE, "dve"),
    ("mlp0_in_b", 8, TILE, "act"), ("mlp0_out_b", 8, TILE, "dve"),
    ("m2_dt", 1, TILE // 2, None), ("m2_z", 8, TILE, "act"), ("m2_xbc", 12, TILE, "dve"),
    ("m2_out", 8, TILE, "dve"),
    ("mlp1_in_a", 8, TILE, "act"), ("mlp1_out_a", 8, TILE, "dve"),
    ("mlp1_in_b", 8, TILE, "act"), ("mlp1_out_b", 8, TILE, "dve"),
]
FIRST = {}
_n = 0
for _name, _tiles, _w, _e in PHASES:
    FIRST[_name] = _n
    _n += _tiles
NT = _n
TILES = {name: tiles for name, tiles, _, _ in PHASES}

VECS = {}
_at = 0
for _name, _cols in [
    ("mix_pre", 16), ("mix_post", 16), ("pool_scale", 8), ("kv_norm", 8), ("ffn_pre", 16),
    ("ffn_post", 16), ("conv_w", 2 * 3 * 2 * FC), ("conv_b", 2 * 2 * FC), ("c", 8),
    ("ada_b", 2 * ADA), ("norm_mix", 16), ("norm_mlp", 16), ("final", 8), ("lam_re", 32),
    ("lam_im", 32), ("log_dt", 32), ("s5_d", 8), ("b_glu", 16), ("m2_conv_w", 4 * XC),
    ("m2_conv_b", XC), ("m2_d", ZC), ("m2_norm", ZC), ("dt_bias", 1), ("a_log", 1), ("sinks", 16),
    ("inv_freq", 1), ("rope_sign", 1), ("tok", P),
]:
    VECS[_name] = (_at, _cols)
    _at += _cols
NV = _at


STOP_X = {"x1": 8, "x2": 16, "x3": 24, "x4": 32, "x5": 40, "x6": 56, "x7": 64}
TWO_PI_A, TWO_PI_B = 6.28125, 4058 / 2 ** 21
TWO_PI_C = 2 * np.pi - TWO_PI_A - TWO_PI_B
MAGIC = 1.5 * 2 ** 23


UPPER = 2 * P + 64 + (NB + 1) * P

START = {"s_read": 1, "o_split": 1, "o_done": 1, "bu_copied": 1, "bu_used": 2, "scanned": 1, "y5_read": 2, "y5_done": 2}


class Count:

    def __init__(self, start=0):
        self.n, self.r, self.per, self.n0 = start, None, 0, 0

    def after(self, k=1):
        self.n += k
        return self.now()

    def now(self, back=0):
        v = self.n - back
        return v if self.r is None or not self.per else self.r * self.per + v


@contextmanager
def rounds(eng, n, *counts):
    with eng.Fori(0, n) as r:
        for c, per in counts:
            c.r, c.per, c.n0 = r, per, c.n
        yield r
    for c, per in counts:
        assert c.n - c.n0 == per, (c.n, c.n0, per)
        c.r, c.per, c.n = None, 0, c.n0 + n * per


def build(nc, weights, ada, vecs, consts, x_in, pos_in, s5_b, s5_c, out, stop=None):
    f32, f32r, i32 = mybir.dt.float32, mybir.dt.float32r, mybir.dt.int32
    ALU, ACT, AX = mybir.AluOpType, mybir.ActivationFunctionType, mybir.AxisListType
    ADD, SUB, MUL, MAX = ALU.add, ALU.subtract, ALU.mult, ALU.max

    at = [16512]

    def place(name, cols, dt=f32, offset=None):
        if offset is None:
            offset, at[0] = at[0], at[0] + (cols * 4 + 31) // 32 * 32
        return nc.alloc_sbuf_tensor_at(name, [P, cols], dt, offset=offset)

    KB = 1024
    H0 = at[0]
    h_hi, h_lo = place("h_hi", DC * T, f32r), place("h_lo", DC * T, f32r)
    A0 = at[0]
    a_hi, a_lo = place("a_hi", 16 * T, f32r), place("a_lo", 16 * T, f32r)
    F0 = at[0]
    f = place("f", DC * T)
    x = place("x", DC * T)
    raw = place("raw", 2 * TILE)
    w_hi, w_lo = place("w_hi", 2 * TILE, f32r), place("w_lo", 2 * TILE, f32r)
    S0 = at[0]
    tg, tv, gl = place("tg", 2 * T), place("tv", 2 * T), place("gl", 2 * T)
    sq, sqsum, rstd = place("sq", 2 * T), place("sqsum", T), place("rstd", T)
    vec, mod = place("vec", NV), place("mod", 2 * ADA)
    gain = place("gain", DC)
    cond = place("cond", DC)
    zero = place("zero", 1)
    ident, perm, ones = place("ident", P), place("perm", P), place("ones", P)
    at[0] = (at[0] + 31) // 32 * 32
    W0 = at[0]
    assert W0 + 5 * KB + 512 <= 229344, W0
    ada_w = [place("ada_w0", TILE, offset=A0 + 22 * KB), place("ada_w1", TILE, offset=A0 + 54 * KB)]

    PW = 16 + T
    hp = place("pool_h", DC * PW, offset=A0)
    win = [place("pool_s0", 2 * PW, offset=H0), place("pool_s1", 2 * PW, offset=H0 + 5 * KB)]
    edge = place("pool_edge", 4 * 16, offset=H0 + 12 * KB)
    dd_hi, dd_lo = place("pool_d_hi", DC * T, f32r, offset=A0 + 20 * KB), place("pool_d_lo", DC * T, f32r, offset=A0 + 40 * KB)

    cosT, sinT = place("cos", T, offset=A0 + 16 * KB), place("sin", T, offset=A0 + 18 * KB)
    kdup = place("kdup", 4 * (P + T), offset=A0 + 20 * KB)
    posi = place("posi", T, i32, offset=W0 + 3 * KB)
    v_tok = place("v_tok", (NB + 1) * 256, offset=A0 + 48 * KB)
    kb, vb = place("kb", 4 * 256, offset=A0 + 53 * KB), place("vb", 2 * 256, offset=A0 + 57 * KB)
    qb = place("qb", DC * P, offset=A0 + 59 * KB)
    mb = place("mb", 256, offset=A0 + 63 * KB)
    s_sb = place("s_sb", 2 * 1024, offset=A0)
    p_t = place("p_t", 2 * 1024, offset=A0 + 8 * KB)
    masks = place("masks", (NB + 1) * P, offset=W0)
    mx = place("mx", 6 * 8, offset=W0 + 5 * KB)
    q = f

    cos5, sin5, turn5 = (place(n, 32 * P, offset=A0 + 16 * KB * k) for k, n in enumerate(("cos5", "sin5", "turn5")))
    b_raw, b_bar = place("b_raw", 2048, offset=A0 + 48 * KB), place("b_bar", 2048, offset=A0 + 56 * KB)
    b_tmp = turn5[:, 0:1024]
    b_t = b_raw
    c_mat = place("c_mat", 3072, offset=S0)
    small = place("small", 32 * 32, offset=W0)
    w5 = [[place(f"s5_w{u}{k}", T, offset=H0 + (4 * u + k) * 2 * KB) for k in range(4)] for u in range(2)]
    p5 = [[place(f"s5_p{u}{k}", T, offset=(H0 + (8 + 4 * u + k) * 2 * KB)) for k in range(4)] for u in range(2)]
    ub = sq
    bu5 = [place(f"s5_bu{u}", 2 * T, offset=A0 + (36 + 4 * u) * KB) for u in range(2)]
    g5 = [[place(f"s5_g{u}{k}", T, offset=A0 + (32 + 12 * u + 2 * k) * KB) for k in range(2)] for u in range(2)]

    zt, xbc = place("zt", ZC * T, offset=A0), place("xbc", XC * T, offset=A0 + 32 * KB)
    xdt, xdtd = place("xdt", NB * T, offset=H0), place("xdtd", NB * T, offset=H0 + 8 * KB)
    prev = place("prev", 3 * T, offset=H0 + 16 * KB)
    b_tok, cbm = place("b_tok", T, offset=H0 + 22 * KB), place("cbm", T, offset=H0 + 24 * KB)
    ea, ytmp = place("ea", 2 * T, offset=H0 + 26 * KB), place("ytmp", T, offset=H0 + 30 * KB)
    yg = place("yg", 4 * T, offset=S0 + 4 * KB)
    acs_row, ea_row = place("acs_row", T, offset=W0), place("ea_row", T, offset=W0 + 2 * KB)
    cdec, upper = place("cdec", P, offset=W0 + 4 * KB), place("upper", P, offset=W0 + 4 * KB + 512)
    one_col = place("one_col", 1, offset=W0 + 5 * KB)
    small32 = place("a_exp_col", 1, offset=W0 + 5 * KB + 32)[0:32, :]
    dt_row = place("dt_row", T, offset=S0 + 10 * KB)
    acs_t, dt_t, decay, diag = (sq[:, k * P:(k + 1) * P] for k in range(4))

    ps = nc.psum_tensor("ps", [P, 8 * T], f32).__enter__()

    def bank(b, cols=T, p0=0, p1=P, off=0):
        return ps[p0:p1, b * T + off:b * T + off + cols]

    NORM, MOD = 4, 5

    def v(name, col=0, p=P):
        a, n = VECS[name]
        if isinstance(col, int):
            assert col < n
            return vec[0:p, a + col:a + col + 1]
        return vec[0:p, bass.ds(col + a, 1)]

    def vs(name, lo, hi, p=P):
        a, _ = VECS[name]
        return vec[0:p, a + lo:a + hi]

    def chunk(t, c, n=1):
        return t[:, c * T:(c + n) * T] if isinstance(c, int) else t[:, bass.ds(c * T, n * T)]

    def as3(ap, a):
        return ap.rearrange("p (a b) -> p a b", a=a)

    sems = {}

    def sem(name):
        if name not in sems:
            sems[name] = nc.semaphore(name).__enter__()
        return sems[name]

    order = [n for n, *_ in PHASES]
    freed = {"act": {}, "dve": {}}
    na = {"act": 2, "dve": 2}
    for n, tiles, _, e in PHASES:
        for k in na:
            freed[k][n] = na[k]
        if e:
            na[e] += tiles
    EMPTY = {n: e for n, _, _, e in PHASES}
    raw_landed = [sem("raw_landed0"), sem("raw_landed1")]
    w_hi_done, w_split, tile_done = sem("w_hi_done"), sem("w_split"), sem("tile_done")
    acc_free = {"act": sem("acc_free_act"), "dve": sem("acc_free_dve")}
    sq_ready, sq_added, norm_sum, std_done = sem("sq_ready"), sem("sq_added"), sem("norm_sum"), sem("std_done")
    hf_done, h_hi_done, h_ready = sem("hf_done"), sem("h_hi_done"), sem("h_ready")
    a_hi_done, a_ready = sem("a_hi_done"), sem("a_ready")
    x_ready, dve_step = sem("x_ready"), sem("dve_step")
    pool_out, pool_d = sem("pool_out"), sem("pool_d")
    conv_pre, gate_conv, gelu_done, prod_done = sem("conv_pre"), sem("gate_conv"), sem("gelu_done"), sem("prod_done")
    ada_landed, ada_used = [sem("ada_landed0"), sem("ada_landed1")], sem("ada_used")

    def tile_at(g):
        return g + 4

    done = {"x1": "ffn0_in_a", "x2": "kproj", "x3": "ffn1_in_a", "x4": "s5_in", "x5": "mlp0_in_a",
            "x6": "m2_dt", "x7": "mlp1_in_a"}.get(stop)
    phases = PHASES[:order.index(done)] if done else PHASES
    total = sum(t for _, t, _, _ in phases)
    block = nc.Block().__enter__()

    @block.sync
    def _(sp):
        sp.dma_start(x[:, :], x_in).then_inc(sem("x_landed"), 16)
        sp.dma_start(vec[:, :], vecs).then_inc(sem("vec_landed"), 16)
        sp.dma_start(posi[:, :], pos_in).then_inc(sem("pos_landed"), 16)
        sp.dma_start(edge[:, :], consts[:, 2 * P:2 * P + 64]).then_inc(sem("edge_landed"), 16)
        g = Count()

        def load(width):
            u = g.n % 2
            src = weights[bass.ds(g.now() * P, P), 0:width]
            sp.dma_start(raw[:, u * TILE:u * TILE + width], src).then_inc(raw_landed[u], 16)
            g.after()

        for name, tiles, width, _ in phases:
            pairs = tiles // 2 if g.n >= 2 else 0
            if pairs:
                with rounds(sp, pairs, (g, 2)):
                    for _ in range(2):
                        sp.wait_ge(w_split, g.now(1))
                        load(width)
            for _ in range(tiles - 2 * pairs):
                if g.n >= 2:
                    sp.wait_ge(w_split, g.now(1))
                load(width)
            if name == "pool":
                sp.dma_start(ident[:, :], consts[:, 0:P]).then_inc(sem("ident_landed"), 16)
                sp.dma_start(perm[:, :], consts[:, P:2 * P]).then_inc(sem("perm_landed"), 16)
                sp.dma_start(masks[:, :], consts[:, 2 * P + 64:2 * P + 64 + (NB + 1) * P]).then_inc(sem("masks_landed"), 16)
        for c in range(DC):
            if stop in ("x5", "x6", "x7"):
                sp.wait_ge(acc_free["dve"], freed["dve"][done])
            elif stop:
                sp.wait_ge(x_ready, STOP_X[stop])
            else:
                sp.wait_ge(sem("y_ready"), c + 1)
            sp.dma_start(out[:, c * T:(c + 1) * T], chunk(x, c)).then_inc(sem("y_stored"), 16)
        sp.wait_ge(sem("y_stored"), 16 * DC)


    @block.tensor
    def _(pe):
        g = Count()
        C = {k: Count() for k in ("sum", "ada", "ada0", "ada1", "qraw")}
        fr = {"act": Count(2), "dve": Count(2)}

        def products(dst, o, rhs_hi, rhs_lo, start, last):
            nc.tensor.matmul(dst, w_hi[:, o:o + P], rhs_hi, start=start, stop=False)
            nc.tensor.matmul(dst, w_hi[:, o:o + P], rhs_lo, start=False, stop=False)
            return nc.tensor.matmul(dst, w_lo[:, o:o + P], rhs_hi, start=False, stop=last)

        def linear_tile(name, k_chunks, outs, src_hi, src_lo, ready, base):
            u = g.n % 2
            pe.wait_ge(w_split, g.after())
            if EMPTY[name]:
                e = EMPTY[name]
                pe.wait_ge(acc_free[e], fr[e].now(1))
                fr[e].after()
            for m in range(outs):
                for k in range(k_chunks):
                    if m == 0:
                        pe.wait_ge(ready, base + k + 1)
                    last = products(bank(2 * u + m), u * TILE + (m * k_chunks + k) * P,
                                    chunk(src_hi, k), chunk(src_lo, k), k == 0, k == k_chunks - 1)
            last.then_inc(tile_done, 1)

        def ada_tile(s):
            pe.wait_ge(ada_landed[s], C[f"ada{s}"].after(16))
            for m in range(2):
                for k in range(DC):
                    o = (k * 2 + m) * P
                    last = nc.tensor.matmul(ps[:, bass.ds(C["ada"].now() * 2 + MOD * T + m, 1)],
                                            ada_w[s][:, o:o + P], cond[:, k:k + 1],
                                            start=(k == 0), stop=(k == DC - 1))
            last.then_inc(ada_used, 1)
            C["ada"].after()

        def phase(name, k_chunks, outs, hi, lo, ready, base, with_ada=False):
            e = EMPTY[name]
            for k in ("act", "dve"):
                pe.wait_ge(acc_free[k], freed[k][name])
                assert fr[k].n == freed[k][name]
            n, peel = divmod(TILES[name], 2)
            per = [(g, 2)] + ([(fr[e], 2)] if e else [])
            if with_ada:
                per += [(C["ada"], 2), (C["ada0"], 16), (C["ada1"], 16)]
            if name == "qproj":
                per += [(C["qraw"], 4)]
            with rounds(pe, n, *per):
                for s in range(2):
                    linear_tile(name, k_chunks, outs, hi, lo, ready, base)
                    if with_ada:
                        ada_tile(s)
                    if name == "qproj":
                        rope_pair()
            if peel:
                linear_tile(name, k_chunks, outs, hi, lo, ready, base)
            if with_ada:
                ada_tile(0)
                ada_tile(1)

        def norm_sum_matmul():
            n = C["sum"].n
            pe.wait_ge(sq_added, 9 * (n + 1))
            if n:
                pe.wait_ge(std_done, n)
            nc.tensor.matmul(bank(NORM), ones[:, :], sqsum[:, :], start=True, stop=True).then_inc(norm_sum, 1)
            C["sum"].after()

        def ffn(layer, hb):
            ab = 2 * FH * layer
            phase(f"ffn{layer}_in_a", DC, 2, h_hi, h_lo, h_ready, hb, with_ada=True)
            phase(f"ffn{layer}_out_a", FH, 1, a_hi, a_lo, a_ready, ab)
            phase(f"ffn{layer}_in_b", DC, 2, h_hi, h_lo, h_ready, hb, with_ada=True)
            phase(f"ffn{layer}_out_b", FH, 1, a_hi, a_lo, a_ready, ab + FH)
            norm_sum_matmul()
            norm_sum_matmul()

        def rope_pair():
            for s in range(2):
                pe.wait_ge(sem("qraw"), C["qraw"].after())
                nc.tensor.matmul(bank(6 + s), perm[:, :], chunk(tg, s), start=True, stop=True).then_inc(sem("rot"), 1)

        pe.wait_ge(sem("ones_set"), 1)
        norm_sum_matmul()

        pe.wait_ge(w_split, g.after())
        for grp in range(4):
            if grp >= 2:
                pe.wait_ge(pool_out, grp - 1)
            for m in range(2):
                for k in range(2):
                    c = 2 * grp + k
                    pe.wait_ge(pool_d, c + 1)
                    last = products(bank(2 * (grp % 2) + m), (c * 2 + m) * P, chunk(dd_hi, c),
                                    chunk(dd_lo, c), k == 0, k == 1)
            last.then_inc(tile_done, 1)
        norm_sum_matmul()
        norm_sum_matmul()
        if stop == "x1":
            return
        pe.wait_ge(pool_out, 4)
        pe.wait_ge(sem("cond_ready"), 1)
        ffn(0, 0)
        if stop == "x2":
            return

        pe.wait_ge(sem("perm_landed"), 16)
        phase_base = 8
        for k_ in ("act", "dve"):
            pe.wait_ge(acc_free[k_], freed[k_]["kproj"])
        linear_tile("kproj", DC, 2, a_hi, a_lo, h_ready, phase_base)
        rope_pair()
        u = g.n % 2
        pe.wait_ge(w_split, g.after())
        for n in range(NB):
            for k in range(DC):
                t0, o = k * T + n * P, u * TILE + k * 256
                nc.tensor.matmul(bank(n, 256), a_hi[:, t0:t0 + P], w_hi[:, o:o + 256], start=(k == 0), stop=False)
                nc.tensor.matmul(bank(n, 256), a_hi[:, t0:t0 + P], w_lo[:, o:o + 256], start=False, stop=False)
                last = nc.tensor.matmul(bank(n, 256), a_lo[:, t0:t0 + P], w_hi[:, o:o + 256],
                                        start=False, stop=(k == DC - 1))
        last.then_inc(tile_done, 1)
        pe.wait_ge(sem("v_copied"), 1)
        phase("qproj", DC, 2, h_hi, h_lo, h_ready, 16)

        pe.wait_ge(sem("ident_landed"), 16)
        A = {k: Count() for k in ("blk", "sc", "sc_read", "p", "pt", "o_read", "pt_done")}

        def scores(gkv):
            pe.wait_ge(sem("s_read"), A["sc_read"].now(-1))
            A["sc_read"].after()
            for hh in range(4):
                h = 4 * gkv + hh
                p0, c = 64 * (h % 2), h // 2
                last = nc.tensor.matmul(bank(hh % 2, 256, off=256 * (hh // 2)), qb[p0:p0 + 64, c * P:(c + 1) * P],
                                        kb[p0:p0 + 64, gkv * 256:(gkv + 1) * 256], start=True, stop=True)
            last.then_inc(sem("s_done"), 1)

        def values(gkv):
            pe.wait_ge(sem("p_ready"), A["p"].after())
            b = gkv % 2
            for kb_ in range(2):
                for hh in range(4):
                    o = b * 1024 + hh * 256 + kb_ * P
                    last = nc.tensor.transpose(bank(2 + kb_, P, off=hh * P), s_sb[:, o:o + P], ident[:, :])
            last.then_inc(sem("pt_psum"), 1)
            pe.wait_ge(sem("pt_a"), A["pt"].after())
            pe.wait_ge(sem("pt_b"), A["pt"].now())
            pe.wait_ge(sem("o_split"), A["o_read"].now(-1))
            A["o_read"].after()
            for par in range(2):
                for kb_ in range(2):
                    o = b * 1024 + kb_ * 512 + par * 256
                    rhs = as3(p_t[:, o:o + 256], 2)
                    last = nc.tensor.matmul(as3(bank(6, 256, 64 * par, 64 * par + 64), 2), vb[:, kb_ * 256 + gkv * 64:kb_ * 256 + gkv * 64 + 64],
                                            rhs, start=(kb_ == 0), stop=(kb_ == 1))
            last.then_inc(sem("o_done"), 1)

        with rounds(pe, NB, (A["blk"], 1), (A["sc_read"], 4), (A["p"], 4), (A["pt"], 4), (A["o_read"], 4)):
            pe.wait_ge(sem("blk_ready"), A["blk"].after())
            scores(0)
            for gkv in range(4):
                if gkv < 3:
                    scores(gkv + 1)
                values(gkv)
        pe.wait_ge(sem("o_split"), 17)
        phase("oproj", DC, 2, h_hi, h_lo, sem("o_split"), 1)
        norm_sum_matmul()
        norm_sum_matmul()
        if stop == "x3":
            return
        ffn(1, 24)
        if stop == "x4":
            return

        phase("s5_in", DC, 2, h_hi, h_lo, h_ready, 32)
        for half in range(2):
            pe.wait_ge(sem("b_bar_done"), half + 1)
            for j in range(DC):
                last = nc.tensor.transpose(bank(6 + j // 4, P, off=(j % 4) * P),
                                           b_bar[:, half * 1024 + j * P:half * 1024 + (j + 1) * P], ident[:, :])
            last.then_inc(sem("b_t_psum"), 1)
            pe.wait_ge(sem("b_t_done"), half + 1)
        for k_ in ("act", "dve"):
            pe.wait_ge(acc_free[k_], freed[k_]["s5_glu"])
        pe.wait_ge(sem("c_ready"), 1)
        S = {"bu": Count(1), "ub": Count(), "h": Count(), "y": Count(2)}

        def inputs5(j):
            pe.wait_ge(sem("bu_copied"), S["bu"].now())
            pe.wait_ge(sem("ub_ready"), S["ub"].after())
            S["bu"].after()
            for i in range(4):
                rhs = ub[32 * i:32 * i + 32, j * P:(j + 1) * P]
                for half in range(2):
                    last = nc.tensor.matmul(bank(i, P, off=half * P),
                                            b_t[32 * i:32 * i + 32, half * 1024 + j * P:half * 1024 + (j + 1) * P],
                                            rhs, start=True, stop=True)
            last.then_inc(sem("bu_done"), 1)

        def outputs5(j):
            pe.wait_ge(sem("p_dve"), S["h"].after())
            pe.wait_ge(sem("p_gp"), S["h"].now())
            pe.wait_ge(sem("y5_read"), S["y"].now(1))
            S["y"].after()
            for i in range(4):
                for k, part in enumerate((0, 2, 1, 1)):
                    c0 = part * 1024 + (4 * j + i) * 32
                    last = nc.tensor.matmul(bank(6 + j % 2, P, 32 * i, 32 * i + 32), c_mat[:, c0:c0 + 32],
                                            p5[j % 2][k][:, i * P:(i + 1) * P], start=(k == 0), stop=(k == 3))
            last.then_inc(sem("y5_done"), 1)

        def block5(more):
            for j in range(DC):
                if j < DC - 2 or more:
                    inputs5((j + 2) % DC)
                outputs5(j)

        inputs5(0)
        inputs5(1)
        with rounds(pe, NB - 1, *[(c, DC) for c in S.values()]):
            block5(True)
        block5(False)
        phase("s5_glu", DC, 2, h_hi, h_lo, h_ready, 40)
        norm_sum_matmul()
        if stop == "x5":
            return

        def mlp(layer):
            ab = 4 * FH + 2 * MH * layer
            hb = 48 + 16 * layer
            phase(f"mlp{layer}_in_a", DC, 2, h_hi, h_lo, h_ready, hb)
            phase(f"mlp{layer}_out_a", MH, 1, a_hi, a_lo, a_ready, ab)
            phase(f"mlp{layer}_in_b", DC, 2, h_hi, h_lo, h_ready, hb)
            phase(f"mlp{layer}_out_b", MH, 1, a_hi, a_lo, a_ready, ab + MH)
            norm_sum_matmul()

        mlp(0)
        if stop == "x6":
            return

        for k_ in ("act", "dve"):
            pe.wait_ge(acc_free[k_], freed[k_]["m2_dt"])
        linear_tile("m2_dt", DC, 1, h_hi, h_lo, h_ready, 56)
        pe.wait_ge(sem("dt_copied"), 1)
        phase("m2_z", DC, 2, h_hi, h_lo, h_ready, 56)
        pe.wait_ge(sem("acs_done"), 1)
        for k_, row in enumerate((acs_row, dt_row)):
            for c in range(NB):
                last = nc.tensor.transpose(bank(6, 32, off=k_ * P + c * 32), row[0:32, c * P:(c + 1) * P], ident[0:32, 0:32])
        last.then_inc(sem("rows_t"), 1)
        nc.tensor.matmul(bank(7, P), ones[0:32, :], diag[0:32, :], start=True, stop=True).then_inc(sem("alast_done"), 1)
        phase("m2_xbc", DC, 2, h_hi, h_lo, h_ready, 56)

        for k_ in ("act", "dve"):
            pe.wait_ge(acc_free[k_], freed[k_]["m2_out"])
        pe.wait_ge(sem("xbc_done"), ZC // 2 + XC)
        pe.wait_ge(sem("cdec_done"), 1)
        for grp in range(4):
            Bf, Cf = 16 + grp, 20 + grp
            blk = lambda ch, c: xbc[:, ch * T + c * P:ch * T + (c + 1) * P]
            for c in range(NB):
                for q_ in range(4):
                    last = nc.tensor.transpose(bank(c, P, off=q_ * P), blk(4 * grp + q_, c), ident[:, :])
                last.then_inc(sem("xt_done"), 1)
            if grp:
                pe.wait_ge(sem("gstd_done"), grp)
            for c in range(NB - 1):
                last = nc.tensor.transpose(bank(4, P, off=c * P), blk(Bf, c), ident[:, :])
            last.then_inc(sem("bt_done"), 1)
            for c in range(NB):
                last = nc.tensor.matmul(bank(5, P, off=c * P), blk(Bf, c), blk(Cf, c), start=True, stop=True)
            last.then_inc(sem("cb_done"), 1)
            pe.wait_ge(sem("bt_copied"), grp + 1)
            for c in range(NB - 1):
                pe.wait_ge(sem("xdtd_done"), 3 * grp + c + 1)
                nc.tensor.matmul(bank((6, 7, 4)[c]), b_tok[:, c * P:(c + 1) * P], xdtd[:, c * T:(c + 1) * T],
                                 start=True, stop=True).then_inc(sem("st_done"), 1)
            pe.wait_ge(sem("xdt_done"), NB * (grp + 1))
            pe.wait_ge(sem("prev_done"), 3 * (grp + 1))
            pe.wait_ge(sem("cb_masked"), grp + 1)

            def spread(hh):
                n = 8 * grp + hh
                if hh >= 2:
                    pe.wait_ge(sem("diff_done"), n - 1)
                nc.tensor.matmul(bank(hh % 2), ident[0:32, n:n + 1].broadcast_to([32, P]), acs_row[0:32, :],
                                 start=True, stop=True).then_inc(sem("bc_done"), 1)

            spread(0)
            for hh in range(8):
                if hh < 7:
                    spread(hh + 1)
                n, pair, q_ = 8 * grp + hh, 4 * grp + hh // 2, hh // 2
                if hh % 2 == 0:
                    if q_ >= 2:
                        pe.wait_ge(sem("y_summed"), pair - 1)
                    for c in range(1, NB):
                        last = nc.tensor.matmul(bank(4 + q_ % 2, P, off=c * P), prev[:, (c - 1) * T + q_ * P:(c - 1) * T + (q_ + 1) * P],
                                                blk(Cf, c), start=True, stop=True)
                    last.then_inc(sem("off_done"), 1)
                    for k_ in range(2):
                        last = nc.tensor.matmul(bank(6 + q_ % 2, T, 64 * k_, 64 * k_ + 64), ident[0:32, n + k_:n + k_ + 1].broadcast_to([32, 64]),
                                                ea_row[0:32, :], start=True, stop=True)
                    last.then_inc(sem("ea_done"), 1)
                pe.wait_ge(sem("m_ready"), n + 1)
                p0 = 64 * (hh % 2)
                for c in range(NB):
                    last = nc.tensor.matmul(bank(2 + q_ % 2, P, p0, p0 + 64, off=c * P),
                                            xdt[:, c * T + hh * 64:c * T + (hh + 1) * 64],
                                            tg[:, (hh % 2) * T + c * P:(hh % 2) * T + (c + 1) * P], start=True, stop=True)
                last.then_inc(sem("yd_done"), 1)
            pe.wait_ge(sem("y_summed"), 4 * (grp + 1))
            for q_ in range(4):
                pe.wait_ge(sem("gsq_done"), 4 * grp + q_ + 1)
                last = nc.tensor.matmul(bank(4), ones[:, :], chunk(ea, q_ % 2), start=(q_ == 0), stop=(q_ == 3))
                last.then_inc(sem("gsum_done"), 1)
        phase("m2_out", ZC, 1, a_hi, a_lo, sem("y_split"), 0)
        norm_sum_matmul()
        if stop == "x7":
            return
        mlp(1)

    @block.scalar
    def _(act):
        g, split = Count(), Count()
        C = {k: Count() for k in ("norm", "sq", "x", "hf", "conv", "prod", "qraw", "land0", "land1")}
        C["free_dve"] = Count(2)

        def split_hi():
            if split.n >= total:
                return
            u = split.n % 2
            act.wait_ge(raw_landed[u], C[f"land{u}"].after(16))
            if split.n >= 2:
                act.wait_ge(tile_done, split.now() + 2)
            nc.scalar.activation(w_hi[:, u * TILE:(u + 1) * TILE], raw[:, u * TILE:(u + 1) * TILE],
                                 ACT.Copy).then_inc(w_hi_done, 1)
            split.after()

        def tiles(name, body, *counts):
            def step():
                split_hi()
                act.wait_ge(tile_done, tile_at(g.now()))
                body(g.n % 2)
                g.after()

            left = TILES[name]
            n = (left - (2 if split.n + left > total else 0)) // 2
            with rounds(act, n, (g, 2), (split, 2), (C["land0"], 16), (C["land1"], 16),
                        *[(c, 2 * per) for c, per in counts]):
                step()
                step()
            for _ in range(left - 2 * n):
                step()

        def square(src, slot, **scaled):
            act.wait_ge(sq_added, C["sq"].now())
            nc.scalar.activation(chunk(sq, slot), src, ACT.Square, **scaled).then_inc(sq_ready, 1)
            C["sq"].after()

        def norm_start():
            C["sq"].n = 9 * C["norm"].n

        def norm_std(eps, scale=1.0):
            act.wait_ge(norm_sum, C["norm"].after())
            nc.scalar.activation(rstd[:, :], bank(NORM), ACT.Sqrt, bias=eps, scale=scale).then_inc(std_done, 1)

        def x_squares():
            norm_start()
            for c in range(DC):
                act.wait_ge(x_ready, C["x"].after())
                square(chunk(x, c), c % 2)

        def split_norm(dst, shift=None):
            for c in range(DC):
                act.wait_ge(hf_done, C["hf"].after())
                b = 0.0 if shift is None else shift(c)
                nc.scalar.activation(chunk(dst, c), chunk(tg, c % 2), ACT.Identity, bias=b).then_inc(h_hi_done, 1)

        act.wait_ge(sem("x_landed"), 16)
        norm_start()
        for c in range(DC):
            square(chunk(x, c), c % 2)
        act.wait_ge(sem("vec_landed"), 16)
        nc.scalar.activation(cond[:, :], vs("c", 0, 8), ACT.Silu).then_inc(sem("cond_ready"), 1)
        norm_std(EPS_A)
        split_hi()
        split_hi()
        for c in range(DC):
            act.wait_ge(sem("pool_df"), c + 1)
            nc.scalar.activation(chunk(dd_hi, c), chunk(f, c), ACT.Copy).then_inc(sem("pool_dhi"), 1)
        norm_start()
        for grp in range(4):
            act.wait_ge(tile_done, grp + 1)
            for m in range(2):
                square(bank(2 * (grp % 2) + m), m, scale=v("pool_scale", 2 * grp + m))
            for m in range(2):
                ins = nc.scalar.activation(chunk(f, 2 * grp + m), bank(2 * (grp % 2) + m), ACT.Identity,
                                           scale=v("pool_scale", 2 * grp + m))
            ins.then_inc(pool_out, 1)
        g.after()
        norm_std(EPS_A)
        x_squares()
        norm_std(EPS_A)
        split_norm(h_hi)
        if stop == "x1":
            return

        def ffn(layer):
            wcol, bcol = 3 * 2 * FC * layer, 2 * FC * layer
            hidden = Count()

            def conv_glu(u):
                j = hidden.now()
                for m, t in ((0, tg), (1, tv)):
                    nc.scalar.activation(chunk(t, u), bank(2 * u + m), ACT.Identity,
                                         scale=v("conv_w", j + (wcol + 2 * 2 * FC + m * FC)),
                                         bias=v("conv_b", j + (bcol + m * FC))).then_inc(conv_pre, 1)
                act.wait_ge(gate_conv, C["conv"].after())
                nc.scalar.activation(chunk(gl, u), chunk(tg, u), ACT.Gelu_apprx_tanh).then_inc(gelu_done, 1)
                act.wait_ge(prod_done, C["prod"].after())
                nc.scalar.activation(chunk(a_hi, slot.now()), chunk(gl, u), ACT.Copy).then_inc(a_hi_done, 1)
                hidden.after()
                slot.after()

            out_chunk = Count()

            def copy_out(u):
                nc.scalar.activation(chunk(f, out_chunk.now()), bank(2 * u), ACT.Copy).then_inc(acc_free["act"], 1)
                out_chunk.after()

            def squares(u):
                act.wait_ge(acc_free["dve"], C["free_dve"].after())
                square(chunk(f, out_chunk.now()), (u + FIRST[f"ffn{layer}_out_b"]) % 2)
                out_chunk.after()

            for half in "ab":
                slot = Count()
                tiles(f"ffn{layer}_in_{half}", conv_glu, (hidden, 1), (slot, 1), (C["conv"], 1), (C["prod"], 1))
                C["free_dve"].n += FH
                out_chunk = Count()
                if half == "a":
                    tiles(f"ffn{layer}_out_a", copy_out, (out_chunk, 1))
                else:
                    norm_start()
                    tiles(f"ffn{layer}_out_b", squares, (out_chunk, 1), (C["free_dve"], 1), (C["sq"], 1))
            norm_std(EPS_A)
            x_squares()
            norm_std(EPS_A if layer == 0 else EPS_B)

        ffn(0)
        if stop == "x2":
            return

        act.wait_ge(sem("angles"), 1)
        nc.scalar.activation(cosT[:, :], sinT[:, :], ACT.Sin, scale=0.5).then_inc(sem("half_sin"), 1)
        nc.scalar.activation(chunk(tv, 1), sinT[:, :], ACT.Sin).then_inc(sem("full_sin"), 1)
        split_norm(a_hi)
        split_norm(h_hi)
        rope_done, qraw = sem("rope_done"), sem("qraw")

        def copy_raw(u):
            for m in range(2):
                act.wait_ge(rope_done, C["qraw"].now())
                nc.scalar.activation(chunk(tg, m), bank(2 * u + m), ACT.Copy).then_inc(qraw, 1)
                C["qraw"].after()

        split_hi()
        act.wait_ge(tile_done, tile_at(g.n))
        act.wait_ge(h_ready, 24)
        for m in range(2):
            nc.scalar.activation(chunk(tg, m), bank(2 * (g.n % 2) + m), ACT.Copy).then_inc(qraw, 1)
        for m in range(2):
            act.wait_ge(rope_done, m + 1)
            for half in range(2):
                dst0 = (2 * m + half) * (P + T) + P
                for to in range(2):
                    ins = nc.scalar.activation(kdup[64 * to:64 * to + 64, dst0:dst0 + T],
                                               sq[64 * half:64 * half + 64, m * T:(m + 1) * T], ACT.Copy)
            ins.then_inc(sem("k_copied"), 1)
        g.after()
        split_hi()
        act.wait_ge(tile_done, tile_at(g.n))
        for n in range(NB):
            ins = nc.scalar.activation(v_tok[:, (n + 1) * 256:(n + 2) * 256], bank(n, 256), ACT.Copy)
        ins.then_inc(sem("v_copied"), 1)
        g.after()
        C["qraw"].n = 1
        tiles("qproj", copy_raw, (C["qraw"], 2))

        N = {k: Count() for k in ("nm", "pt", "o")}

        def exps(gkv):
            b = gkv % 2
            act.wait_ge(sem("nm_ready"), N["nm"].after())
            for hh in range(4):
                o = b * 1024 + hh * 256
                nc.scalar.activation(s_sb[:, o:o + 256], s_sb[:, o:o + 256], ACT.Exp,
                                     bias=mx[:, b * 24 + 4 + hh:b * 24 + 5 + hh],
                                     accum_out=mx[:, b * 24 + 12 + hh:b * 24 + 13 + hh])
            nc.scalar.activation(mx[:, b * 24 + 16:b * 24 + 20], mx[:, b * 24 + 8:b * 24 + 12],
                                 ACT.Exp).then_inc(sem("exp_done"), 1)

        def outputs(gkv, n):
            b = gkv % 2
            act.wait_ge(sem("pt_psum"), N["pt"].after())
            nc.scalar.activation(p_t[:, b * 1024:b * 1024 + 512], bank(2), ACT.Copy).then_inc(sem("pt_a"), 1)
            act.wait_ge(sem("o_done"), N["o"].after(1) + 1)
            nc.scalar.activation(as3(h_hi[:, :], DC)[:, 2 * gkv:2 * gkv + 2, bass.ds(n * P, P)],
                                 as3(bank(6, 256), 2), ACT.Copy).then_inc(sem("o_hi"), 1)

        with rounds(act, NB, *[(c, 4) for c in N.values()]) as n:
            exps(0)
            for gkv in range(4):
                if gkv < 3:
                    exps(gkv + 1)
                outputs(gkv, n)

        o_chunk = Count()

        def copy_f(u):
            for m in range(2):
                square(bank(2 * u + m), m)
            for m in range(2):
                ins = nc.scalar.activation(chunk(f, o_chunk.now() + m), bank(2 * u + m), ACT.Copy)
            ins.then_inc(acc_free["act"], 1)
            o_chunk.after(2)

        norm_start()
        tiles("oproj", copy_f, (o_chunk, 2), (C["sq"], 2))
        norm_std(EPS_A)
        x_squares()
        norm_std(EPS_A)
        split_norm(h_hi)
        if stop == "x3":
            return
        ffn(1)
        if stop == "x4":
            return

        def sv(k, n=1):
            return small[:, k * 32:(k + n) * 32]

        split_norm(h_hi, lambda c: mod[:, c:c + 1])

        def copy_u(u):
            for m in range(2):
                ins = nc.scalar.activation(chunk(f, u_chunk.now() + m), bank(2 * u + m), ACT.Copy)
            ins.then_inc(acc_free["act"], 1)
            u_chunk.after(2)

        u_chunk = Count()
        nc.scalar.activation(sv(0), vs("log_dt", 0, 32), ACT.Exp).then_inc(sem("s5_dt"), 1)
        act.wait_ge(sem("s5_angles"), 1)
        nc.scalar.activation(sv(6), sv(1), ACT.Exp)
        nc.scalar.activation(sv(7), sv(4), ACT.Tanh, scale=0.5)
        nc.scalar.activation(sv(8), sv(3), ACT.Sin)
        nc.scalar.activation(sv(9), sv(3), ACT.Sin, scale=0.5).then_inc(sem("s5_funcs"), 1)
        tiles("s5_in", copy_u, (u_chunk, 2))
        act.wait_ge(sem("turns_done"), 1)
        nc.scalar.activation(sin5[:, :], turn5[:, :], ACT.Sin, scale=6.283185)
        nc.scalar.activation(cos5[:, :], turn5[:, :], ACT.Sin, scale=3.1415925).then_inc(sem("tables"), 1)
        for half in range(2):
            act.wait_ge(sem("b_t_psum"), half + 1)
            nc.scalar.activation(b_t[:, half * 1024:(half + 1) * 1024], ps[:, 6 * T:8 * T], ACT.Copy).then_inc(sem("b_t_done"), 1)
        S = {"done": Count(), "used": Count(2)}
        act.wait_ge(sem("turns_used"), 1)
        nc.scalar.activation(as3(ub[:, :], DC), as3(f[:, :], DC)[:, :, 0:P], ACT.Copy).then_inc(sem("ub_ready"), DC)

        def block5(b):
            for j in range(DC):
                act.wait_ge(sem("bu_done"), S["done"].after())
                act.wait_ge(sem("bu_used"), S["used"].now(1))
                S["used"].after()
                nc.scalar.activation(as3(bu5[j % 2][:, :], 4), as3(ps[:, 0:4 * T], 4)[:, :, 0:2 * P],
                                     ACT.Copy).then_inc(sem("bu_copied"), 1)
                if b is not None:
                    nc.scalar.activation(ub[:, j * P:(j + 1) * P], f[:, bass.ds(b * P + (j * T + P), P)],
                                         ACT.Copy).then_inc(sem("ub_ready"), 1)

        with rounds(act, NB - 1, *[(c, DC) for c in S.values()]) as b:
            block5(b)
        block5(None)
        act.wait_ge(sem("y5_read"), NB * DC + 2)
        for c in range(DC):
            if c >= 2:
                act.wait_ge(h_ready, 40 + c - 1)
            nc.scalar.activation(chunk(gl, c % 2), chunk(f, c), ACT.Gelu_apprx_tanh).then_inc(sem("act_step"), 1)
            act.wait_ge(sem("act_step"), c + 1)
            nc.scalar.activation(chunk(h_hi, c), chunk(gl, c % 2), ACT.Copy).then_inc(h_hi_done, 1)
        oc, xw = Count(), Count(freed["dve"]["s5_glu"])

        def glu(u):
            j = oc.now()
            nc.scalar.activation(chunk(tg, u), bank(2 * u), ACT.Identity, bias=v("b_glu", j)).then_inc(sem("glu_pre"), 1)
            nc.scalar.activation(chunk(tv, u), bank(2 * u + 1), ACT.Sigmoid, bias=v("b_glu", j + DC)).then_inc(sem("glu_pre"), 1)
            act.wait_ge(acc_free["dve"], xw.after())
            square(chunk(x, j), (u + FIRST["s5_glu"]) % 2)
            oc.after()

        norm_start()
        tiles("s5_glu", glu, (oc, 1), (xw, 1), (C["sq"], 1))
        norm_std(EPS_B)
        split_norm(h_hi, lambda c: mod[:, 24 + c:25 + c])
        if stop == "x5":
            return

        def mlp(layer):
            ar = Count(4 * FH + 2 * MH * layer)
            rsq = Count(2 * MH * layer)

            def relu(u):
                act.wait_ge(a_ready, ar.now(2))
                nc.scalar.activation(chunk(tg, u), bank(2 * u), ACT.Relu)
                nc.scalar.activation(chunk(tv, u), bank(2 * u + 1), ACT.Relu).then_inc(acc_free["act"], 1)
                for t in (tg, tv):
                    act.wait_ge(sem("relu_sq"), rsq.after())
                    nc.scalar.activation(chunk(a_hi, hc.now()), chunk(t, u), ACT.Copy).then_inc(a_hi_done, 1)
                    hc.after()
                ar.after(2)

            def nothing(u):
                pass

            oc = Count()

            def squares(u):
                act.wait_ge(acc_free["dve"], xw.after())
                square(chunk(x, oc.now()), (u + FIRST[f"mlp{layer}_out_b"]) % 2)
                oc.after()

            for half in "ab":
                hc = Count()
                tiles(f"mlp{layer}_in_{half}", relu, (hc, 2), (rsq, 2), (ar, 2))
                if half == "a":
                    tiles(f"mlp{layer}_out_a", nothing)
                else:
                    xw = Count(freed["dve"][f"mlp{layer}_out_b"])
                    norm_start()
                    tiles(f"mlp{layer}_out_b", squares, (oc, 1), (xw, 1), (C["sq"], 1))
            norm_std(EPS_B)

        mlp(0)
        split_norm(h_hi, lambda c: mod[:, ADA + c:ADA + c + 1])
        if stop == "x6":
            return

        split_hi()
        act.wait_ge(tile_done, tile_at(g.n))
        act.wait_ge(h_ready, 64)
        nc.scalar.activation(tg[0:32, 0:T], bank(2 * (g.n % 2), T, 0, 32), ACT.Identity, bias=v("dt_bias", 0, 32)).then_inc(sem("dt_copied"), 1)
        nc.scalar.activation(small32, v("a_log", 0, 32), ACT.Exp).then_inc(sem("a_exp"), 1)
        g.after()
        act.wait_ge(sem("dt_abs"), 1)
        nc.scalar.activation(tg[0:32, T:2 * T], gl[0:32, 0:T], ACT.Exp, scale=-1.0).then_inc(sem("dt_exp"), 1)
        act.wait_ge(sem("dt_onep"), 1)
        nc.scalar.activation(tv[0:32, 0:T], tv[0:32, T:2 * T], ACT.Ln).then_inc(sem("dt_ln"), 1)
        zc = Count()

        def silu_z(u):
            nc.scalar.activation(chunk(zt, zc.now()), bank(2 * u), ACT.Silu).then_inc(sem("xbc_done"), 1)
            nc.scalar.activation(chunk(zt, zc.now() + 1), bank(2 * u + 1), ACT.Silu).then_inc(acc_free["act"], 1)
            zc.after(2)

        tiles("m2_z", silu_z, (zc, 2))
        act.wait_ge(sem("acs_done"), 1)
        nc.scalar.activation(ea_row[0:32, :], acs_row[0:32, :], ACT.Exp)
        act.wait_ge(sem("rows_t"), 1)
        nc.scalar.activation(sq[:, 0:256], bank(6, 256), ACT.Copy).then_inc(sem("rows_copied"), 1)
        act.wait_ge(sem("decay_arg"), 1)
        nc.scalar.activation(decay, decay, ACT.Exp)
        nc.scalar.activation(cdec[:, :], bank(7, P), ACT.Exp, scale=float(D)).then_inc(sem("cdec_done"), 1)
        xc, xd, fd, gc = Count(), Count(ZC // 2), Count(freed["dve"]["m2_xbc"]), Count(2 * FH * 2)

        def conv_silu(u):
            act.wait_ge(sem("xbc_done"), xd.now(2))
            for m, t in ((0, tg), (1, tv)):
                nc.scalar.activation(chunk(t, u), bank(2 * u + m), ACT.Identity, scale=v("m2_conv_w", xc.now() + (3 * XC + m)),
                                     bias=v("m2_conv_b", xc.now() + m)).then_inc(conv_pre, 1)
            act.wait_ge(gate_conv, gc.after())
            nc.scalar.activation(chunk(xbc, xc.now()), chunk(tg, u), ACT.Silu).then_inc(sem("xbc_done"), 1)
            act.wait_ge(acc_free["dve"], fd.after())
            nc.scalar.activation(chunk(xbc, xc.now() + 1), chunk(tv, u), ACT.Silu).then_inc(sem("xbc_done"), 1)
            xc.after(2)
            xd.after(2)

        tiles("m2_xbc", conv_silu, (xc, 2), (xd, 2), (fd, 1), (gc, 1))

        for grp in range(4):
            act.wait_ge(sem("bt_done"), grp + 1)
            nc.scalar.activation(b_tok[:, 0:384], bank(4, 384), ACT.Copy).then_inc(sem("bt_copied"), 1)
            for hh in range(8):
                n, pair = 8 * grp + hh, 4 * grp + hh // 2
                if hh % 2 == 0:
                    act.wait_ge(sem("ea_done"), pair + 1)
                    if grp and hh == 0:
                        act.wait_ge(sem("gsum_done"), 4 * grp)
                    nc.scalar.activation(chunk(ea, (hh // 2) % 2), bank(6 + (hh // 2) % 2), ACT.Copy).then_inc(sem("ea_copied"), 1)
                act.wait_ge(sem("min_done"), n + 1)
                nc.scalar.activation(chunk(tg, hh % 2), chunk(tg, hh % 2), ACT.Exp).then_inc(sem("exp2_done"), 1)
            for q_ in range(4):
                act.wait_ge(sem("gated"), 4 * grp + q_ + 1)
                if q_ < 2:
                    act.wait_ge(sem("y_summed"), 4 * (grp + 1))
                else:
                    act.wait_ge(sem("gsum_done"), 4 * grp + q_ - 1)
                nc.scalar.activation(chunk(ea, q_ % 2), chunk(yg, q_), ACT.Square).then_inc(sem("gsq_done"), 1)
            act.wait_ge(sem("gsum_done"), 4 * (grp + 1))
            nc.scalar.activation(rstd[:, :], bank(4), ACT.Sqrt, bias=EPS_B, scale=D / 512.0).then_inc(sem("gstd_done"), 1)
            for q_ in range(4):
                act.wait_ge(sem("y_normed"), 4 * grp + q_ + 1)
                nc.scalar.activation(chunk(a_hi, 4 * grp + q_), chunk(yg, q_), ACT.Copy).then_inc(sem("y_hi"), 1)
        oc, xw = Count(), Count(freed["dve"]["m2_out"])

        def squares(u):
            act.wait_ge(acc_free["dve"], xw.after())
            square(chunk(x, oc.now()), (u + FIRST["m2_out"]) % 2)
            oc.after()

        norm_start()
        tiles("m2_out", squares, (oc, 1), (xw, 1), (C["sq"], 1))
        norm_std(EPS_B)
        split_norm(h_hi, lambda c: mod[:, ADA + 24 + c:ADA + 25 + c])
        if stop == "x7":
            return
        mlp(1)

    @block.vector
    def _(dve):
        g, split = Count(), Count()
        C = {k: Count() for k in ("norm", "step", "hi", "lo", "conv", "a_hi", "x", "qraw")}

        def mark(ins):
            ins.then_inc(dve_step, 1)
            return C["step"].after()

        def split_lo():
            if split.n >= total:
                return
            u = split.n % 2
            dve.wait_ge(w_hi_done, split.after())
            o = slice(u * TILE, (u + 1) * TILE)
            nc.vector.tensor_tensor(w_lo[:, o], raw[:, o], w_hi[:, o].bitcast(f32), SUB).then_inc(w_split, 1)

        def tiles(name, body, *counts):
            def step():
                split_lo()
                body(g.n % 2)
                g.after()

            left = TILES[name]
            n = (left - (2 if split.n + left > total else 0)) // 2
            with rounds(dve, n, (g, 2), (split, 2), *[(c, 2 * per) for c, per in counts]):
                step()
                step()
            for _ in range(left - 2 * n):
                step()

        def norm_rstd():
            dve.wait_ge(std_done, C["norm"].after())
            at_ = mark(nc.vector.reciprocal(rstd[:, :], rstd[:, :]))
            dve.wait_ge(dve_step, at_)

        def norm_x(gains, dst_hi, dst_lo, shift=None):
            def lo(c):
                dve.wait_ge(h_hi_done, C["hi"].after())
                C["lo"].after()
                args = (chunk(dst_lo, c), chunk(tg, c % 2))
                if shift is None:
                    ins = nc.vector.tensor_tensor(*args, chunk(dst_hi, c).bitcast(f32), SUB)
                else:
                    ins = nc.vector.scalar_tensor_tensor(*args, shift(c), chunk(dst_hi, c).bitcast(f32), ADD, SUB)
                ins.then_inc(h_ready, 1)

            for c in range(DC):
                dve.wait_ge(h_ready, C["lo"].now())
                nc.vector.scalar_tensor_tensor(chunk(tg, c % 2), chunk(x, c), gains(c), rstd[:, :],
                                               MUL, MUL).then_inc(hf_done, 1)
                if c:
                    lo(c - 1)
            lo(DC - 1)

        def post_norm(gain_name, col):
            norm_rstd()
            steps = []
            for c in range(DC + 1):
                if c < DC:
                    steps.append(mark(nc.vector.scalar_tensor_tensor(
                        chunk(f, c), chunk(f, c), v(gain_name, col + c), rstd[:, :], MUL, MUL)))
                if c:
                    dve.wait_ge(dve_step, steps[c - 1])
                    nc.vector.tensor_tensor(chunk(x, c - 1), chunk(x, c - 1), chunk(f, c - 1), ADD).then_inc(x_ready, 1)

        dve.wait_ge(sem("pads_zero"), 1)
        dve.wait_ge(sem("vec_landed"), 16)
        norm_rstd()
        hp3 = as3(hp[:, :], DC)
        at_h = []
        for c in range(DC):
            at_h.append(mark(nc.vector.scalar_tensor_tensor(hp3[:, c, 16:], chunk(x, c), v("mix_pre", c), rstd[:, :], MUL, MUL)))
        dve.wait_ge(sem("edge_landed"), 16)
        w3 = [as3(w[:, :], 2) for w in win]

        def pool_lo(grp):
            for c in (2 * grp, 2 * grp + 1):
                dve.wait_ge(sem("pool_dhi"), c + 1)
                nc.vector.tensor_tensor(chunk(dd_lo, c), chunk(f, c), chunk(dd_hi, c).bitcast(f32), SUB).then_inc(pool_d, 1)

        for grp in range(4):
            w = 2 << grp
            src, last = hp3[:, 2 * grp:2 * grp + 2], at_h[2 * grp + 1]
            if grp:
                dve.wait_ge(sem("pool_df"), 2 * grp)
            for lv in range(grp + 1):
                dve.wait_ge(dve_step, last)
                sh = 1 << lv
                last = mark(nc.vector.tensor_tensor(w3[lv % 2][:, :, 16:], src[:, :, 16:], src[:, :, 16 - sh:16 - sh + T], ADD))
                src = w3[lv % 2]
            dve.wait_ge(dve_step, last)
            e = edge[:, grp * 16:(grp + 1) * 16].rearrange("p (o a) -> p o a", o=1).broadcast_to([P, 2, 16])
            last = mark(nc.vector.tensor_tensor(src[:, :, 16:32], src[:, :, 16:32], e, MUL))
            dve.wait_ge(dve_step, last)
            for k in range(2):
                nc.vector.scalar_tensor_tensor(chunk(f, 2 * grp + k), src[:, k, 16:], 1.0 / w, hp3[:, 2 * grp + k, 16:],
                                               MUL, SUB).then_inc(sem("pool_df"), 1)
            if grp:
                pool_lo(grp - 1)
            if grp == 0:
                split_lo()
        pool_lo(3)
        split_lo()
        g.after()
        post_norm("mix_post", 0)
        norm_rstd()
        norm_x(lambda c: v("ffn_pre", c), h_hi, h_lo)
        if stop == "x1":
            return

        def ffn(layer):
            wcol = 3 * 2 * FC * layer
            hidden = Count()

            def conv_glu(u):
                j = hidden.now()
                for s in (1, 2):
                    for m, t in ((0, tg), (1, tv)):
                        if s == 1:
                            dve.wait_ge(conv_pre, C["conv"].after())
                        else:
                            dve.wait_ge(dve_step, C["step"].now(1 - m))
                        ins = nc.vector.scalar_tensor_tensor(
                            t[:, u * T + s:(u + 1) * T], ps[:, (2 * u + m) * T:(2 * u + m) * T + T - s],
                            v("conv_w", j + (wcol + (2 - s) * 2 * FC + m * FC)), t[:, u * T + s:(u + 1) * T], MUL, ADD)
                        if s == 1:
                            mark(ins)
                        else:
                            ins.then_inc(gate_conv if m == 0 else acc_free["dve"], 1)
                dve.wait_ge(a_hi_done, C["a_hi"].after())
                nc.vector.tensor_tensor(chunk(a_lo, slot.now()), chunk(gl, u), chunk(a_hi, slot.now()).bitcast(f32),
                                        SUB).then_inc(a_ready, 1)
                hidden.after()
                slot.after()

            def nothing(u):
                pass

            out_chunk = Count()

            def add_out(u):
                dve.wait_ge(tile_done, tile_at(g.now()))
                d = chunk(f, out_chunk.now())
                nc.vector.tensor_tensor(d, d, bank(2 * u), ADD).then_inc(acc_free["dve"], 1)
                out_chunk.after()

            for half in "ab":
                slot = Count()
                tiles(f"ffn{layer}_in_{half}", conv_glu, (hidden, 1), (slot, 1), (C["conv"], 2), (C["step"], 2), (C["a_hi"], 1))
                if half == "a":
                    tiles(f"ffn{layer}_out_a", nothing)
                else:
                    dve.wait_ge(acc_free["act"], freed["act"][f"ffn{layer}_in_b"])
                    tiles(f"ffn{layer}_out_b", add_out, (out_chunk, 1))
            post_norm("ffn_post", 8 * layer)

        ffn(0)
        if stop == "x2":
            return

        dve.wait_ge(sem("pos_landed"), 16)

        def chain(ins):
            dve.wait_ge(dve_step, mark(ins))

        chain(nc.vector.tensor_copy(cosT[:, :], posi[:, :]))
        chain(nc.vector.tensor_scalar(sinT[:, :], cosT[:, :], v("inv_freq"), None, MUL))
        chain(nc.vector.tensor_scalar(cosT[:, :], sinT[:, :], float(1 / (2 * np.pi)), MAGIC, MUL, ADD))
        chain(nc.vector.tensor_scalar(cosT[:, :], cosT[:, :], MAGIC, None, SUB))
        for part in (TWO_PI_A, TWO_PI_B, TWO_PI_C):
            chain(nc.vector.scalar_tensor_tensor(sinT[:, :], cosT[:, :], -float(part), sinT[:, :], MUL, ADD))
        nc.vector.tensor_scalar(sinT[:, :], sinT[:, :], 3.1415925, -3.1415925, ALU.min, MAX).then_inc(sem("angles"), 1)
        norm_rstd()
        norm_x(lambda c: v("kv_norm", c), a_hi, a_lo)
        norm_x(lambda c: v("mix_pre", 8 + c), h_hi, h_lo)
        dve.wait_ge(sem("half_sin"), 1)
        chain(nc.vector.tensor_tensor(cosT[:, :], cosT[:, :], cosT[:, :], MUL))
        chain(nc.vector.tensor_scalar(cosT[:, :], cosT[:, :], -2.0, 1.0, MUL, ADD))
        dve.wait_ge(sem("full_sin"), 1)
        chain(nc.vector.tensor_scalar(sinT[:, :], chunk(tv, 1), v("rope_sign"), None, MUL))

        def rope(u):
            for m in range(2):
                dve.wait_ge(sem("qraw"), C["qraw"].after())
                nc.vector.tensor_tensor(chunk(tv, m), chunk(tg, m), cosT[:, :], MUL)
                dve.wait_ge(sem("rot"), C["qraw"].now())
                nc.vector.tensor_tensor(chunk(gl, m), bank(6 + m), sinT[:, :], MUL).then_inc(sem("rope_parts"), 1)

        split_lo()
        rope(0)
        g.after()
        split_lo()
        g.after()
        tiles("qproj", rope, (C["qraw"], 2))

        N = {k: Count() for k in ("s", "exp", "pt", "o")}

        def soften(gkv):
            b = gkv % 2
            m4 = lambda i: mx[:, b * 24 + 4 * i:b * 24 + 4 * i + 4]
            sb4 = as3(s_sb[:, b * 1024:(b + 1) * 1024], 4)
            dve.wait_ge(sem("s_done"), N["s"].after())
            mask4 = mb[:, :].rearrange("p (o k) -> p o k", o=1).broadcast_to([P, 4, 256])
            nc.vector.scalar_tensor_tensor(sb4, as3(ps[:, 0:1024], 4), 0.125, mask4, MUL, ADD).then_inc(sem("s_read"), 1)
            dve.wait_ge(sem("s_read"), N["s"].now(-1))
            chain(nc.vector.tensor_reduce(m4(0), sb4, AX.X, MAX))
            sinks4 = vs("sinks", 4 * gkv, 4 * gkv + 4)
            chain(nc.vector.tensor_tensor(m4(0), m4(0), sinks4, MAX))
            chain(nc.vector.tensor_scalar(m4(1), m4(0), -1.0, None, MUL))
            nc.vector.tensor_tensor(m4(2), sinks4, m4(1), ADD).then_inc(sem("nm_ready"), 1)

        def weigh(gkv, n):
            b = gkv % 2
            m4 = lambda i: mx[:, b * 24 + 4 * i:b * 24 + 4 * i + 4]
            sb4 = as3(s_sb[:, b * 1024:(b + 1) * 1024], 4)
            dve.wait_ge(sem("exp_done"), N["exp"].after())
            chain(nc.vector.tensor_tensor(m4(3), m4(3), m4(4), ADD))
            chain(nc.vector.reciprocal(m4(5), m4(3)))
            rec = m4(5).rearrange("p (a o) -> p a o", o=1).broadcast_to([P, 4, 256])
            nc.vector.tensor_tensor(sb4, sb4, rec, MUL).then_inc(sem("p_ready"), 1)
            dve.wait_ge(sem("pt_psum"), N["pt"].after())
            nc.vector.tensor_copy(p_t[:, b * 1024 + 512:(b + 1) * 1024], bank(3)).then_inc(sem("pt_b"), 1)
            dve.wait_ge(sem("o_hi"), N["o"].after())
            dst = (slice(None), slice(2 * gkv, 2 * gkv + 2), bass.ds(n * P, P))
            nc.vector.tensor_tensor(as3(h_lo[:, :], DC)[dst], as3(bank(6, 256), 2), as3(h_hi[:, :], DC)[dst].bitcast(f32),
                                    SUB).then_inc(sem("o_split"), 1)

        with rounds(dve, NB, (C["step"], 4 * 5), *[(c, 4) for c in N.values()]) as n:
            soften(0)
            for gkv in range(4):
                if gkv < 3:
                    soften(gkv + 1)
                weigh(gkv, n)

        def nothing(u):
            pass

        tiles("oproj", nothing)
        post_norm("mix_post", 8)
        norm_rstd()
        norm_x(lambda c: v("ffn_pre", 8 + c), h_hi, h_lo)
        if stop == "x3":
            return
        ffn(1)
        if stop == "x4":
            return

        dve.wait_ge(ada_used, ADA_TILES)
        chain(nc.vector.tensor_tensor(mod[:, :], bank(MOD, 2 * ADA), vs("ada_b", 0, 2 * ADA), ADD))

        def modulation(layer, scale_at, norm):
            c0 = ADA * layer + scale_at
            a, _ = VECS[norm]
            chain(nc.vector.scalar_tensor_tensor(gain[:, :], mod[:, c0:c0 + 8], 1.0, vec[:, a + 8 * layer:a + 8 * layer + 8], ADD, MUL))

        def norm_mod(layer, shift_at):
            norm_rstd()
            norm_x(lambda c: gain[:, c:c + 1], h_hi, h_lo, lambda c: mod[:, ADA * layer + shift_at + c:ADA * layer + shift_at + c + 1])

        modulation(0, 8, "norm_mix")
        norm_mod(0, 0)

        def sv(k):
            return small[:, k * 32:(k + 1) * 32]

        TT = lambda o, a, b, op: chain(nc.vector.tensor_tensor(sv(o), a, b, op))
        TS = lambda o, a, s1, s2, op1, op2=None: chain(
            nc.vector.tensor_scalar(sv(o), a, s1, s2, op1, op2) if op2 is not None else nc.vector.tensor_scalar(sv(o), a, s1, None, op1))
        STT = lambda o, a, s1, b, op1, op2: chain(nc.vector.scalar_tensor_tensor(sv(o), a, s1, b, op1, op2))
        lre, lim = vs("lam_re", 0, 32), vs("lam_im", 0, 32)
        dve.wait_ge(sem("s5_dt"), 1)
        TT(1, lre, sv(0), MUL)
        TT(2, lim, sv(0), MUL)
        TS(3, sv(2), float(1 / (2 * np.pi)), MAGIC, MUL, ADD)
        TS(5, sv(3), MAGIC, None, SUB)
        STT(3, sv(5), -TWO_PI_A, sv(2), MUL, ADD)
        STT(3, sv(5), -TWO_PI_B, sv(3), MUL, ADD)
        STT(3, sv(5), -float(TWO_PI_C), sv(3), MUL, ADD)
        TS(3, sv(3), 3.1415925, -3.1415925, ALU.min, MAX)
        TS(10, sv(3), float(1 / (2 * np.pi)), None, MUL)
        nc.vector.tensor_scalar(sv(4), sv(1), -0.5, 0.5, MAX, ALU.min).then_inc(sem("s5_angles"), 1)
        dve.wait_ge(sem("s5_funcs"), 1)
        TS(11, sv(7), -1.0, 1.0, MUL, ADD)
        chain(nc.vector.reciprocal(sv(11), sv(11)))
        STT(11, sv(7), 2.0, sv(11), MUL, MUL)
        TS(12, sv(6), 1.0, 3e38, SUB, ALU.min)
        TT(13, sv(1), sv(4), ALU.is_equal)
        TT(11, sv(11), sv(12), SUB)
        TT(11, sv(11), sv(13), MUL)
        TT(11, sv(11), sv(12), ADD)
        TT(12, sv(9), sv(9), MUL)
        TS(13, sv(12), -2.0, None, MUL)
        TS(12, sv(12), -2.0, 1.0, MUL, ADD)
        TT(12, sv(11), sv(12), MUL)
        TT(12, sv(12), sv(13), ADD)
        TT(13, sv(6), sv(8), MUL)
        TT(14, lre, lre, MUL)
        TT(15, lim, lim, MUL)
        TT(14, sv(14), sv(15), ADD)
        chain(nc.vector.reciprocal(sv(14), sv(14)))
        TT(15, sv(12), lre, MUL)
        TT(16, sv(13), lim, MUL)
        TT(15, sv(15), sv(16), ADD)
        TT(15, sv(15), sv(14), MUL)
        TT(16, sv(13), lre, MUL)
        TT(17, sv(12), lim, MUL)
        TT(16, sv(16), sv(17), SUB)
        TT(16, sv(16), sv(14), MUL)
        dve.wait_ge(sem("b_landed"), 16)
        wide = lambda k: sv(k).rearrange("p (a o) -> p a o", o=1).broadcast_to([P, 32, 32])
        t3 = lambda ap: as3(ap, 32)
        br, bi_ = t3(b_raw[:, 0:1024]), t3(b_raw[:, 1024:2048])
        for half, (x_, y_, op) in enumerate(((br, bi_, SUB), (bi_, br, ADD))):
            dst = t3(b_bar[:, half * 1024:(half + 1) * 1024])
            chain(nc.vector.tensor_tensor(dst, x_, wide(15), MUL))
            chain(nc.vector.tensor_tensor(t3(b_tmp), y_, wide(16), MUL))
            nc.vector.tensor_tensor(dst, dst, t3(b_tmp), op).then_inc(sem("b_bar_done"), 1)
            dve.wait_ge(sem("b_bar_done"), half + 1)
        tok = vs("tok", 0, P).rearrange("p (o t) -> p o t", o=1).broadcast_to([P, 32, P])
        phi = sv(10).rearrange("p (a o) -> p a o", o=1).broadcast_to([P, 32, P])
        chain(nc.vector.tensor_tensor(as3(turn5[:, :], 32), tok, phi, MUL))
        chain(nc.vector.tensor_scalar(cos5[:, :], turn5[:, :], MAGIC, MAGIC, ADD, SUB))
        nc.vector.tensor_tensor(turn5[:, :], turn5[:, :], cos5[:, :], SUB).then_inc(sem("turns_done"), 1)
        tiles("s5_in", nothing)
        dve.wait_ge(sem("tables"), 1)
        chain(nc.vector.tensor_tensor(cos5[:, :], cos5[:, :], cos5[:, :], MUL))
        nc.vector.tensor_scalar(cos5[:, :], cos5[:, :], -2.0, 1.0, MUL, ADD).then_inc(sem("turns_used"), 1)
        dve.wait_ge(sem("turns_used"), 1)

        S = {"bu": Count(1), "v": Count(), "scan": Count(1), "carry": Count(2), "y": Count(2)}
        cs = lambda t, j: as3(t[:, j * T:(j + 1) * T], 4)

        def rotate_in(j):
            w = [as3(t[:, :], 4) for t in w5[j % 2]]
            b4 = as3(bu5[j % 2][:, :], 4)
            dve.wait_ge(sem("bu_copied"), S["bu"].after())
            dve.wait_ge(sem("scanned"), S["scan"].now())
            nc.vector.tensor_tensor(w[0], cs(cos5, j), b4[:, :, 0:P], MUL)
            nc.vector.tensor_tensor(w[1], cs(sin5, j), b4[:, :, P:2 * P], MUL).then_inc(sem("rot_in"), 1)
            nc.vector.tensor_tensor(w[2], cs(cos5, j), b4[:, :, P:2 * P], MUL)
            nc.vector.tensor_tensor(w[3], cs(sin5, j), b4[:, :, 0:P], MUL).then_inc(sem("bu_used"), 1)

        def scan(j):
            dve.wait_ge(sem("carry"), S["carry"].now(1))
            S["carry"].after()
            for half in range(2):
                dve.wait_ge(sem("v_ready"), S["v"].after())
                for i in range(4):
                    s_ = 4 * j + i
                    ins = nc.vector.tensor_tensor_scan(
                        g5[j % 2][half][:, i * P:(i + 1) * P], sv(6)[:, s_:s_ + 1].broadcast_to([P, P]),
                        w5[j % 2][2 * half][:, i * P:(i + 1) * P], sv(18 + half)[:, s_:s_ + 1], MUL, ADD)
            ins.then_inc(sem("scanned"), 1)
            S["scan"].after()

        def rotate_out(j):
            dve.wait_ge(sem("scanned"), S["scan"].now())
            gr, gi = g5[j % 2]
            nc.vector.tensor_tensor(p5[j % 2][0][:, :], cos5[:, j * T:(j + 1) * T], gr[:, :], MUL)
            nc.vector.tensor_tensor(p5[j % 2][1][:, :], sin5[:, j * T:(j + 1) * T], gi[:, :], MUL).then_inc(sem("p_dve"), 1)

        def finish(j, b):
            dve.wait_ge(sem("y5_done"), S["y"].after())
            c0 = j * T + b * P
            uj = f[:, c0:c0 + P] if isinstance(b, int) else f[:, bass.ds(c0, P)]
            nc.vector.scalar_tensor_tensor(uj, uj, v("s5_d", j), bank(6 + j % 2, P), MUL, ADD).then_inc(sem("y5_read"), 1)

        def block5(b, more):
            for j in range(DC):
                if j < DC - 1 or more:
                    rotate_in((j + 1) % DC)
                scan(j)
                rotate_out(j)
                if j:
                    finish(j - 1, b)
            finish(DC - 1, b)

        rotate_in(0)
        with rounds(dve, NB - 1, *[(c, DC * (2 if k == "v" else 1)) for k, c in S.items()]) as b:
            block5(b, True)
        block5(NB - 1, False)
        dve.wait_ge(sem("carry"), 2 + DC * NB)
        for c in range(DC):
            dve.wait_ge(h_hi_done, C["hi"].after())
            C["lo"].after()
            nc.vector.tensor_tensor(chunk(h_lo, c), chunk(gl, c % 2), chunk(h_hi, c).bitcast(f32), SUB).then_inc(h_ready, 1)
        oc, gp_ = Count(), Count()

        def glu(u):
            dve.wait_ge(sem("glu_pre"), gp_.after(2))
            chain(nc.vector.tensor_tensor(chunk(tg, u), chunk(tg, u), chunk(tv, u), MUL))
            xx = chunk(x, oc.now())
            nc.vector.scalar_tensor_tensor(xx, chunk(tg, u), mod[:, bass.ds(oc.now() + 16, 1)], xx, MUL, ADD).then_inc(acc_free["dve"], 1)
            oc.after()

        tiles("s5_glu", glu, (oc, 1), (gp_, 2), (C["step"], 1))
        modulation(0, 32, "norm_mlp")
        norm_mod(0, 24)
        if stop == "x5":
            return

        def mlp(layer):
            fa = Count(freed["act"][f"mlp{layer}_in_a"])

            def squared(u):
                dve.wait_ge(acc_free["act"], fa.after())
                for t in (tg, tv):
                    nc.vector.tensor_tensor(chunk(t, u), chunk(t, u), chunk(t, u), MUL).then_inc(sem("relu_sq"), 1)
                for t in (tg, tv):
                    dve.wait_ge(a_hi_done, C["a_hi"].after())
                    nc.vector.tensor_tensor(chunk(a_lo, hc.now()), chunk(t, u), chunk(a_hi, hc.now()).bitcast(f32), SUB).then_inc(a_ready, 1)
                    hc.after()

            def residual(u):
                dve.wait_ge(tile_done, tile_at(g.now()))
                xx = chunk(x, oc.now())
                nc.vector.scalar_tensor_tensor(xx, bank(2 * u), mod[:, bass.ds(oc.now() + (ADA * layer + 40), 1)], xx,
                                               MUL, ADD).then_inc(acc_free["dve"], 1)
                oc.after()

            for half in "ab":
                hc, oc = Count(), Count()
                tiles(f"mlp{layer}_in_{half}", squared, (fa, 1), (hc, 2), (C["a_hi"], 2))
                if half == "b":
                    dve.wait_ge(acc_free["dve"], freed["dve"][f"mlp{layer}_out_b"])
                tiles(f"mlp{layer}_out_{half}", residual, (oc, 1))

        mlp(0)
        modulation(1, 8, "norm_mix")
        norm_mod(1, 0)
        if stop == "x6":
            return

        r32 = slice(0, 32)
        V, E_, L, W_, Ab = tg[r32, 0:T], tg[r32, T:2 * T], tv[r32, 0:T], tv[r32, T:2 * T], gl[r32, 0:T]
        split_lo()
        g.after()
        dve.wait_ge(sem("dt_copied"), 1)
        nc.vector.memset(one_col[:, :], 1.0)
        nc.vector.scalar_tensor_tensor(Ab, V, -1.0, V, MUL, MAX).then_inc(sem("dt_abs"), 1)
        dve.wait_ge(sem("dt_exp"), 1)
        nc.vector.tensor_scalar(W_, E_, 1.0, None, ADD).then_inc(sem("dt_onep"), 1)
        dve.wait_ge(sem("dt_ln"), 1)
        chain(nc.vector.tensor_scalar(W_, W_, 1.0, None, SUB))
        chain(nc.vector.tensor_scalar(Ab, W_, 0.0, None, ALU.is_equal))
        chain(nc.vector.tensor_tensor(W_, W_, Ab, ADD))
        chain(nc.vector.tensor_tensor(L, L, Ab, ADD))
        chain(nc.vector.reciprocal(W_, W_))
        chain(nc.vector.tensor_tensor(L, L, E_, MUL))
        chain(nc.vector.tensor_tensor(L, L, W_, MUL))
        chain(nc.vector.scalar_tensor_tensor(dt_row[r32, :], V, 0.0, L, MAX, ADD))
        dve.wait_ge(sem("a_exp"), 1)
        chain(nc.vector.tensor_scalar(Ab, dt_row[r32, :], small32, -1.0, MUL, MUL))
        for c in range(NB):
            o = slice(c * P, (c + 1) * P)
            chain(nc.vector.tensor_tensor_scan(acs_row[r32, o], one_col[r32, :].broadcast_to([32, P]), Ab[:, o], 0.0, MUL, ADD))
        for c in range(NB):
            ins = nc.vector.tensor_scalar(diag[r32, c * 32:(c + 1) * 32], ident[r32, 0:32], acs_row[r32, (c + 1) * P - 1:(c + 1) * P], None, MUL)
        ins.then_inc(sem("acs_done"), 1)
        tiles("m2_z", nothing)
        dve.wait_ge(sem("rows_copied"), 1)
        dve.wait_ge(sem("alast_done"), 1)
        nc.vector.scalar_tensor_tensor(decay, bank(7, P), float(D), acs_t, MUL, SUB).then_inc(sem("decay_arg"), 1)
        xc = Count()

        def conv4(u):
            for s in (1, 2, 3):
                for m, t in ((0, tg), (1, tv)):
                    if s == 1:
                        dve.wait_ge(conv_pre, C["conv"].after())
                    else:
                        dve.wait_ge(dve_step, C["step"].now(0 if s == 3 and m else 1))
                    ins = nc.vector.scalar_tensor_tensor(
                        t[:, u * T + s:(u + 1) * T], ps[:, (2 * u + m) * T:(2 * u + m) * T + T - s],
                        v("m2_conv_w", xc.now() + ((3 - s) * XC + m)), t[:, u * T + s:(u + 1) * T], MUL, ADD)
                    if s < 3:
                        mark(ins)
                    else:
                        ins.then_inc(gate_conv if m == 0 else acc_free["dve"], 1)
            xc.after(2)

        tiles("m2_xbc", conv4, (xc, 2), (C["conv"], 2), (C["step"], 4))

        dve.wait_ge(sem("cdec_done"), 1)
        dve.wait_ge(sem("upper_landed"), 16)
        for grp in range(4):
            for c in range(NB):
                dve.wait_ge(sem("xt_done"), 4 * grp + c + 1)
                d8 = dt_t[:, c * 32 + 8 * grp:c * 32 + 8 * grp + 8].rearrange("p (a o) -> p a o", o=1).broadcast_to([P, 8, 64])
                nc.vector.tensor_tensor(as3(xdt[:, c * T:(c + 1) * T], 8), as3(bank(c), 8), d8, MUL).then_inc(sem("xdt_done"), 1)
            dve.wait_ge(sem("cb_done"), grp + 1)
            up = upper[:, :].rearrange("p (o k) -> p o k", o=1).broadcast_to([P, NB, P])
            nc.vector.tensor_tensor(as3(cbm[:, :], NB), as3(bank(5), NB), up, MUL).then_inc(sem("cb_masked"), 1)
            for c in range(NB - 1):
                dve.wait_ge(sem("st_done"), 3 * grp + c + 1)
                dst = prev[:, c * T:(c + 1) * T]
                if c == 0:
                    nc.vector.tensor_copy(dst, bank(6)).then_inc(sem("prev_done"), 1)
                else:
                    dve.wait_ge(sem("prev_done"), 3 * grp + c)
                    h8 = cdec[:, c * 32 + 8 * grp:c * 32 + 8 * grp + 8].rearrange("p (a o) -> p a o", o=1).broadcast_to([P, 8, 64])
                    chain(nc.vector.tensor_tensor(as3(ytmp[:, :], 8), as3(prev[:, (c - 1) * T:c * T], 8), h8, MUL))
                    nc.vector.tensor_tensor(dst, ytmp[:, :], bank((6, 7, 4)[c]), ADD).then_inc(sem("prev_done"), 1)

            def differ(hh):
                n = 8 * grp + hh
                dve.wait_ge(sem("bc_done"), n + 1)
                if n >= 2:
                    dve.wait_ge(sem("yd_done"), n - 1)
                a_s = as3(acs_t, NB)[:, :, n:n + 1].broadcast_to([P, NB, P])
                nc.vector.tensor_tensor(as3(chunk(tg, hh % 2), NB), as3(bank(hh % 2), NB), a_s, SUB).then_inc(sem("diff_done"), 1)

            differ(0)
            for hh in range(8):
                n, q_ = 8 * grp + hh, hh // 2
                pair = 4 * grp + q_
                if hh < 7:
                    differ(hh + 1)
                dve.wait_ge(sem("exp2_done"), n + 1)
                nc.vector.tensor_tensor(chunk(tg, hh % 2), chunk(tg, hh % 2), cbm[:, :], MUL).then_inc(sem("m_ready"), 1)
                if hh % 2:
                    dve.wait_ge(sem("off_done"), pair + 1)
                    dve.wait_ge(sem("ea_copied"), pair + 1)
                    chain(nc.vector.tensor_tensor(ytmp[:, P:], bank(4 + q_ % 2, T - P, off=P), ea[:, (q_ % 2) * T + P:(q_ % 2 + 1) * T], MUL))
                    dve.wait_ge(sem("yd_done"), n + 1)
                    if grp:
                        dve.wait_ge(sem("y_split"), 4 * (grp - 1) + q_ + 1)
                    chain(nc.vector.scalar_tensor_tensor(chunk(yg, q_), chunk(xbc, pair), v("m2_d", pair), bank(2 + q_ % 2), MUL, ADD))
                    yy = yg[:, q_ * T + P:(q_ + 1) * T]
                    nc.vector.tensor_tensor(yy, yy, ytmp[:, P:], ADD).then_inc(sem("y_summed"), 1)
                    dve.wait_ge(sem("y_summed"), pair + 1)
            dve.wait_ge(sem("gstd_done"), grp + 1)
            chain(nc.vector.reciprocal(rstd[:, :], rstd[:, :]))
            for q_ in range(4):
                n = 4 * grp + q_
                nc.vector.scalar_tensor_tensor(chunk(yg, q_), chunk(yg, q_), v("m2_norm", n), rstd[:, :], MUL, MUL).then_inc(sem("y_normed"), 1)
            for q_ in range(4):
                n = 4 * grp + q_
                dve.wait_ge(sem("y_hi"), n + 1)
                nc.vector.tensor_tensor(chunk(a_lo, n), chunk(yg, q_), chunk(a_hi, n).bitcast(f32), SUB).then_inc(sem("y_split"), 1)
        oc = Count()

        def residual(u):
            dve.wait_ge(tile_done, tile_at(g.now()))
            xx = chunk(x, oc.now())
            nc.vector.scalar_tensor_tensor(xx, bank(2 * u), mod[:, bass.ds(oc.now() + (ADA + 16), 1)], xx, MUL, ADD).then_inc(acc_free["dve"], 1)
            oc.after()

        tiles("m2_out", residual, (oc, 1))
        modulation(1, 32, "norm_mlp")
        norm_mod(1, 24)
        if stop == "x7":
            return
        mlp(1)
        norm_rstd()
        for c in range(DC):
            nc.vector.scalar_tensor_tensor(chunk(x, c), chunk(x, c), v("final", c), rstd[:, :], MUL, MUL).then_inc(sem("y_ready"), 1)

    @block.gpsimd
    def _(gp):
        C = {k: Count() for k in ("norm", "gelu", "ada", "used", "rope")}
        C["free_dve"] = Count(2)

        def norm_adds():
            n = C["norm"].n
            if n:
                gp.wait_ge(norm_sum, n)
            gp.memset(sqsum[:, :], 0.0).then_inc(sq_added, 1)
            for c in range(DC):
                gp.wait_ge(sq_ready, DC * n + c + 1)
                gp.wait_ge(sq_added, 9 * n + c + 1)
                gp.tensor_tensor(sqsum[:, :], sqsum[:, :], chunk(sq, c % 2), ADD).then_inc(sq_added, 1)
            C["norm"].after()

        zeros8 = zero[:, :].rearrange("p (a o) -> p a o", o=1).broadcast_to([P, DC, P])
        gp.memset(zero[:, :], 0.0)
        gp.memset(ones[:, :], 1.0 / D).then_inc(sem("ones_set"), 1)
        for k, (name, start) in enumerate(START.items()):
            gp.memset(gain[:, k:k + 1], 0.0).then_inc(sem(name), start)
        gp.memset(as3(hp[:, :], DC)[:, :, 0:16], 0.0)
        gp.memset(as3(win[0][:, :], 2)[:, :, 0:16], 0.0)
        gp.memset(as3(win[1][:, :], 2)[:, :, 0:16], 0.0).then_inc(sem("pads_zero"), 1)
        gp.memset(tv[:, 0:1], 0.0).then_inc(acc_free["act"], 2)
        gp.memset(tv[:, 1:2], 0.0).then_inc(acc_free["dve"], 2)
        norm_adds()
        norm_adds()
        norm_adds()
        if stop == "x1":
            return

        def ada_load(s):
            src = ada[bass.ds(C["ada"].now() * P, P), :]
            gp.dma_start(ada_w[s][:, :], src).then_inc(ada_landed[s], 16)
            C["ada"].after()

        def ffn(layer):
            def product(s, load):
                u = (s + first) % 2
                gp.wait_ge(gelu_done, C["gelu"].after())
                gp.wait_ge(acc_free["dve"], C["free_dve"].after())
                gp.tensor_tensor(chunk(gl, u), chunk(gl, u), chunk(tv, u), MUL).then_inc(prod_done, 1)
                if load:
                    gp.wait_ge(ada_used, C["used"].after())
                    ada_load(s)

            ada_load(0)
            ada_load(1)
            for half in "ab":
                first = FIRST[f"ffn{layer}_in_{half}"]
                with rounds(gp, FH // 2, (C["gelu"], 2), (C["free_dve"], 2), (C["used"], 2), (C["ada"], 2)):
                    product(0, True)
                    product(1, True)
                product(0, False)
                if half == "a":
                    for s in range(2):
                        gp.wait_ge(ada_used, C["used"].after())
                        ada_load(s)
            C["used"].after(2)
            C["free_dve"].after(8)
            norm_adds()
            norm_adds()

        gp.wait_ge(tile_done, 4)
        ffn(0)
        if stop == "x2":
            return

        gp.wait_ge(acc_free["dve"], freed["dve"]["kproj"])
        kd3 = as3(kdup[:, :], 4)
        gp.memset(kd3[:, :, 0:P], 0.0)
        gp.memset(v_tok[:, 0:256], 0.0)

        def rope_add(dst, m):
            gp.wait_ge(sem("rope_parts"), C["rope"].after())
            gp.tensor_tensor(dst, chunk(tv, m), chunk(gl, m), ADD).then_inc(sem("rope_done"), 1)

        for m in range(2):
            rope_add(chunk(sq, m), m)
        qc = Count()
        with rounds(gp, 2, (C["rope"], 4), (qc, 4)):
            for m in range(4):
                rope_add(chunk(q, qc.now()), m % 2)
                qc.after()
        blk = Count()
        gp.wait_ge(sem("k_copied"), 2)
        gp.wait_ge(sem("v_copied"), 1)
        gp.wait_ge(sem("masks_landed"), 16)
        gp.wait_ge(sem("rope_done"), 10)
        gp.tensor_copy(mb[:, P:], masks[:, NB * P:])
        with rounds(gp, NB, (blk, 4)) as n:
            gp.wait_ge(sem("o_done"), blk.now(-1))
            blk.after(4)
            q_b = as3(q[:, :], DC)[:, :, bass.ds(n * P, P)]
            gp.tensor_tensor(as3(qb[:, :], DC), q_b, zeros8, ADD)
            gp.tensor_copy(as3(kb[:, :], 4), kd3[:, :, bass.ds(n * P, 256)])
            gp.tensor_copy(vb[:, :], v_tok[:, bass.ds(n * 256, 512)])
            gp.tensor_copy(mb[:, 0:P], masks[:, bass.ds(n * P, P)]).then_inc(sem("blk_ready"), 1)
        norm_adds()
        norm_adds()
        if stop == "x3":
            return
        ffn(1)
        if stop == "x4":
            return

        gp.wait_ge(ada_used, ADA_TILES)
        gp.wait_ge(acc_free["dve"], freed["dve"]["s5_in"])
        gp.dma_start(b_raw[:, :], s5_b).then_inc(sem("b_landed"), 16)
        gp.wait_ge(h_ready, 40)
        gp.dma_start(c_mat[:, 0:2048], s5_c).then_inc(sem("c_landed"), 16)
        gp.wait_ge(sem("c_landed"), 16)
        gp.tensor_scalar(c_mat[:, 1024:2048], c_mat[:, 1024:2048], -1.0, None, MUL)
        gp.tensor_scalar(c_mat[:, 2048:], c_mat[:, 0:1024], -1.0, None, MUL).then_inc(sem("c_ready"), 1)
        gp.wait_ge(sem("s5_angles"), 1)
        gp.memset(small[:, 18 * 32:20 * 32], 0.0).then_inc(sem("carry"), 2)
        gp.wait_ge(sem("turns_used"), 1)
        S = {"in": Count(), "used": Count(2), "scan": Count(1), "dve": Count(), "y": Count(2), "gp": Count()}

        def add_inputs(j):
            w = w5[j % 2]
            gp.wait_ge(sem("rot_in"), S["in"].after())
            gp.tensor_tensor(w[0][:, :], w[0][:, :], w[1][:, :], ADD).then_inc(sem("v_ready"), 1)
            gp.wait_ge(sem("bu_used"), S["used"].after())
            gp.tensor_tensor(w[2][:, :], w[2][:, :], w[3][:, :], SUB).then_inc(sem("v_ready"), 1)

        def rotate_out(j):
            pp, (gr, gi) = p5[j % 2], g5[j % 2]
            gp.wait_ge(sem("scanned"), S["scan"].after())
            gp.wait_ge(sem("y5_done"), S["y"].now(1))
            S["y"].after()
            gp.tensor_tensor(pp[2][:, :], sin5[:, j * T:(j + 1) * T], gr[:, :], MUL)
            gp.tensor_tensor(pp[3][:, :], cos5[:, j * T:(j + 1) * T], gi[:, :], MUL).then_inc(sem("p_gp"), 1)
            gp.wait_ge(sem("p_dve"), S["dve"].after())
            gp.wait_ge(sem("p_gp"), S["gp"].after())
            for half, op in enumerate((SUB, ADD)):
                ends = [as3(pp[2 * half + k][:, :], 4)[:, :, P - 1:P] for k in range(2)]
                dst = small[:, (18 + half) * 32 + 4 * j:(18 + half) * 32 + 4 * j + 4].rearrange("p (a o) -> p a o", o=1)
                ins = gp.tensor_tensor(dst, *ends, op)
            ins.then_inc(sem("carry"), 1)

        def block5(more):
            for j in range(DC):
                if j < DC - 1 or more:
                    add_inputs((j + 1) % DC)
                rotate_out(j)

        add_inputs(0)
        with rounds(gp, NB - 1, *[(c, DC) for c in S.values()]):
            block5(True)
        block5(False)
        norm_adds()
        if stop == "x5":
            return
        norm_adds()
        if stop == "x6":
            return

        gp.wait_ge(h_ready, 64)
        gp.dma_start(upper[:, :], consts[:, UPPER:UPPER + P]).then_inc(sem("upper_landed"), 16)
        gp.wait_ge(sem("upper_landed"), 16)
        gp.wait_ge(sem("cdec_done"), 1)

        def gate(grp, q_):
            n = 4 * grp + q_
            gp.wait_ge(sem("y_summed"), n + 1)
            gp.tensor_tensor(chunk(yg, q_), chunk(yg, q_), chunk(zt, n), MUL).then_inc(sem("gated"), 1)

        for grp in range(4):
            for c in range(NB - 1):
                gp.wait_ge(sem("xdt_done"), 4 * grp + c + 1)
                d8 = decay[:, c * 32 + 8 * grp:c * 32 + 8 * grp + 8].rearrange("p (a o) -> p a o", o=1).broadcast_to([P, 8, 64])
                gp.tensor_tensor(as3(xdtd[:, c * T:(c + 1) * T], 8), as3(xdt[:, c * T:(c + 1) * T], 8), d8, MUL).then_inc(sem("xdtd_done"), 1)
            for hh in range(8):
                n, q_ = 8 * grp + hh, hh // 2
                gp.wait_ge(sem("diff_done"), n + 1)
                gp.tensor_scalar(chunk(tg, hh % 2), chunk(tg, hh % 2), 0.0, None, ALU.min).then_inc(sem("min_done"), 1)
                if hh % 2 == 0 and hh:
                    gate(grp, q_ - 1)
            gate(grp, 3)
        norm_adds()
        if stop == "x7":
            return
        norm_adds()

    block.__exit__(None, None, None)


def _col_blocks(w, rows, cols):
    w = w.reshape(w.shape[0] // P, P, w.shape[1] // P, P)
    return w[rows][:, :, cols].transpose(1, 2, 0, 3).reshape(P, -1)


def pack_weights(i):
    w = np.zeros((NT, P, TILE), np.float32)
    at = [0]

    def put(a):
        w[at[0], :, :a.shape[1]] = a
        at[0] += 1

    k8 = list(range(DC))
    pw = i["pool_w"][0].reshape(4, 2, P, 2, P)
    put(pw.transpose(2, 0, 1, 3, 4).reshape(P, -1))

    def ffn(l):
        for half in range(2):
            for j in range(half * FH, (half + 1) * FH):
                put(_col_blocks(i["ffn_w_in"][l], k8, [j, FC + j]))
            for m in range(DC):
                put(_col_blocks(i["ffn_w_out"][l], list(range(half * FH, (half + 1) * FH)), [m]))

    def pairs(mat, cols=None):
        cols = cols or list(range(mat.shape[1] // P))
        for j in range(0, len(cols), 2):
            put(_col_blocks(mat, k8, cols[j:j + 2]))

    def mlp(l):
        for half in range(2):
            pairs(i["mlp_w1_2"][l], list(range(half * MH, (half + 1) * MH)))
            for m in range(DC):
                put(_col_blocks(i["mlp_w2_2"][l], list(range(half * MH, (half + 1) * MH)), [m]))

    ffn(0)
    put(_col_blocks(i["w_kv"], k8, [0, 1]))
    put(i["w_kv"][:, 256:].reshape(DC, P, 256).transpose(1, 0, 2).reshape(P, -1))
    pairs(i["w_q"][0])
    pairs(i["w_o"][0])
    ffn(1)
    pairs(i["s5_w_in_2"][0])
    pairs(i["s5_w_glu_2"][0], [c for j in range(DC) for c in (j, DC + j)])
    mlp(0)
    m2 = i["m2_w_in_2"][0]
    dt_cols = np.zeros((D, P), np.float32)
    dt_cols[:, :NH2] = m2[:, DI + XC * P:]
    put(_col_blocks(dt_cols, k8, [0]))
    pairs(m2[:, :DI + XC * P])
    for m in range(DC):
        put(_col_blocks(i["m2_w_out_2"][0], list(range(ZC)), [m]))
    mlp(1)
    assert at[0] == NT, (at[0], NT)
    return w.reshape(NT * P, TILE)


def pack_vecs(i):
    o = np.zeros((P, NV), np.float32)

    def put(name, a):
        c0, n = VECS[name]
        o[:a.shape[0], c0:c0 + n] = a.reshape(a.shape[0], n)

    feat = lambda a: np.asarray(a, np.float32).reshape(-1, P).T
    for name, key in [("mix_pre", "mix_pre_g"), ("mix_post", "mix_post_g"), ("pool_scale", "pool_scale"),
                      ("kv_norm", "kv_norm_g"), ("ffn_pre", "ffn_pre_g"), ("ffn_post", "ffn_post_g"),
                      ("conv_w", "ffn_conv_w"), ("conv_b", "ffn_conv_b"), ("c", "c_2"), ("ada_b", "ada_b_2"),
                      ("norm_mix", "norm_mix_g_2"), ("norm_mlp", "norm_mlp_g_2"), ("final", "final_norm_g_2"),
                      ("s5_d", "s5_d_2"), ("b_glu", "s5_b_glu_2"), ("m2_conv_w", "m2_conv_w_2"),
                      ("m2_conv_b", "m2_conv_b_2"), ("m2_norm", "m2_norm_g_2"),
                      ("lam_re", "s5_lambda_re_2"), ("lam_im", "s5_lambda_im_2")]:
        put(name, feat(i[key]))
    put("log_dt", feat(np.repeat(i["s5_log_dt_2"][0], 64)))
    put("m2_d", feat(np.repeat(i["m2_d_2"][0], 64)))
    put("dt_bias", i["m2_dt_bias_2"][0][:, None])
    put("a_log", i["m2_a_log_2"][0][:, None])
    put("sinks", np.broadcast_to(i["sinks"][0].reshape(4, 2, 2).transpose(0, 2, 1).reshape(1, 16), (P, 16)))
    freq = 1.0 / (np.float32(10000.0) ** (np.arange(0, 64, 2, dtype=np.float32) / np.float32(64)))
    put("inv_freq", np.tile(freq.astype(np.float32), 4)[:, None])
    put("rope_sign", np.where(np.arange(P) % 64 < 32, -1.0, 1.0)[:, None])
    put("tok", np.broadcast_to(np.arange(1, P + 1, dtype=np.float32)[None], (P, P)))
    return o


def shape_constants():
    p = np.arange(P)
    swap = np.zeros((P, P), np.float32)
    swap[(p // 64) * 64 + (p + 32) % 64, p] = 1.0
    edge = np.ones((4, 16), np.float32)
    for g, w in enumerate((2, 4, 8, 16)):
        edge[g] = w / np.minimum(np.arange(1, 17), w)
    qi, kj = p[:, None], np.arange(256)[None]
    rel = P + qi - kj
    valid = (rel >= 0) & (rel < P)
    masks = [np.where(valid & (n * P + kj - P >= 0), 0.0, NEG)[:, :P] for n in range(NB)]
    masks.append(np.where(valid, 0.0, NEG)[:, P:])
    upper = (p[None] >= p[:, None]).astype(np.float32)
    return np.concatenate([np.eye(P), swap, np.broadcast_to(edge.reshape(1, -1), (P, 64))] + masks + [upper],
                          axis=1).astype(np.float32)


def arrays(inputs):
    i = {k: np.asarray(a) for k, a in inputs.items()}
    f = lambda a: np.ascontiguousarray(a, dtype=a.dtype)
    ada = i["ada_w_2"].reshape(2, DC, P, ADA // 2, 2, P).transpose(0, 3, 2, 1, 4, 5).reshape(ADA_TILES * P, TILE)
    b = np.zeros((2, 2, 64, 32, 32), np.float32)
    c = np.zeros((2, 2, 64, 32, 32), np.float32)
    for n, part in enumerate(("re", "im")):
        bb = i[f"s5_b_{part}_2"][0].reshape(32, 2, 64, 16)
        cc = i[f"s5_c_{part}_2"][0].transpose(0, 2, 1).reshape(32, 2, 64, 16)
        for g in range(2):
            b[n, g, :, :, 16 * g:16 * g + 16] = bb[:, g].transpose(1, 0, 2)
            c[n, g, :, :, 16 * g:16 * g + 16] = cc[:, g].transpose(1, 0, 2)
    lay = lambda a: np.ascontiguousarray(a.reshape(2, P, 1024).transpose(1, 0, 2).reshape(P, 2048))
    return {
        "weights": pack_weights(i), "ada": f(ada), "vecs": pack_vecs(i), "consts": shape_constants(),
        "x_in": f(i["x"][0].T.reshape(DC, P, T).transpose(1, 0, 2).reshape(P, DC * T)),
        "pos_in": f(np.broadcast_to(i["positions"][0][None], (P, T)).astype(np.int32)),
        "s5_b": lay(b), "s5_c": lay(c),
    }


def kernel(**inputs):
    import concourse.bacc as bacc
    from concourse.bass_utils import run_bass_kernel_spmd

    nc = bacc.Bacc("TRN2", target_bir_lowering=False, num_devices=1)
    ins = arrays(inputs)
    aps = {k: nc.dram_tensor(f"{k}_dram", a.shape, mybir.dt.from_np(a.dtype), kind="ExternalInput").ap()
           for k, a in ins.items()}
    out = nc.dram_tensor("out_dram", (P, DC * T), mybir.dt.float32, kind="ExternalOutput").ap()
    build(nc, **aps, out=out)
    r = run_bass_kernel_spmd(nc, [{f"{k}_dram": a for k, a in ins.items()}], core_ids=[0])
    y = r.results[0]["out_dram"]
    return np.ascontiguousarray(y.reshape(P, DC, T).transpose(2, 1, 0).reshape(1, T, D))
```

```python
from contextlib import ExitStack, contextmanager

import numpy as np

import concourse.bass as bass
from concourse import mybir

P = 128
T = 512
D = 1024
DC = D // P
FF = 2816
FC = FF // P
FH = FC // 2
MC = 4 * D // P
MH = MC // 2
DI = 2 * D
ZC = DI // P
XC = (DI + 2 * 4 * P) // P
NH2 = DI // 64
NB = T // P
TILE = 16 * P
HALF = FH * P
EPS_A, EPS_B = 1e-6, 1e-5
NEG = -1e30
ADA = 48
ADA_TILES = 2 * ADA // 2

PHASES = [
    ("pool", 1, TILE, None),
    ("ffn0_in_a", FH, TILE, "dve"), ("ffn0_out_a", 8, HALF, "act"),
    ("ffn0_in_b", FH, TILE, "dve"), ("ffn0_out_b", 8, HALF, "dve"),
    ("kproj", 1, TILE, None), ("vproj", 1, TILE, None),
    ("qproj", 4, TILE, None), ("oproj", 4, TILE, "act"),
    ("ffn1_in_a", FH, TILE, "dve"), ("ffn1_out_a", 8, HALF, "act"),
    ("ffn1_in_b", FH, TILE, "dve"), ("ffn1_out_b", 8, HALF, "dve"),
    ("s5_in", 4, TILE, "act"), ("s5_glu", 8, TILE, "dve"),
    ("mlp0_in_a", 8, TILE, "act"), ("mlp0_out_a", 8, TILE, "dve"),
    ("mlp0_in_b", 8, TILE, "act"), ("mlp0_out_b", 8, TILE, "dve"),
    ("m2_dt", 1, TILE // 2, None), ("m2_z", 8, TILE, "act"), ("m2_xbc", 12, TILE, "dve"),
    ("m2_out", 8, TILE, "dve"),
    ("mlp1_in_a", 8, TILE, "act"), ("mlp1_out_a", 8, TILE, "dve"),
    ("mlp1_in_b", 8, TILE, "act"), ("mlp1_out_b", 8, TILE, "dve"),
]
FIRST = {}
_n = 0
for _name, _tiles, _w, _e in PHASES:
    FIRST[_name] = _n
    _n += _tiles
NT = _n
TILES = {name: tiles for name, tiles, _, _ in PHASES}

VECS = {}
_at = 0
for _name, _cols in [
    ("mix_pre", 16), ("mix_post", 16), ("pool_scale", 8), ("kv_norm", 8), ("ffn_pre", 16),
    ("ffn_post", 16), ("conv_w", 2 * 3 * 2 * FC), ("conv_b", 2 * 2 * FC), ("c", 8),
    ("ada_b", 2 * ADA), ("norm_mix", 16), ("norm_mlp", 16), ("final", 8), ("lam_re", 32),
    ("lam_im", 32), ("log_dt", 32), ("s5_d", 8), ("b_glu", 16), ("m2_conv_w", 4 * XC),
    ("m2_conv_b", XC), ("m2_d", ZC), ("m2_norm", ZC), ("dt_bias", 1), ("a_log", 1), ("sinks", 16),
    ("inv_freq", 1), ("rope_sign", 1), ("tok", P),
]:
    VECS[_name] = (_at, _cols)
    _at += _cols
NV = _at


STOP_X = {"x1": 8, "x2": 16, "x3": 24, "x4": 32, "x5": 40, "x6": 56, "x7": 64}
TWO_PI_A, TWO_PI_B = 6.28125, 4058 / 2 ** 21
TWO_PI_C = 2 * np.pi - TWO_PI_A - TWO_PI_B
MAGIC = 1.5 * 2 ** 23


UPPER = 2 * P + 64 + 4 * P

START = {"bu_copied": 1, "bu_used": 2, "scanned": 1, "y5_read": 2, "y5_done": 2}


class Count:

    def __init__(self, start=0):
        self.n, self.r, self.per, self.n0 = start, None, 0, 0

    def after(self, k=1):
        self.n += k
        return self.now()

    def now(self, back=0):
        v = self.n - back
        return v if self.r is None or not self.per else self.r * self.per + v


@contextmanager
def rounds(eng, n, *counts):
    with eng.Fori(0, n) as r:
        for c, per in counts:
            c.r, c.per, c.n0 = r, per, c.n
        yield r
    for c, per in counts:
        assert c.n - c.n0 == per, (c.n, c.n0, per)
        c.r, c.per, c.n = None, 0, c.n0 + n * per


def build(nc, weights, ada, vecs, consts, x_in, pos_in, s5_b, s5_c, out, stop=None):
    f32, f32r, i32 = mybir.dt.float32, mybir.dt.float32r, mybir.dt.int32
    ALU, ACT, AX = mybir.AluOpType, mybir.ActivationFunctionType, mybir.AxisListType
    ADD, SUB, MUL, MAX = ALU.add, ALU.subtract, ALU.mult, ALU.max

    at = [16512]

    def place(name, cols, dt=f32, offset=None):
        if offset is None:
            offset, at[0] = at[0], at[0] + (cols * 4 + 31) // 32 * 32
        return nc.alloc_sbuf_tensor_at(name, [P, cols], dt, offset=offset)

    KB = 1024
    H0 = at[0]
    h_hi, h_lo = place("h_hi", DC * T, f32r), place("h_lo", DC * T, f32r)
    A0 = at[0]
    a_hi, a_lo = place("a_hi", 16 * T, f32r), place("a_lo", 16 * T, f32r)
    F0 = at[0]
    f = place("f", DC * T)
    x = place("x", DC * T)
    raw = place("raw", 2 * TILE)
    w_hi, w_lo = place("w_hi", 2 * TILE, f32r), place("w_lo", 2 * TILE, f32r)
    S0 = at[0]
    tg, tv, gl = place("tg", 2 * T), place("tv", 2 * T), place("gl", 2 * T)
    sq, sqsum, rstd = place("sq", 2 * T), place("sqsum", T), place("rstd", T)
    vec, mod = place("vec", NV), place("mod", 2 * ADA)
    gain, rcol = place("gain", DC), place("rcol", NB)
    cond = place("cond", DC)
    ident, perm, ones = place("ident", P), place("perm", P), place("ones", P)
    at[0] = (at[0] + 31) // 32 * 32
    W0 = at[0]
    assert W0 + 5 * KB + 512 <= 229344, W0
    ada_w, ada_acc = place("ada_w", TILE, offset=A0 + 56 * KB), place("ada_acc", 2 * P, offset=W0 + 2 * KB)

    PW = 16 + T
    hp = place("pool_h", DC * PW, offset=A0)
    win = [place("pool_s0", 2 * PW, offset=H0), place("pool_s1", 2 * PW, offset=H0 + 5 * KB)]
    edge = place("pool_edge", 4 * 16, offset=H0 + 12 * KB)
    dd_hi, dd_lo = place("pool_d_hi", DC * T, f32r, offset=A0 + 20 * KB), place("pool_d_lo", DC * T, f32r, offset=A0 + 40 * KB)

    cosT, sinT = place("cos", T, offset=A0 + 16 * KB), place("sin", T, offset=A0 + 18 * KB)
    kdup = place("kdup", 4 * (P + T), offset=A0 + 20 * KB)
    posi = place("posi", T, i32, offset=W0 + 3 * KB)
    v_tok = place("v_tok", (NB + 1) * 256, offset=A0 + 48 * KB)
    s_sb = place("s_sb", 2 * 1024, offset=A0)
    p_t = place("p_t", 2 * 1024, offset=A0 + 8 * KB)
    masks = place("masks", 4 * P, offset=W0)
    mx = place("mx", 6 * 8, offset=W0 + 5 * KB)
    q = f

    cos5, sin5, turn5 = (place(n, 32 * P, offset=A0 + 16 * KB * k) for k, n in enumerate(("cos5", "sin5", "turn5")))
    b_raw, b_bar = place("b_raw", 2048, offset=A0 + 48 * KB), place("b_bar", 2048, offset=A0 + 56 * KB)
    b_tmp = turn5[:, 0:1024]
    b_t = b_raw
    c_mat = place("c_mat", 3072, offset=S0)
    small = place("small", 32 * 32, offset=W0)
    w5 = [[place(f"s5_w{u}{k}", T, offset=H0 + (4 * u + k) * 2 * KB) for k in range(4)] for u in range(2)]
    p5 = [[place(f"s5_p{u}{k}", T, offset=(H0 + (8 + 4 * u + k) * 2 * KB)) for k in range(4)] for u in range(2)]
    ub = sq
    bu5 = [place(f"s5_bu{u}", 2 * T, offset=A0 + (36 + 4 * u) * KB) for u in range(2)]
    g5 = [[place(f"s5_g{u}{k}", T, offset=A0 + (32 + 12 * u + 2 * k) * KB) for k in range(2)] for u in range(2)]

    zt, xbc = place("zt", ZC * T, offset=A0), place("xbc", XC * T, offset=A0 + 32 * KB)
    xdt, xdtd = place("xdt", NB * T, offset=H0), place("xdtd", NB * T, offset=H0 + 8 * KB)
    prev = place("prev", 3 * T, offset=H0 + 16 * KB)
    b_tok, cbm = place("b_tok", T, offset=H0 + 22 * KB), place("cbm", T, offset=H0 + 24 * KB)
    ea, ytmp = place("ea", 2 * T, offset=H0 + 26 * KB), place("ytmp", T, offset=H0 + 30 * KB)
    yg = place("yg", 4 * T, offset=S0 + 4 * KB)
    acs_row, acs_hi = place("acs_row", T, offset=W0), place("acs_hi", T, f32r, offset=W0 + 2 * KB)
    acs_lo = place("acs_lo", T, f32r, offset=W0)
    ident_r = place("ident_r", 32, f32r, offset=W0 + 5 * KB + 64)
    cdec, causal = place("cdec", P, offset=W0 + 4 * KB), place("causal", P, offset=W0 + 4 * KB + 512)
    lmat = [tg[:, 0:T], tg[:, T:2 * T], sqsum[:, :]]
    one_col = place("one_col", 1, offset=W0 + 5 * KB)
    small32 = place("a_exp_col", 1, offset=W0 + 5 * KB + 32)[0:32, :]
    dt_row = place("dt_row", T, offset=S0 + 10 * KB)
    acs_t, dt_t, decay, diag = (sq[:, k * P:(k + 1) * P] for k in range(4))

    ps = nc.psum_tensor("ps", [P, 8 * T], f32).__enter__()

    def bank(b, cols=T, p0=0, p1=P, off=0):
        return ps[p0:p1, b * T + off:b * T + off + cols]

    NORM, MOD = 4, 5

    def v(name, col=0, p=P):
        a, n = VECS[name]
        if isinstance(col, int):
            assert col < n
            return vec[0:p, a + col:a + col + 1]
        return vec[0:p, bass.ds(col + a, 1)]

    def vs(name, lo, hi, p=P):
        a, _ = VECS[name]
        return vec[0:p, a + lo:a + hi]

    def chunk(t, c, n=1):
        return t[:, c * T:(c + n) * T] if isinstance(c, int) else t[:, bass.ds(c * T, n * T)]

    def as3(ap, a):
        return ap.rearrange("p (a b) -> p a b", a=a)

    sems = {}

    def sem(name):
        if name not in sems:
            sems[name] = nc.semaphore(name).__enter__()
        return sems[name]

    order = [n for n, *_ in PHASES]
    freed = {"act": {}, "dve": {}}
    na = {"act": 2, "dve": 2}
    for n, tiles, _, e in PHASES:
        for k in na:
            freed[k][n] = na[k]
        if e:
            na[e] += tiles
    EMPTY = {n: e for n, _, _, e in PHASES}
    raw_landed = [sem("raw_landed0"), sem("raw_landed1")]
    w_hi_done, w_split, tile_done = sem("w_hi_done"), sem("w_split"), sem("tile_done")
    acc_free = {"act": sem("acc_free_act"), "dve": sem("acc_free_dve")}
    sq_ready, sq_added, norm_sum, std_done = sem("sq_ready"), sem("sq_added"), sem("norm_sum"), sem("std_done")
    hf_done, h_hi_done, h_ready = sem("hf_done"), sem("h_hi_done"), sem("h_ready")
    a_hi_done, a_ready = sem("a_hi_done"), sem("a_ready")
    x_ready, dve_step = sem("x_ready"), sem("dve_step")
    pool_out, pool_d = sem("pool_out"), sem("pool_d")
    conv_pre, gate_conv, gelu_done, prod_done = sem("conv_pre"), sem("gate_conv"), sem("gelu_done"), sem("prod_done")
    rstd_ready, rstd_spread = sem("rstd_ready"), sem("rstd_spread")
    ada_landed, ada_summed, ada_used = sem("ada_landed"), sem("ada_summed"), sem("ada_used")
    ADA_STEPS = {"in_a": ((1,), True), "out_a": ((0, 1), False), "in_b": ((1,), True), "out_b": ((1,), False)}

    def tile_at(g):
        return g + 4

    done = {"x1": "ffn0_in_a", "x2": "kproj", "x3": "ffn1_in_a", "x4": "s5_in", "x5": "mlp0_in_a",
            "x6": "m2_dt", "x7": "mlp1_in_a"}.get(stop)
    phases = PHASES[:order.index(done)] if done else PHASES
    total = sum(t for _, t, _, _ in phases)
    block = nc.Block().__enter__()

    @block.sync
    def _(sp):
        sp.dma_start(x[:, :], x_in).then_inc(sem("x_landed"), 16)
        sp.dma_start(vec[:, :], vecs).then_inc(sem("vec_landed"), 16)
        sp.dma_start(ident[:, :], consts[:, 0:P]).then_inc(sem("ident_landed"), 16)
        sp.dma_start(posi[:, :], pos_in).then_inc(sem("pos_landed"), 16)
        sp.dma_start(edge[:, :], consts[:, 2 * P:2 * P + 64]).then_inc(sem("edge_landed"), 16)
        g = Count()

        def load(width):
            u = g.n % 2
            src = weights[bass.ds(g.now() * P, P), 0:width]
            sp.dma_start(raw[:, u * TILE:u * TILE + width], src).then_inc(raw_landed[u], 16)
            g.after()

        for name, tiles, width, _ in phases:
            pairs = tiles // 2 if g.n >= 2 else 0
            if pairs:
                with rounds(sp, pairs, (g, 2)):
                    for _ in range(2):
                        sp.wait_ge(w_split, g.now(1))
                        load(width)
            for _ in range(tiles - 2 * pairs):
                if g.n >= 2:
                    sp.wait_ge(w_split, g.now(1))
                load(width)
            if name == "pool":
                sp.dma_start(perm[:, :], consts[:, P:2 * P]).then_inc(sem("perm_landed"), 16)
                sp.dma_start(masks[:, :], consts[:, 2 * P + 64:UPPER]).then_inc(sem("masks_landed"), 16)
        for c in range(DC):
            if stop in ("x5", "x6", "x7"):
                sp.wait_ge(acc_free["dve"], freed["dve"][done])
            elif stop:
                sp.wait_ge(x_ready, STOP_X[stop])
            else:
                sp.wait_ge(sem("y_ready"), c + 1)
            sp.dma_start(out[:, c * T:(c + 1) * T], chunk(x, c)).then_inc(sem("y_stored"), 16)
        sp.wait_ge(sem("y_stored"), 16 * DC)


    @block.tensor
    def _(pe):
        g = Count()
        C = {k: Count() for k in ("sum", "ada", "qraw")}
        fr = {"act": Count(2), "dve": Count(2)}

        def products(dst, o, rhs_hi, rhs_lo, start, last):
            nc.tensor.matmul(dst, w_hi[:, o:o + P], rhs_hi, start=start, stop=False)
            nc.tensor.matmul(dst, w_hi[:, o:o + P], rhs_lo, start=False, stop=False)
            return nc.tensor.matmul(dst, w_lo[:, o:o + P], rhs_hi, start=False, stop=last)

        def linear_tile(name, k_chunks, outs, src_hi, src_lo, ready, base):
            u = g.n % 2
            pe.wait_ge(w_split, g.after())
            if EMPTY[name]:
                e = EMPTY[name]
                pe.wait_ge(acc_free[e], fr[e].now(1))
                fr[e].after()
            for m in range(outs):
                for k in range(k_chunks):
                    if m == 0:
                        pe.wait_ge(ready, base + k + 1)
                    last = products(bank(2 * u + m), u * TILE + (m * k_chunks + k) * P,
                                    chunk(src_hi, k), chunk(src_lo, k), k == 0, k == k_chunks - 1)
            last.then_inc(tile_done, 1)

        def ada_sum():
            col = C["ada"].now() * 2 + MOD * T
            pe.wait_ge(ada_summed, C["ada"].after())
            for m in range(2):
                last = nc.tensor.matmul(ps[:, bass.ds(col + m, 1)], ada_acc[:, m * P:(m + 1) * P], ones[:, 0:1],
                                        start=True, stop=True)
            last.then_inc(ada_used, 1)

        def phase(name, k_chunks, outs, hi, lo, ready, base, ada=None):
            steps, at_end = ADA_STEPS[ada] if ada else ((), False)
            e = EMPTY[name]
            for k in ("act", "dve"):
                pe.wait_ge(acc_free[k], freed[k][name])
                assert fr[k].n == freed[k][name]
            n, peel = divmod(TILES[name], 2)
            per = [(g, 2)] + ([(fr[e], 2)] if e else [])
            per += [(C["ada"], len(steps))]
            if name == "qproj":
                per += [(C["qraw"], 4)]
            with rounds(pe, n, *per):
                for s in range(2):
                    linear_tile(name, k_chunks, outs, hi, lo, ready, base)
                    if (s + 1) % 2 in steps:
                        ada_sum()
                    if name == "qproj":
                        rope_pair()
            if peel:
                linear_tile(name, k_chunks, outs, hi, lo, ready, base)
            if at_end:
                ada_sum()

        def norm_sum_matmul():
            n = C["sum"].n
            pe.wait_ge(sq_added, 9 * (n + 1))
            if n:
                pe.wait_ge(std_done, n)
            for b in range(NB):
                last = nc.tensor.matmul(bank(NORM, 1, off=b), sqsum[:, b * P:(b + 1) * P], ones[:, 0:1], start=True, stop=True)
            last.then_inc(norm_sum, 1)
            C["sum"].after()
            pe.wait_ge(rstd_ready, n + 1)
            for b in range(NB):
                last = nc.tensor.matmul(bank(NORM, P, off=b * P), rcol[:, b:b + 1].broadcast_to([P, P]), ident[:, :],
                                        start=True, stop=True)
            last.then_inc(rstd_spread, 1)

        def ffn(layer, hb):
            ab = 2 * FH * layer
            phase(f"ffn{layer}_in_a", DC, 2, h_hi, h_lo, h_ready, hb, "in_a")
            phase(f"ffn{layer}_out_a", FH, 1, a_hi, a_lo, a_ready, ab, "out_a")
            phase(f"ffn{layer}_in_b", DC, 2, h_hi, h_lo, h_ready, hb, "in_b")
            phase(f"ffn{layer}_out_b", FH, 1, a_hi, a_lo, a_ready, ab + FH, "out_b")
            if layer == 1:
                ada_sum()
            norm_sum_matmul()
            norm_sum_matmul()

        def rope_pair():
            for s in range(2):
                pe.wait_ge(sem("qraw"), C["qraw"].after())
                nc.tensor.matmul(bank(6 + s), perm[:, :], chunk(tg, s), start=True, stop=True).then_inc(sem("rot"), 1)

        pe.wait_ge(sem("ones_set"), 1)
        pe.wait_ge(sem("ident_landed"), 16)
        norm_sum_matmul()

        pe.wait_ge(w_split, g.after())
        for grp in range(4):
            if grp >= 2:
                pe.wait_ge(pool_out, grp - 1)
            for m in range(2):
                for k in range(2):
                    c = 2 * grp + k
                    pe.wait_ge(pool_d, c + 1)
                    last = products(bank(2 * (grp % 2) + m), (c * 2 + m) * P, chunk(dd_hi, c),
                                    chunk(dd_lo, c), k == 0, k == 1)
            last.then_inc(tile_done, 1)
        norm_sum_matmul()
        norm_sum_matmul()
        if stop == "x1":
            return
        pe.wait_ge(pool_out, 4)
        ffn(0, 0)
        if stop == "x2":
            return

        pe.wait_ge(sem("perm_landed"), 16)
        phase_base = 8
        for k_ in ("act", "dve"):
            pe.wait_ge(acc_free[k_], freed[k_]["kproj"])
        linear_tile("kproj", DC, 2, a_hi, a_lo, h_ready, phase_base)
        rope_pair()
        u = g.n % 2
        pe.wait_ge(w_split, g.after())
        for n in range(NB):
            for k in range(DC):
                t0, o = k * T + n * P, u * TILE + k * 256
                nc.tensor.matmul(bank(n, 256), a_hi[:, t0:t0 + P], w_hi[:, o:o + 256], start=(k == 0), stop=False)
                nc.tensor.matmul(bank(n, 256), a_hi[:, t0:t0 + P], w_lo[:, o:o + 256], start=False, stop=False)
                last = nc.tensor.matmul(bank(n, 256), a_lo[:, t0:t0 + P], w_hi[:, o:o + 256],
                                        start=False, stop=(k == DC - 1))
        last.then_inc(tile_done, 1)
        pe.wait_ge(sem("v_copied"), 1)
        phase("qproj", DC, 2, h_hi, h_lo, h_ready, 16)

        pe.wait_ge(sem("ident_landed"), 16)
        pe.wait_ge(sem("rope_done"), 10)
        pe.wait_ge(sem("k_copied"), 2)
        UNITS = 4 * NB

        def scores(i):
            n, gkv = divmod(i, 4)
            if i:
                pe.wait_ge(sem("s_read"), i)
            for hh in range(4):
                h = 4 * gkv + hh
                p0, c0, k0 = 64 * (h % 2), (h // 2) * T + n * P, gkv * (P + T) + n * P
                last = nc.tensor.matmul(bank(hh % 2, 256, off=256 * (hh // 2)), q[p0:p0 + 64, c0:c0 + P],
                                        kdup[p0:p0 + 64, k0:k0 + 256], start=True, stop=True)
            last.then_inc(sem("s_done"), 1)

        scores(0)
        scores(1)
        for i in range(UNITS):
            n, gkv = divmod(i, 4)
            pe.wait_ge(sem("p_ready"), i + 1)
            if i:
                pe.wait_ge(sem("pt_a"), i)
                pe.wait_ge(sem("pt_b"), i)
            for kb_ in range(2):
                for hh in range(4):
                    o = (i % 2) * 1024 + hh * 256 + kb_ * P
                    last = nc.tensor.transpose(bank(2 + kb_, P, off=hh * P), s_sb[:, o:o + P], ident[:, :])
            last.then_inc(sem("pt_psum"), 1)
            if i + 2 < UNITS:
                scores(i + 2)
            pe.wait_ge(sem("pt_a"), i + 1)
            pe.wait_ge(sem("pt_b"), i + 1)
            if i:
                pe.wait_ge(sem("o_split"), i)
            for par in range(2):
                for kb_ in range(2):
                    o, v0 = (i % 2) * 1024 + kb_ * 512 + par * 256, (n + kb_) * 256 + gkv * 64
                    last = nc.tensor.matmul(as3(bank(6, 256, 64 * par, 64 * par + 64), 2), v_tok[:, v0:v0 + 64],
                                            as3(p_t[:, o:o + 256], 2), start=(kb_ == 0), stop=(kb_ == 1))
            last.then_inc(sem("o_done"), 1)
        pe.wait_ge(sem("o_split"), 16)
        phase("oproj", DC, 2, h_hi, h_lo, sem("o_split"), 0)
        norm_sum_matmul()
        norm_sum_matmul()
        if stop == "x3":
            return
        ffn(1, 24)
        if stop == "x4":
            return

        phase("s5_in", DC, 2, h_hi, h_lo, h_ready, 32)
        for half in range(2):
            pe.wait_ge(sem("b_bar_done"), half + 1)
            for j in range(DC):
                last = nc.tensor.transpose(bank(6 + j // 4, P, off=(j % 4) * P),
                                           b_bar[:, half * 1024 + j * P:half * 1024 + (j + 1) * P], ident[:, :])
            last.then_inc(sem("b_t_psum"), 1)
            pe.wait_ge(sem("b_t_done"), half + 1)
        for k_ in ("act", "dve"):
            pe.wait_ge(acc_free[k_], freed[k_]["s5_glu"])
        pe.wait_ge(sem("c_ready"), 1)
        S = {"bu": Count(1), "ub": Count(), "h": Count(), "y": Count(2)}

        def inputs5(j):
            pe.wait_ge(sem("bu_copied"), S["bu"].now())
            pe.wait_ge(sem("ub_ready"), S["ub"].after())
            S["bu"].after()
            for i in range(4):
                rhs = ub[32 * i:32 * i + 32, j * P:(j + 1) * P]
                for half in range(2):
                    last = nc.tensor.matmul(bank(i, P, off=half * P),
                                            b_t[32 * i:32 * i + 32, half * 1024 + j * P:half * 1024 + (j + 1) * P],
                                            rhs, start=True, stop=True)
            last.then_inc(sem("bu_done"), 1)

        def outputs5(j):
            pe.wait_ge(sem("p_dve"), S["h"].after())
            pe.wait_ge(sem("p_gp"), S["h"].now())
            pe.wait_ge(sem("y5_read"), S["y"].now(1))
            S["y"].after()
            for i in range(4):
                for k, part in enumerate((0, 2, 1, 1)):
                    c0 = part * 1024 + (4 * j + i) * 32
                    last = nc.tensor.matmul(bank(6 + j % 2, P, 32 * i, 32 * i + 32), c_mat[:, c0:c0 + 32],
                                            p5[j % 2][k][:, i * P:(i + 1) * P], start=(k == 0), stop=(k == 3))
            last.then_inc(sem("y5_done"), 1)

        def block5(more):
            for j in range(DC):
                if j < DC - 2 or more:
                    inputs5((j + 2) % DC)
                outputs5(j)

        inputs5(0)
        inputs5(1)
        with rounds(pe, NB - 1, *[(c, DC) for c in S.values()]):
            block5(True)
        block5(False)
        phase("s5_glu", DC, 2, h_hi, h_lo, h_ready, 40)
        norm_sum_matmul()
        if stop == "x5":
            return

        def mlp(layer):
            ab = 4 * FH + 2 * MH * layer
            hb = 48 + 16 * layer
            phase(f"mlp{layer}_in_a", DC, 2, h_hi, h_lo, h_ready, hb)
            phase(f"mlp{layer}_out_a", MH, 1, a_hi, a_lo, a_ready, ab)
            phase(f"mlp{layer}_in_b", DC, 2, h_hi, h_lo, h_ready, hb)
            phase(f"mlp{layer}_out_b", MH, 1, a_hi, a_lo, a_ready, ab + MH)
            norm_sum_matmul()

        mlp(0)
        if stop == "x6":
            return

        for k_ in ("act", "dve"):
            pe.wait_ge(acc_free[k_], freed[k_]["m2_dt"])
        linear_tile("m2_dt", DC, 1, h_hi, h_lo, h_ready, 56)
        pe.wait_ge(sem("dt_copied"), 1)
        phase("m2_z", DC, 2, h_hi, h_lo, h_ready, 56)
        pe.wait_ge(sem("acs_done"), 1)
        for k_, row in enumerate((acs_row, dt_row)):
            for c in range(NB):
                last = nc.tensor.transpose(bank(6, 32, off=k_ * P + c * 32), row[0:32, c * P:(c + 1) * P], ident[0:32, 0:32])
        last.then_inc(sem("rows_t"), 1)
        nc.tensor.matmul(bank(7, P), ones[0:32, :], diag[0:32, :], start=True, stop=True).then_inc(sem("alast_done"), 1)
        phase("m2_xbc", DC, 2, h_hi, h_lo, h_ready, 56)
        pe.wait_ge(sem("acs_split"), 1)

        for k_ in ("act", "dve"):
            pe.wait_ge(acc_free[k_], freed[k_]["m2_out"])
        pe.wait_ge(sem("xbc_done"), ZC // 2 + XC)
        pe.wait_ge(sem("cdec_done"), 1)
        def transposes(grp):
            Bf, Cf = 16 + grp, 20 + grp
            blk = lambda ch, c: xbc[:, ch * T + c * P:ch * T + (c + 1) * P]
            if grp:
                pe.wait_ge(sem("ea_done"), 8 * grp)
                pe.wait_ge(sem("y_summed"), 4 * grp)
            for c in range(NB):
                for q_ in range(4):
                    last = nc.tensor.transpose(bank(c, P, off=q_ * P), blk(4 * grp + q_, c), ident[:, :])
                last.then_inc(sem("xt_done"), 1)
            for c in range(NB - 1):
                last = nc.tensor.transpose(bank(6, P, off=c * P), blk(Bf, c), ident[:, :])
            last.then_inc(sem("bt_done"), 1)
            for c in range(NB):
                last = nc.tensor.matmul(bank(5, P, off=c * P), blk(Bf, c), blk(Cf, c), start=True, stop=True)
            last.then_inc(sem("cb_done"), 1)
        def heads(grp):
            Bf, Cf = 16 + grp, 20 + grp
            blk = lambda ch, c: xbc[:, ch * T + c * P:ch * T + (c + 1) * P]
            pe.wait_ge(sem("bt_copied"), grp + 1)
            for c in range(NB - 1):
                pe.wait_ge(sem("xdtd_done"), 3 * grp + c + 1)
                if c == 1:
                    pe.wait_ge(sem("cb_copied"), grp + 1)
                nc.tensor.matmul(bank(4 + c), b_tok[:, c * P:(c + 1) * P], xdtd[:, c * T:(c + 1) * T],
                                 start=True, stop=True).then_inc(sem("st_done"), 1)
            pe.wait_ge(sem("xdt_done"), NB * (grp + 1))
            pe.wait_ge(sem("prev_done"), 3 * (grp + 1))
            pe.wait_ge(sem("cb_copied"), grp + 1)

            def spread(hh):
                n = 8 * grp + hh
                if hh >= 2:
                    pe.wait_ge(sem("diff_done"), n - 1)
                    pe.wait_ge(sem("ea_done"), n - 1)
                pick = ident_r[0:32, n:n + 1].broadcast_to([32, P])
                nc.tensor.matmul(bank(hh % 2), pick, acs_hi[0:32, :], start=True, stop=False)
                nc.tensor.matmul(bank(hh % 2), pick, acs_lo[0:32, :], start=False, stop=True).then_inc(sem("bc_done"), 1)

            spread(0)
            spread(1)
            for hh in range(8):
                n, pair, q_ = 8 * grp + hh, 4 * grp + hh // 2, hh // 2
                if hh % 2 == 0:
                    if q_ >= 2:
                        pe.wait_ge(sem("y_summed"), pair - 1)
                    for c in range(1, NB):
                        last = nc.tensor.matmul(bank(4 + q_ % 2, P, off=c * P), prev[:, (c - 1) * T + q_ * P:(c - 1) * T + (q_ + 1) * P],
                                                blk(Cf, c), start=True, stop=True)
                    last.then_inc(sem("off_done"), 1)
                if hh < 6:
                    spread(hh + 2)
                pe.wait_ge(sem("m_ready"), n + 1)
                p0 = 64 * (hh % 2)
                for c in range(NB):
                    last = nc.tensor.matmul(bank(2 + q_ % 2, P, p0, p0 + 64, off=c * P),
                                            xdt[:, c * T + hh * 64:c * T + (hh + 1) * 64],
                                            lmat[n % 3][:, c * P:(c + 1) * P], start=True, stop=True)
                last.then_inc(sem("yd_done"), 1)
        def group_sum(grp):
            pe.wait_ge(sem("y_summed"), 4 * (grp + 1))
            if grp:
                pe.wait_ge(sem("gstd_done"), grp)
            for q_ in range(4):
                pe.wait_ge(sem("gsq_done"), 4 * grp + q_ + 1)
                last = nc.tensor.matmul(bank(7), ones[:, :], chunk(ea, q_ % 2), start=(q_ == 0), stop=(q_ == 3))
                last.then_inc(sem("gsum_done"), 1)
        transposes(0)
        heads(0)
        for grp in range(1, 4):
            transposes(grp)
            group_sum(grp - 1)
            heads(grp)
        group_sum(3)
        phase("m2_out", ZC, 1, a_hi, a_lo, sem("y_split"), 0)
        norm_sum_matmul()
        if stop == "x7":
            return
        mlp(1)

    @block.scalar
    def _(act):
        g, split = Count(), Count()
        C = {k: Count() for k in ("norm", "sq", "x", "hf", "conv", "prod", "qraw", "land0", "land1")}
        C["free_dve"] = Count(2)

        def split_hi():
            if split.n >= total:
                return
            u = split.n % 2
            act.wait_ge(raw_landed[u], C[f"land{u}"].after(16))
            if split.n >= 2:
                act.wait_ge(tile_done, split.now() + 2)
            nc.scalar.activation(w_hi[:, u * TILE:(u + 1) * TILE], raw[:, u * TILE:(u + 1) * TILE],
                                 ACT.Copy).then_inc(w_hi_done, 1)
            split.after()

        def tiles(name, body, *counts, splits=False):
            def step():
                if not splits:
                    split_hi()
                act.wait_ge(tile_done, tile_at(g.now()))
                body(g.n % 2)
                g.after()

            left = TILES[name]
            n = (left - (2 if split.n + left > total else 0)) // 2
            with rounds(act, n, (g, 2), (split, 2), (C["land0"], 16), (C["land1"], 16),
                        *[(c, 2 * per) for c, per in counts]):
                step()
                step()
            for _ in range(left - 2 * n):
                step()

        def square(src, slot, **scaled):
            act.wait_ge(sq_added, C["sq"].now())
            nc.scalar.activation(chunk(sq, slot), src, ACT.Square, **scaled).then_inc(sq_ready, 1)
            C["sq"].after()

        def norm_start():
            C["sq"].n = 9 * C["norm"].n

        def norm_std(eps, scale=1.0):
            act.wait_ge(norm_sum, C["norm"].after())
            nc.scalar.activation(rcol[:, :], bank(NORM, NB), ACT.Sqrt, bias=eps, scale=scale).then_inc(std_done, 1)

        def x_squares():
            norm_start()
            for c in range(DC):
                act.wait_ge(x_ready, C["x"].after())
                square(chunk(x, c), c % 2)

        def split_norm(dst, shift=None):
            for c in range(DC):
                act.wait_ge(hf_done, C["hf"].after())
                b = 0.0 if shift is None else shift(c)
                nc.scalar.activation(chunk(dst, c), chunk(tg, c % 2), ACT.Identity, bias=b).then_inc(h_hi_done, 1)

        act.wait_ge(sem("x_landed"), 16)
        norm_start()
        for c in range(DC):
            square(chunk(x, c), c % 2)
        act.wait_ge(sem("vec_landed"), 16)
        nc.scalar.activation(cond[:, :], vs("c", 0, 8), ACT.Silu).then_inc(sem("cond_ready"), 1)
        norm_std(EPS_A)
        split_hi()
        split_hi()
        for c in range(DC):
            act.wait_ge(sem("pool_df"), c + 1)
            nc.scalar.activation(chunk(dd_hi, c), chunk(f, c), ACT.Copy).then_inc(sem("pool_dhi"), 1)
        norm_start()
        for grp in range(4):
            act.wait_ge(tile_done, grp + 1)
            for m in range(2):
                square(bank(2 * (grp % 2) + m), m, scale=v("pool_scale", 2 * grp + m))
            for m in range(2):
                ins = nc.scalar.activation(chunk(f, 2 * grp + m), bank(2 * (grp % 2) + m), ACT.Identity,
                                           scale=v("pool_scale", 2 * grp + m))
            ins.then_inc(pool_out, 1)
        g.after()
        norm_std(EPS_A)
        x_squares()
        norm_std(EPS_A)
        split_norm(h_hi)
        split_hi()
        if stop == "x1":
            return

        def ffn(layer):
            wcol, bcol = 3 * 2 * FC * layer, 2 * FC * layer
            hidden = Count()

            def conv_glu(u):
                j = hidden.now()
                for m, t in ((0, tg), (1, tv)):
                    nc.scalar.activation(chunk(t, u), bank(2 * u + m), ACT.Identity,
                                         scale=v("conv_w", j + (wcol + 2 * 2 * FC + m * FC)),
                                         bias=v("conv_b", j + (bcol + m * FC))).then_inc(conv_pre, 1)
                split_hi()
                act.wait_ge(gate_conv, C["conv"].after())
                nc.scalar.activation(chunk(gl, u), chunk(tg, u), ACT.Gelu_apprx_tanh).then_inc(gelu_done, 1)
                act.wait_ge(prod_done, C["prod"].after())
                nc.scalar.activation(chunk(a_hi, slot.now()), chunk(gl, u), ACT.Copy).then_inc(a_hi_done, 1)
                hidden.after()
                slot.after()

            out_chunk = Count()

            def copy_out(u):
                nc.scalar.activation(chunk(f, out_chunk.now()), bank(2 * u), ACT.Copy).then_inc(acc_free["act"], 1)
                out_chunk.after()

            def squares(u):
                act.wait_ge(acc_free["dve"], C["free_dve"].after())
                square(chunk(f, out_chunk.now()), (u + FIRST[f"ffn{layer}_out_b"]) % 2)
                out_chunk.after()

            for half in "ab":
                slot = Count()
                tiles(f"ffn{layer}_in_{half}", conv_glu, (hidden, 1), (slot, 1), (C["conv"], 1), (C["prod"], 1),
                      splits=True)
                C["free_dve"].n += FH
                out_chunk = Count()
                if half == "a":
                    tiles(f"ffn{layer}_out_a", copy_out, (out_chunk, 1))
                else:
                    norm_start()
                    tiles(f"ffn{layer}_out_b", squares, (out_chunk, 1), (C["free_dve"], 1), (C["sq"], 1))
            norm_std(EPS_A)
            x_squares()
            norm_std(EPS_A if layer == 0 else EPS_B)

        ffn(0)
        if stop == "x2":
            return

        act.wait_ge(sem("angles"), 1)
        nc.scalar.activation(cosT[:, :], sinT[:, :], ACT.Sin, scale=0.5).then_inc(sem("half_sin"), 1)
        nc.scalar.activation(chunk(tv, 1), sinT[:, :], ACT.Sin).then_inc(sem("full_sin"), 1)
        split_norm(a_hi)
        split_norm(h_hi)
        rope_done, qraw = sem("rope_done"), sem("qraw")

        def copy_raw(u):
            for m in range(2):
                act.wait_ge(rope_done, C["qraw"].now())
                nc.scalar.activation(chunk(tg, m), bank(2 * u + m), ACT.Copy).then_inc(qraw, 1)
                C["qraw"].after()

        split_hi()
        act.wait_ge(tile_done, tile_at(g.n))
        act.wait_ge(h_ready, 24)
        for m in range(2):
            nc.scalar.activation(chunk(tg, m), bank(2 * (g.n % 2) + m), ACT.Copy).then_inc(qraw, 1)
        for m in range(2):
            act.wait_ge(rope_done, m + 1)
            for half in range(2):
                dst0 = (2 * m + half) * (P + T) + P
                for to in range(2):
                    ins = nc.scalar.activation(kdup[64 * to:64 * to + 64, dst0:dst0 + T],
                                               sq[64 * half:64 * half + 64, m * T:(m + 1) * T], ACT.Copy)
            ins.then_inc(sem("k_copied"), 1)
        g.after()
        split_hi()
        act.wait_ge(tile_done, tile_at(g.n))
        for n in range(NB):
            ins = nc.scalar.activation(v_tok[:, (n + 1) * 256:(n + 2) * 256], bank(n, 256), ACT.Copy)
        ins.then_inc(sem("v_copied"), 1)
        g.after()
        C["qraw"].n = 1
        tiles("qproj", copy_raw, (C["qraw"], 2))

        def exps(i):
            b = (i % 2) * 24
            act.wait_ge(sem("nm_ready"), i + 1)
            for hh in range(4):
                o = (i % 2) * 1024 + hh * 256
                nc.scalar.activation(s_sb[:, o:o + 256], s_sb[:, o:o + 256], ACT.Exp,
                                     bias=mx[:, b + 4 + hh:b + 5 + hh], accum_out=mx[:, b + 12 + hh:b + 13 + hh])
            nc.scalar.activation(mx[:, b + 16:b + 20], mx[:, b + 8:b + 12], ACT.Exp).then_inc(sem("exp_done"), 1)

        exps(0)
        for i in range(4 * NB):
            n, gkv = divmod(i, 4)
            act.wait_ge(sem("pt_psum"), i + 1)
            if i >= 2:
                act.wait_ge(sem("o_done"), i - 1)
            nc.scalar.activation(p_t[:, (i % 2) * 1024:(i % 2) * 1024 + 512], bank(2), ACT.Copy).then_inc(sem("pt_a"), 1)
            if i + 1 < 4 * NB:
                exps(i + 1)
            act.wait_ge(sem("o_done"), i + 1)
            nc.scalar.activation(as3(h_hi[:, :], DC)[:, 2 * gkv:2 * gkv + 2, n * P:(n + 1) * P],
                                 as3(bank(6, 256), 2), ACT.Copy).then_inc(sem("o_hi"), 1)

        o_chunk = Count()

        def copy_f(u):
            for m in range(2):
                square(bank(2 * u + m), m)
            for m in range(2):
                ins = nc.scalar.activation(chunk(f, o_chunk.now() + m), bank(2 * u + m), ACT.Copy)
            ins.then_inc(acc_free["act"], 1)
            o_chunk.after(2)

        norm_start()
        tiles("oproj", copy_f, (o_chunk, 2), (C["sq"], 2))
        norm_std(EPS_A)
        x_squares()
        norm_std(EPS_A)
        split_norm(h_hi)
        if stop == "x3":
            return
        ffn(1)
        if stop == "x4":
            return

        def sv(k, n=1):
            return small[:, k * 32:(k + n) * 32]

        split_norm(h_hi, lambda c: mod[:, c:c + 1])

        def copy_u(u):
            for m in range(2):
                ins = nc.scalar.activation(chunk(f, u_chunk.now() + m), bank(2 * u + m), ACT.Copy)
            ins.then_inc(acc_free["act"], 1)
            u_chunk.after(2)

        u_chunk = Count()
        nc.scalar.activation(sv(0), vs("log_dt", 0, 32), ACT.Exp).then_inc(sem("s5_dt"), 1)
        act.wait_ge(sem("s5_angles"), 1)
        nc.scalar.activation(sv(6), sv(1), ACT.Exp)
        nc.scalar.activation(sv(7), sv(4), ACT.Tanh, scale=0.5)
        nc.scalar.activation(sv(8), sv(3), ACT.Sin)
        nc.scalar.activation(sv(9), sv(3), ACT.Sin, scale=0.5).then_inc(sem("s5_funcs"), 1)
        tiles("s5_in", copy_u, (u_chunk, 2))
        act.wait_ge(sem("turns_done"), 1)
        nc.scalar.activation(sin5[:, :], turn5[:, :], ACT.Sin, scale=6.283185)
        nc.scalar.activation(cos5[:, :], turn5[:, :], ACT.Sin, scale=3.1415925).then_inc(sem("tables"), 1)
        for half in range(2):
            act.wait_ge(sem("b_t_psum"), half + 1)
            nc.scalar.activation(b_t[:, half * 1024:(half + 1) * 1024], ps[:, 6 * T:8 * T], ACT.Copy).then_inc(sem("b_t_done"), 1)
        S = {"done": Count(), "used": Count(2)}
        act.wait_ge(sem("turns_used"), 1)
        nc.scalar.activation(as3(ub[:, :], DC), as3(f[:, :], DC)[:, :, 0:P], ACT.Copy).then_inc(sem("ub_ready"), DC)

        def block5(b):
            for j in range(DC):
                act.wait_ge(sem("bu_done"), S["done"].after())
                act.wait_ge(sem("bu_used"), S["used"].now(1))
                S["used"].after()
                nc.scalar.activation(as3(bu5[j % 2][:, :], 4), as3(ps[:, 0:4 * T], 4)[:, :, 0:2 * P],
                                     ACT.Copy).then_inc(sem("bu_copied"), 1)
                if b is not None:
                    nc.scalar.activation(ub[:, j * P:(j + 1) * P], f[:, bass.ds(b * P + (j * T + P), P)],
                                         ACT.Copy).then_inc(sem("ub_ready"), 1)

        with rounds(act, NB - 1, *[(c, DC) for c in S.values()]) as b:
            block5(b)
        block5(None)
        act.wait_ge(sem("y5_read"), NB * DC + 2)
        for c in range(DC):
            if c >= 2:
                act.wait_ge(h_ready, 40 + c - 1)
            nc.scalar.activation(chunk(gl, c % 2), chunk(f, c), ACT.Gelu_apprx_tanh).then_inc(sem("act_step"), 1)
            act.wait_ge(sem("act_step"), c + 1)
            nc.scalar.activation(chunk(h_hi, c), chunk(gl, c % 2), ACT.Copy).then_inc(h_hi_done, 1)
        oc, xw = Count(), Count(freed["dve"]["s5_glu"])

        def glu(u):
            j = oc.now()
            nc.scalar.activation(chunk(tg, u), bank(2 * u), ACT.Identity, bias=v("b_glu", j)).then_inc(sem("glu_pre"), 1)
            nc.scalar.activation(chunk(tv, u), bank(2 * u + 1), ACT.Sigmoid, bias=v("b_glu", j + DC)).then_inc(sem("glu_pre"), 1)
            act.wait_ge(acc_free["dve"], xw.after())
            square(chunk(x, j), (u + FIRST["s5_glu"]) % 2)
            oc.after()

        norm_start()
        tiles("s5_glu", glu, (oc, 1), (xw, 1), (C["sq"], 1))
        norm_std(EPS_B)
        split_norm(h_hi, lambda c: mod[:, 24 + c:25 + c])
        if stop == "x5":
            return

        def mlp(layer):
            ar = Count(4 * FH + 2 * MH * layer)
            rsq = Count(2 * MH * layer)

            def relu(u):
                act.wait_ge(a_ready, ar.now(2))
                nc.scalar.activation(chunk(tg, u), bank(2 * u), ACT.Relu)
                nc.scalar.activation(chunk(tv, u), bank(2 * u + 1), ACT.Relu).then_inc(acc_free["act"], 1)
                for t in (tg, tv):
                    act.wait_ge(sem("relu_sq"), rsq.after())
                    nc.scalar.activation(chunk(a_hi, hc.now()), chunk(t, u), ACT.Copy).then_inc(a_hi_done, 1)
                    hc.after()
                ar.after(2)

            def nothing(u):
                pass

            oc = Count()

            def squares(u):
                act.wait_ge(acc_free["dve"], xw.after())
                square(chunk(x, oc.now()), (u + FIRST[f"mlp{layer}_out_b"]) % 2)
                oc.after()

            for half in "ab":
                hc = Count()
                tiles(f"mlp{layer}_in_{half}", relu, (hc, 2), (rsq, 2), (ar, 2))
                if half == "a":
                    tiles(f"mlp{layer}_out_a", nothing)
                else:
                    xw = Count(freed["dve"][f"mlp{layer}_out_b"])
                    norm_start()
                    tiles(f"mlp{layer}_out_b", squares, (oc, 1), (xw, 1), (C["sq"], 1))
            norm_std(EPS_B)

        mlp(0)
        split_norm(h_hi, lambda c: mod[:, ADA + c:ADA + c + 1])
        if stop == "x6":
            return

        split_hi()
        act.wait_ge(tile_done, tile_at(g.n))
        act.wait_ge(h_ready, 64)
        nc.scalar.activation(tg[0:32, 0:T], bank(2 * (g.n % 2), T, 0, 32), ACT.Identity, bias=v("dt_bias", 0, 32)).then_inc(sem("dt_copied"), 1)
        nc.scalar.activation(small32, v("a_log", 0, 32), ACT.Exp).then_inc(sem("a_exp"), 1)
        g.after()
        act.wait_ge(sem("dt_abs"), 1)
        nc.scalar.activation(tg[0:32, T:2 * T], gl[0:32, 0:T], ACT.Exp, scale=-1.0).then_inc(sem("dt_exp"), 1)
        act.wait_ge(sem("dt_onep"), 1)
        nc.scalar.activation(tv[0:32, 0:T], tv[0:32, T:2 * T], ACT.Ln).then_inc(sem("dt_ln"), 1)
        zc = Count()

        def silu_z(u):
            nc.scalar.activation(chunk(zt, zc.now()), bank(2 * u), ACT.Silu).then_inc(sem("xbc_done"), 1)
            nc.scalar.activation(chunk(zt, zc.now() + 1), bank(2 * u + 1), ACT.Silu).then_inc(acc_free["act"], 1)
            zc.after(2)

        tiles("m2_z", silu_z, (zc, 2))
        act.wait_ge(sem("acs_done"), 1)
        act.wait_ge(sem("ident_landed"), 16)
        nc.scalar.activation(ident_r[0:32, :], ident[0:32, 0:32], ACT.Copy)
        nc.scalar.activation(acs_hi[0:32, :], acs_row[0:32, :], ACT.Copy).then_inc(sem("acs_hi_done"), 1)
        act.wait_ge(sem("rows_t"), 1)
        nc.scalar.activation(sq[:, 0:256], bank(6, 256), ACT.Copy).then_inc(sem("rows_copied"), 1)
        act.wait_ge(sem("decay_arg"), 1)
        nc.scalar.activation(decay, decay, ACT.Exp)
        nc.scalar.activation(cdec[:, :], bank(7, P), ACT.Exp, scale=float(D)).then_inc(sem("cdec_done"), 1)
        xc, xd, fd, gc = Count(), Count(ZC // 2), Count(freed["dve"]["m2_xbc"]), Count(2 * FH * 2)

        def conv_silu(u):
            act.wait_ge(sem("xbc_done"), xd.now(2))
            for m, t in ((0, tg), (1, tv)):
                nc.scalar.activation(chunk(t, u), bank(2 * u + m), ACT.Identity, scale=v("m2_conv_w", xc.now() + (3 * XC + m)),
                                     bias=v("m2_conv_b", xc.now() + m)).then_inc(conv_pre, 1)
            split_hi()
            act.wait_ge(gate_conv, gc.after())
            nc.scalar.activation(chunk(xbc, xc.now()), chunk(tg, u), ACT.Silu).then_inc(sem("xbc_done"), 1)
            act.wait_ge(acc_free["dve"], fd.after())
            nc.scalar.activation(chunk(xbc, xc.now() + 1), chunk(tv, u), ACT.Silu).then_inc(sem("xbc_done"), 1)
            xc.after(2)
            xd.after(2)

        tiles("m2_xbc", conv_silu, (xc, 2), (xd, 2), (fd, 1), (gc, 1), splits=True)

        def copies(grp):
            act.wait_ge(sem("bt_done"), grp + 1)
            nc.scalar.activation(b_tok[:, 0:384], bank(6, 384), ACT.Copy).then_inc(sem("bt_copied"), 1)
            act.wait_ge(sem("cb_done"), grp + 1)
            if grp:
                act.wait_ge(sem("m_ready"), 8 * grp)
            nc.scalar.activation(cbm[:, :], bank(5), ACT.Copy).then_inc(sem("cb_copied"), 1)

        def heads(grp):
            for hh in range(8):
                n, pair, q_ = 8 * grp + hh, 4 * grp + hh // 2, hh // 2
                p0 = 64 * (hh % 2)
                act.wait_ge(sem("diff_done"), n + 1)
                nc.scalar.activation(lmat[n % 3], lmat[n % 3], ACT.Exp).then_inc(sem("exp2_done"), 1)
                if q_ >= 2 and hh % 2 == 0:
                    act.wait_ge(sem("y_summed"), pair - 1)
                nc.scalar.activation(ea[p0:p0 + 64, (q_ % 2) * T:(q_ % 2 + 1) * T], bank(hh % 2, T, p0, p0 + 64),
                                     ACT.Exp).then_inc(sem("ea_done"), 1)
                if hh == 1 and grp:
                    group_hi(grp - 1)

        def group_squares(grp):
            for q_ in range(4):
                act.wait_ge(sem("gated"), 4 * grp + q_ + 1)
                if q_ < 2:
                    act.wait_ge(sem("y_summed"), 4 * (grp + 1))
                else:
                    act.wait_ge(sem("gsum_done"), 4 * grp + q_ - 1)
                nc.scalar.activation(chunk(ea, q_ % 2), chunk(yg, q_), ACT.Square).then_inc(sem("gsq_done"), 1)

        def group_norm(grp):
            act.wait_ge(sem("gsum_done"), 4 * (grp + 1))
            nc.scalar.activation(rstd[:, :], bank(7), ACT.Sqrt, bias=EPS_B, scale=D / 512.0).then_inc(sem("gstd_done"), 1)

        def group_hi(grp):
            for q_ in range(4):
                act.wait_ge(sem("y_normed"), 4 * grp + q_ + 1)
                nc.scalar.activation(chunk(a_hi, 4 * grp + q_), chunk(yg, q_), ACT.Copy).then_inc(sem("y_hi"), 1)

        copies(0)
        heads(0)
        for grp in range(1, 4):
            copies(grp)
            group_squares(grp - 1)
            group_norm(grp - 1)
            heads(grp)
        group_squares(3)
        group_norm(3)
        group_hi(3)
        oc, xw = Count(), Count(freed["dve"]["m2_out"])

        def squares(u):
            act.wait_ge(acc_free["dve"], xw.after())
            square(chunk(x, oc.now()), (u + FIRST["m2_out"]) % 2)
            oc.after()

        norm_start()
        tiles("m2_out", squares, (oc, 1), (xw, 1), (C["sq"], 1))
        norm_std(EPS_B)
        split_norm(h_hi, lambda c: mod[:, ADA + 24 + c:ADA + 25 + c])
        if stop == "x7":
            return
        mlp(1)

    @block.vector
    def _(dve):
        g, split = Count(), Count()
        C = {k: Count() for k in ("norm", "step", "hi", "lo", "conv", "a_hi", "x", "qraw", "ada", "landed")}

        def mark(ins):
            ins.then_inc(dve_step, 1)
            return C["step"].after()

        def split_lo():
            if split.n >= total:
                return
            u = split.n % 2
            dve.wait_ge(w_hi_done, split.after())
            o = slice(u * TILE, (u + 1) * TILE)
            nc.vector.tensor_tensor(w_lo[:, o], raw[:, o], w_hi[:, o].bitcast(f32), SUB).then_inc(w_split, 1)

        def ada_product():
            dve.wait_ge(ada_landed, C["landed"].after(16))
            dve.wait_ge(ada_used, C["ada"].after())
            for i in range(2 * DC):
                k, o = i // 2, slice(i % 2 * P, i % 2 * P + P)
                w, c = ada_w[:, k * 2 * P + i % 2 * P:k * 2 * P + i % 2 * P + P], cond[:, k:k + 1]
                if k == 0:
                    ins = nc.vector.tensor_scalar(ada_acc[:, o], w, c, None, MUL)
                else:
                    dve.wait_ge(dve_step, C["step"].now(1))
                    ins = nc.vector.scalar_tensor_tensor(ada_acc[:, o], w, c, ada_acc[:, o], MUL, ADD)
                if i < 2 * DC - 1:
                    mark(ins)
            ins.then_inc(ada_summed, 1)

        def tiles(name, body, *counts, ada=None, splits=False):
            steps, at_end = ADA_STEPS[ada] if ada else ((), False)

            def step(with_ada):
                if not splits:
                    split_lo()
                body(g.n % 2)
                g.after()
                if with_ada:
                    ada_product()

            left = TILES[name]
            n = (left - (2 if split.n + left > total else 0)) // 2
            per = {id(c): [c, 2 * k] for c, k in counts}
            for c, k in ((C["ada"], 1), (C["landed"], 16), (C["step"], 2 * DC - 1)):
                per.setdefault(id(c), [c, 0])[1] += k * len(steps)
            with rounds(dve, n, (g, 2), (split, 2), *per.values()):
                for k in range(2):
                    step(k in steps)
            for _ in range(left - 2 * n):
                step(at_end)

        def norm_rstd():
            dve.wait_ge(std_done, C["norm"].after())
            nc.vector.reciprocal(rcol[:, :], rcol[:, :]).then_inc(rstd_ready, 1)
            dve.wait_ge(rstd_spread, C["norm"].now())

        def norm_x(gains, dst_hi, dst_lo, shift=None):
            def lo(c):
                dve.wait_ge(h_hi_done, C["hi"].after())
                C["lo"].after()
                args = (chunk(dst_lo, c), chunk(tg, c % 2))
                if shift is None:
                    ins = nc.vector.tensor_tensor(*args, chunk(dst_hi, c).bitcast(f32), SUB)
                else:
                    ins = nc.vector.scalar_tensor_tensor(*args, shift(c), chunk(dst_hi, c).bitcast(f32), ADD, SUB)
                ins.then_inc(h_ready, 1)

            for c in range(DC):
                dve.wait_ge(h_ready, C["lo"].now())
                nc.vector.scalar_tensor_tensor(chunk(tg, c % 2), chunk(x, c), gains(c), bank(NORM),
                                               MUL, MUL).then_inc(hf_done, 1)
                if c:
                    lo(c - 1)
            lo(DC - 1)

        def post_norm(gain_name, col):
            norm_rstd()
            steps = []
            for c in range(DC + 1):
                if c < DC:
                    steps.append(mark(nc.vector.scalar_tensor_tensor(
                        chunk(f, c), chunk(f, c), v(gain_name, col + c), bank(NORM), MUL, MUL)))
                if c:
                    dve.wait_ge(dve_step, steps[c - 1])
                    nc.vector.tensor_tensor(chunk(x, c - 1), chunk(x, c - 1), chunk(f, c - 1), ADD).then_inc(x_ready, 1)

        dve.wait_ge(sem("pads_zero"), 1)
        dve.wait_ge(sem("vec_landed"), 16)
        norm_rstd()
        hp3 = as3(hp[:, :], DC)
        at_h = []
        for c in range(DC):
            at_h.append(mark(nc.vector.scalar_tensor_tensor(hp3[:, c, 16:], chunk(x, c), v("mix_pre", c), bank(NORM), MUL, MUL)))
        dve.wait_ge(sem("edge_landed"), 16)
        w3 = [as3(w[:, :], 2) for w in win]

        def pool_lo(grp):
            for c in (2 * grp, 2 * grp + 1):
                dve.wait_ge(sem("pool_dhi"), c + 1)
                nc.vector.tensor_tensor(chunk(dd_lo, c), chunk(f, c), chunk(dd_hi, c).bitcast(f32), SUB).then_inc(pool_d, 1)

        for grp in range(4):
            w = 2 << grp
            src, last = hp3[:, 2 * grp:2 * grp + 2], at_h[2 * grp + 1]
            if grp:
                dve.wait_ge(sem("pool_df"), 2 * grp)
            for lv in range(grp + 1):
                dve.wait_ge(dve_step, last)
                sh = 1 << lv
                last = mark(nc.vector.tensor_tensor(w3[lv % 2][:, :, 16:], src[:, :, 16:], src[:, :, 16 - sh:16 - sh + T], ADD))
                src = w3[lv % 2]
            dve.wait_ge(dve_step, last)
            e = edge[:, grp * 16:(grp + 1) * 16].rearrange("p (o a) -> p o a", o=1).broadcast_to([P, 2, 16])
            last = mark(nc.vector.tensor_tensor(src[:, :, 16:32], src[:, :, 16:32], e, MUL))
            dve.wait_ge(dve_step, last)
            for k in range(2):
                nc.vector.scalar_tensor_tensor(chunk(f, 2 * grp + k), src[:, k, 16:], 1.0 / w, hp3[:, 2 * grp + k, 16:],
                                               MUL, SUB).then_inc(sem("pool_df"), 1)
            if grp:
                pool_lo(grp - 1)
            if grp == 0:
                split_lo()
        pool_lo(3)
        split_lo()
        g.after()
        post_norm("mix_post", 0)
        norm_rstd()
        norm_x(lambda c: v("ffn_pre", c), h_hi, h_lo)
        split_lo()
        if stop == "x1":
            return

        def ffn(layer):
            wcol = 3 * 2 * FC * layer
            hidden = Count()

            def conv_glu(u):
                j = hidden.now()
                for s in (1, 2):
                    for m, t in ((0, tg), (1, tv)):
                        if s == 1:
                            dve.wait_ge(conv_pre, C["conv"].after())
                        else:
                            dve.wait_ge(dve_step, C["step"].now(1 - m))
                        ins = nc.vector.scalar_tensor_tensor(
                            t[:, u * T + s:(u + 1) * T], ps[:, (2 * u + m) * T:(2 * u + m) * T + T - s],
                            v("conv_w", j + (wcol + (2 - s) * 2 * FC + m * FC)), t[:, u * T + s:(u + 1) * T], MUL, ADD)
                        if s == 1:
                            mark(ins)
                        else:
                            ins.then_inc(gate_conv if m == 0 else acc_free["dve"], 1)
                split_lo()
                dve.wait_ge(a_hi_done, C["a_hi"].after())
                nc.vector.tensor_tensor(chunk(a_lo, slot.now()), chunk(gl, u), chunk(a_hi, slot.now()).bitcast(f32),
                                        SUB).then_inc(a_ready, 1)
                hidden.after()
                slot.after()

            def nothing(u):
                pass

            out_chunk = Count()

            def add_out(u):
                dve.wait_ge(tile_done, tile_at(g.now()))
                d = chunk(f, out_chunk.now())
                nc.vector.tensor_tensor(d, d, bank(2 * u), ADD).then_inc(acc_free["dve"], 1)
                out_chunk.after()

            for half in "ab":
                slot = Count()
                tiles(f"ffn{layer}_in_{half}", conv_glu, (hidden, 1), (slot, 1), (C["conv"], 2), (C["step"], 2), (C["a_hi"], 1),
                      ada="in_" + half, splits=True)
                if half == "a":
                    tiles(f"ffn{layer}_out_a", nothing, ada="out_a")
                else:
                    dve.wait_ge(acc_free["act"], freed["act"][f"ffn{layer}_in_b"])
                    tiles(f"ffn{layer}_out_b", add_out, (out_chunk, 1), ada="out_b")
            post_norm("ffn_post", 8 * layer)

        dve.wait_ge(sem("cond_ready"), 1)
        ffn(0)
        if stop == "x2":
            return

        dve.wait_ge(sem("pos_landed"), 16)

        def chain(ins):
            dve.wait_ge(dve_step, mark(ins))

        chain(nc.vector.tensor_copy(cosT[:, :], posi[:, :]))
        chain(nc.vector.tensor_scalar(sinT[:, :], cosT[:, :], v("inv_freq"), None, MUL))
        chain(nc.vector.tensor_scalar(cosT[:, :], sinT[:, :], float(1 / (2 * np.pi)), MAGIC, MUL, ADD))
        chain(nc.vector.tensor_scalar(cosT[:, :], cosT[:, :], MAGIC, None, SUB))
        for part in (TWO_PI_A, TWO_PI_B, TWO_PI_C):
            chain(nc.vector.scalar_tensor_tensor(sinT[:, :], cosT[:, :], -float(part), sinT[:, :], MUL, ADD))
        nc.vector.tensor_scalar(sinT[:, :], sinT[:, :], 3.1415925, -3.1415925, ALU.min, MAX).then_inc(sem("angles"), 1)
        norm_rstd()
        norm_x(lambda c: v("kv_norm", c), a_hi, a_lo)
        norm_x(lambda c: v("mix_pre", 8 + c), h_hi, h_lo)
        dve.wait_ge(sem("half_sin"), 1)
        chain(nc.vector.tensor_tensor(cosT[:, :], cosT[:, :], cosT[:, :], MUL))
        chain(nc.vector.tensor_scalar(cosT[:, :], cosT[:, :], -2.0, 1.0, MUL, ADD))
        dve.wait_ge(sem("full_sin"), 1)
        chain(nc.vector.tensor_scalar(sinT[:, :], chunk(tv, 1), v("rope_sign"), None, MUL))

        def rope(u):
            for m in range(2):
                dve.wait_ge(sem("qraw"), C["qraw"].after())
                nc.vector.tensor_tensor(chunk(tv, m), chunk(tg, m), cosT[:, :], MUL)
                dve.wait_ge(sem("rot"), C["qraw"].now())
                nc.vector.tensor_tensor(chunk(gl, m), bank(6 + m), sinT[:, :], MUL).then_inc(sem("rope_parts"), 1)

        split_lo()
        rope(0)
        g.after()
        split_lo()
        g.after()
        tiles("qproj", rope, (C["qraw"], 2))

        dve.wait_ge(sem("masks_landed"), 16)

        def soften(i):
            n, gkv = divmod(i, 4)
            m4 = lambda k: mx[:, (i % 2) * 24 + 4 * k:(i % 2) * 24 + 4 * k + 4]
            sb4 = as3(s_sb[:, (i % 2) * 1024:(i % 2 + 1) * 1024], 4)
            dve.wait_ge(sem("s_done"), i + 1)
            m0 = 256 if n else 0
            mask4 = masks[:, m0:m0 + 256].rearrange("p (o k) -> p o k", o=1).broadcast_to([P, 4, 256])
            nc.vector.scalar_tensor_tensor(sb4, as3(ps[:, 0:1024], 4), 0.125, mask4, MUL, ADD).then_inc(sem("s_read"), 1)
            dve.wait_ge(sem("s_read"), i + 1)
            chain(nc.vector.tensor_reduce(m4(0), sb4, AX.X, MAX))
            sinks4 = vs("sinks", 4 * gkv, 4 * gkv + 4)
            chain(nc.vector.tensor_tensor(m4(0), m4(0), sinks4, MAX))
            chain(nc.vector.tensor_scalar(m4(1), m4(0), -1.0, None, MUL))
            nc.vector.tensor_tensor(m4(2), sinks4, m4(1), ADD).then_inc(sem("nm_ready"), 1)

        def weigh(i):
            m4 = lambda k: mx[:, (i % 2) * 24 + 4 * k:(i % 2) * 24 + 4 * k + 4]
            sb4 = as3(s_sb[:, (i % 2) * 1024:(i % 2 + 1) * 1024], 4)
            dve.wait_ge(sem("exp_done"), i + 1)
            chain(nc.vector.tensor_tensor(m4(3), m4(3), m4(4), ADD))
            chain(nc.vector.reciprocal(m4(5), m4(3)))
            rec = m4(5).rearrange("p (a o) -> p a o", o=1).broadcast_to([P, 4, 256])
            nc.vector.tensor_tensor(sb4, sb4, rec, MUL).then_inc(sem("p_ready"), 1)

        def output_lo(i):
            n, gkv = divmod(i, 4)
            dve.wait_ge(sem("o_hi"), i + 1)
            dst = (slice(None), slice(2 * gkv, 2 * gkv + 2), slice(n * P, (n + 1) * P))
            nc.vector.tensor_tensor(as3(h_lo[:, :], DC)[dst], as3(bank(6, 256), 2), as3(h_hi[:, :], DC)[dst].bitcast(f32),
                                    SUB).then_inc(sem("o_split"), 1)

        soften(0)
        for i in range(4 * NB):
            weigh(i)
            if i + 1 < 4 * NB:
                soften(i + 1)
            dve.wait_ge(sem("pt_psum"), i + 1)
            if i >= 2:
                dve.wait_ge(sem("o_done"), i - 1)
            nc.vector.tensor_copy(p_t[:, (i % 2) * 1024 + 512:(i % 2 + 1) * 1024], bank(3)).then_inc(sem("pt_b"), 1)
            if i:
                output_lo(i - 1)
        output_lo(4 * NB - 1)

        def nothing(u):
            pass

        tiles("oproj", nothing)
        post_norm("mix_post", 8)
        norm_rstd()
        norm_x(lambda c: v("ffn_pre", 8 + c), h_hi, h_lo)
        if stop == "x3":
            return
        ffn(1)
        if stop == "x4":
            return

        dve.wait_ge(ada_used, 1 + ADA_TILES)
        chain(nc.vector.scalar_tensor_tensor(mod[:, :], bank(MOD, 2 * ADA, off=2), float(D), vs("ada_b", 0, 2 * ADA), MUL, ADD))

        def modulation(layer, scale_at, norm):
            c0 = ADA * layer + scale_at
            a, _ = VECS[norm]
            chain(nc.vector.scalar_tensor_tensor(gain[:, :], mod[:, c0:c0 + 8], 1.0, vec[:, a + 8 * layer:a + 8 * layer + 8], ADD, MUL))

        def norm_mod(layer, shift_at):
            norm_rstd()
            norm_x(lambda c: gain[:, c:c + 1], h_hi, h_lo, lambda c: mod[:, ADA * layer + shift_at + c:ADA * layer + shift_at + c + 1])

        modulation(0, 8, "norm_mix")
        norm_mod(0, 0)

        def sv(k):
            return small[:, k * 32:(k + 1) * 32]

        TT = lambda o, a, b, op: chain(nc.vector.tensor_tensor(sv(o), a, b, op))
        TS = lambda o, a, s1, s2, op1, op2=None: chain(
            nc.vector.tensor_scalar(sv(o), a, s1, s2, op1, op2) if op2 is not None else nc.vector.tensor_scalar(sv(o), a, s1, None, op1))
        STT = lambda o, a, s1, b, op1, op2: chain(nc.vector.scalar_tensor_tensor(sv(o), a, s1, b, op1, op2))
        lre, lim = vs("lam_re", 0, 32), vs("lam_im", 0, 32)
        dve.wait_ge(sem("s5_dt"), 1)
        TT(1, lre, sv(0), MUL)
        TT(2, lim, sv(0), MUL)
        TS(3, sv(2), float(1 / (2 * np.pi)), MAGIC, MUL, ADD)
        TS(5, sv(3), MAGIC, None, SUB)
        STT(3, sv(5), -TWO_PI_A, sv(2), MUL, ADD)
        STT(3, sv(5), -TWO_PI_B, sv(3), MUL, ADD)
        STT(3, sv(5), -float(TWO_PI_C), sv(3), MUL, ADD)
        TS(3, sv(3), 3.1415925, -3.1415925, ALU.min, MAX)
        TS(10, sv(3), float(1 / (2 * np.pi)), None, MUL)
        nc.vector.tensor_scalar(sv(4), sv(1), -0.5, 0.5, MAX, ALU.min).then_inc(sem("s5_angles"), 1)
        dve.wait_ge(sem("s5_funcs"), 1)
        TS(11, sv(7), -1.0, 1.0, MUL, ADD)
        chain(nc.vector.reciprocal(sv(11), sv(11)))
        STT(11, sv(7), 2.0, sv(11), MUL, MUL)
        TS(12, sv(6), 1.0, 3e38, SUB, ALU.min)
        TT(13, sv(1), sv(4), ALU.is_equal)
        TT(11, sv(11), sv(12), SUB)
        TT(11, sv(11), sv(13), MUL)
        TT(11, sv(11), sv(12), ADD)
        TT(12, sv(9), sv(9), MUL)
        TS(13, sv(12), -2.0, None, MUL)
        TS(12, sv(12), -2.0, 1.0, MUL, ADD)
        TT(12, sv(11), sv(12), MUL)
        TT(12, sv(12), sv(13), ADD)
        TT(13, sv(6), sv(8), MUL)
        TT(14, lre, lre, MUL)
        TT(15, lim, lim, MUL)
        TT(14, sv(14), sv(15), ADD)
        chain(nc.vector.reciprocal(sv(14), sv(14)))
        TT(15, sv(12), lre, MUL)
        TT(16, sv(13), lim, MUL)
        TT(15, sv(15), sv(16), ADD)
        TT(15, sv(15), sv(14), MUL)
        TT(16, sv(13), lre, MUL)
        TT(17, sv(12), lim, MUL)
        TT(16, sv(16), sv(17), SUB)
        TT(16, sv(16), sv(14), MUL)
        dve.wait_ge(sem("b_landed"), 16)
        wide = lambda k: sv(k).rearrange("p (a o) -> p a o", o=1).broadcast_to([P, 32, 32])
        t3 = lambda ap: as3(ap, 32)
        br, bi_ = t3(b_raw[:, 0:1024]), t3(b_raw[:, 1024:2048])
        for half, (x_, y_, op) in enumerate(((br, bi_, SUB), (bi_, br, ADD))):
            dst = t3(b_bar[:, half * 1024:(half + 1) * 1024])
            chain(nc.vector.tensor_tensor(dst, x_, wide(15), MUL))
            chain(nc.vector.tensor_tensor(t3(b_tmp), y_, wide(16), MUL))
            nc.vector.tensor_tensor(dst, dst, t3(b_tmp), op).then_inc(sem("b_bar_done"), 1)
            dve.wait_ge(sem("b_bar_done"), half + 1)
        tok = vs("tok", 0, P).rearrange("p (o t) -> p o t", o=1).broadcast_to([P, 32, P])
        phi = sv(10).rearrange("p (a o) -> p a o", o=1).broadcast_to([P, 32, P])
        chain(nc.vector.tensor_tensor(as3(turn5[:, :], 32), tok, phi, MUL))
        chain(nc.vector.tensor_scalar(cos5[:, :], turn5[:, :], MAGIC, MAGIC, ADD, SUB))
        nc.vector.tensor_tensor(turn5[:, :], turn5[:, :], cos5[:, :], SUB).then_inc(sem("turns_done"), 1)
        tiles("s5_in", nothing)
        dve.wait_ge(sem("tables"), 1)
        chain(nc.vector.tensor_tensor(cos5[:, :], cos5[:, :], cos5[:, :], MUL))
        nc.vector.tensor_scalar(cos5[:, :], cos5[:, :], -2.0, 1.0, MUL, ADD).then_inc(sem("turns_used"), 1)
        dve.wait_ge(sem("turns_used"), 1)

        S = {"bu": Count(1), "v": Count(), "scan": Count(1), "carry": Count(2), "y": Count(2)}
        cs = lambda t, j: as3(t[:, j * T:(j + 1) * T], 4)

        def rotate_in(j):
            w = [as3(t[:, :], 4) for t in w5[j % 2]]
            b4 = as3(bu5[j % 2][:, :], 4)
            dve.wait_ge(sem("bu_copied"), S["bu"].after())
            dve.wait_ge(sem("scanned"), S["scan"].now())
            nc.vector.tensor_tensor(w[0], cs(cos5, j), b4[:, :, 0:P], MUL)
            nc.vector.tensor_tensor(w[1], cs(sin5, j), b4[:, :, P:2 * P], MUL).then_inc(sem("rot_in"), 1)
            nc.vector.tensor_tensor(w[2], cs(cos5, j), b4[:, :, P:2 * P], MUL)
            nc.vector.tensor_tensor(w[3], cs(sin5, j), b4[:, :, 0:P], MUL).then_inc(sem("bu_used"), 1)

        def scan(j):
            dve.wait_ge(sem("carry"), S["carry"].now(1))
            S["carry"].after()
            for half in range(2):
                dve.wait_ge(sem("v_ready"), S["v"].after())
                for i in range(4):
                    s_ = 4 * j + i
                    ins = nc.vector.tensor_tensor_scan(
                        g5[j % 2][half][:, i * P:(i + 1) * P], sv(6)[:, s_:s_ + 1].broadcast_to([P, P]),
                        w5[j % 2][2 * half][:, i * P:(i + 1) * P], sv(18 + half)[:, s_:s_ + 1], MUL, ADD)
            ins.then_inc(sem("scanned"), 1)
            S["scan"].after()

        def rotate_out(j):
            dve.wait_ge(sem("scanned"), S["scan"].now())
            gr, gi = g5[j % 2]
            nc.vector.tensor_tensor(p5[j % 2][0][:, :], cos5[:, j * T:(j + 1) * T], gr[:, :], MUL)
            nc.vector.tensor_tensor(p5[j % 2][1][:, :], sin5[:, j * T:(j + 1) * T], gi[:, :], MUL).then_inc(sem("p_dve"), 1)

        def finish(j, b):
            dve.wait_ge(sem("y5_done"), S["y"].after())
            c0 = j * T + b * P
            uj = f[:, c0:c0 + P] if isinstance(b, int) else f[:, bass.ds(c0, P)]
            nc.vector.scalar_tensor_tensor(uj, uj, v("s5_d", j), bank(6 + j % 2, P), MUL, ADD).then_inc(sem("y5_read"), 1)

        def block5(b, more):
            for j in range(DC):
                if j < DC - 1 or more:
                    rotate_in((j + 1) % DC)
                scan(j)
                rotate_out(j)
                if j:
                    finish(j - 1, b)
            finish(DC - 1, b)

        rotate_in(0)
        with rounds(dve, NB - 1, *[(c, DC * (2 if k == "v" else 1)) for k, c in S.items()]) as b:
            block5(b, True)
        block5(NB - 1, False)
        dve.wait_ge(sem("carry"), 2 + DC * NB)
        for c in range(DC):
            dve.wait_ge(h_hi_done, C["hi"].after())
            C["lo"].after()
            nc.vector.tensor_tensor(chunk(h_lo, c), chunk(gl, c % 2), chunk(h_hi, c).bitcast(f32), SUB).then_inc(h_ready, 1)
        oc, gp_ = Count(), Count()

        def glu(u):
            dve.wait_ge(sem("glu_pre"), gp_.after(2))
            chain(nc.vector.tensor_tensor(chunk(tg, u), chunk(tg, u), chunk(tv, u), MUL))
            xx = chunk(x, oc.now())
            nc.vector.scalar_tensor_tensor(xx, chunk(tg, u), mod[:, bass.ds(oc.now() + 16, 1)], xx, MUL, ADD).then_inc(acc_free["dve"], 1)
            oc.after()

        tiles("s5_glu", glu, (oc, 1), (gp_, 2), (C["step"], 1))
        modulation(0, 32, "norm_mlp")
        norm_mod(0, 24)
        if stop == "x5":
            return

        def mlp(layer):
            fa = Count(freed["act"][f"mlp{layer}_in_a"])

            def squared(u):
                dve.wait_ge(acc_free["act"], fa.after())
                for t in (tg, tv):
                    nc.vector.tensor_tensor(chunk(t, u), chunk(t, u), chunk(t, u), MUL).then_inc(sem("relu_sq"), 1)
                for t in (tg, tv):
                    dve.wait_ge(a_hi_done, C["a_hi"].after())
                    nc.vector.tensor_tensor(chunk(a_lo, hc.now()), chunk(t, u), chunk(a_hi, hc.now()).bitcast(f32), SUB).then_inc(a_ready, 1)
                    hc.after()

            def residual(u):
                dve.wait_ge(tile_done, tile_at(g.now()))
                xx = chunk(x, oc.now())
                nc.vector.scalar_tensor_tensor(xx, bank(2 * u), mod[:, bass.ds(oc.now() + (ADA * layer + 40), 1)], xx,
                                               MUL, ADD).then_inc(acc_free["dve"], 1)
                oc.after()

            for half in "ab":
                hc, oc = Count(), Count()
                tiles(f"mlp{layer}_in_{half}", squared, (fa, 1), (hc, 2), (C["a_hi"], 2))
                if half == "b":
                    dve.wait_ge(acc_free["dve"], freed["dve"][f"mlp{layer}_out_b"])
                tiles(f"mlp{layer}_out_{half}", residual, (oc, 1))

        mlp(0)
        modulation(1, 8, "norm_mix")
        norm_mod(1, 0)
        if stop == "x6":
            return

        r32 = slice(0, 32)
        V, E_, L, W_, Ab = tg[r32, 0:T], tg[r32, T:2 * T], tv[r32, 0:T], tv[r32, T:2 * T], gl[r32, 0:T]
        split_lo()
        g.after()
        dve.wait_ge(sem("dt_copied"), 1)
        nc.vector.memset(one_col[:, :], 1.0)
        nc.vector.scalar_tensor_tensor(Ab, V, -1.0, V, MUL, MAX).then_inc(sem("dt_abs"), 1)
        dve.wait_ge(sem("dt_exp"), 1)
        nc.vector.tensor_scalar(W_, E_, 1.0, None, ADD).then_inc(sem("dt_onep"), 1)
        dve.wait_ge(sem("dt_ln"), 1)
        chain(nc.vector.tensor_scalar(W_, W_, 1.0, None, SUB))
        chain(nc.vector.tensor_scalar(Ab, W_, 0.0, None, ALU.is_equal))
        chain(nc.vector.tensor_tensor(W_, W_, Ab, ADD))
        chain(nc.vector.tensor_tensor(L, L, Ab, ADD))
        chain(nc.vector.reciprocal(W_, W_))
        chain(nc.vector.tensor_tensor(L, L, E_, MUL))
        chain(nc.vector.tensor_tensor(L, L, W_, MUL))
        chain(nc.vector.scalar_tensor_tensor(dt_row[r32, :], V, 0.0, L, MAX, ADD))
        dve.wait_ge(sem("a_exp"), 1)
        chain(nc.vector.tensor_scalar(Ab, dt_row[r32, :], small32, -1.0, MUL, MUL))
        for c in range(NB):
            o = slice(c * P, (c + 1) * P)
            chain(nc.vector.tensor_tensor_scan(acs_row[r32, o], one_col[r32, :].broadcast_to([32, P]), Ab[:, o], 0.0, MUL, ADD))
        for c in range(NB):
            ins = nc.vector.tensor_scalar(diag[r32, c * 32:(c + 1) * 32], ident[r32, 0:32], acs_row[r32, (c + 1) * P - 1:(c + 1) * P], None, MUL)
        ins.then_inc(sem("acs_done"), 1)
        tiles("m2_z", nothing)
        dve.wait_ge(sem("acs_hi_done"), 1)
        dve.wait_ge(sem("rows_t"), 1)
        nc.vector.tensor_tensor(acs_lo[r32, :], acs_row[r32, :], acs_hi[r32, :].bitcast(f32), SUB).then_inc(sem("acs_split"), 1)
        dve.wait_ge(sem("rows_copied"), 1)
        dve.wait_ge(sem("alast_done"), 1)
        nc.vector.scalar_tensor_tensor(decay, bank(7, P), float(D), acs_t, MUL, SUB).then_inc(sem("decay_arg"), 1)
        xc = Count()

        def conv4(u):
            for s in (1, 2, 3):
                for m, t in ((0, tg), (1, tv)):
                    if s == 1:
                        dve.wait_ge(conv_pre, C["conv"].after())
                    else:
                        dve.wait_ge(dve_step, C["step"].now(0 if s == 3 and m else 1))
                    ins = nc.vector.scalar_tensor_tensor(
                        t[:, u * T + s:(u + 1) * T], ps[:, (2 * u + m) * T:(2 * u + m) * T + T - s],
                        v("m2_conv_w", xc.now() + ((3 - s) * XC + m)), t[:, u * T + s:(u + 1) * T], MUL, ADD)
                    if s < 3:
                        mark(ins)
                    else:
                        ins.then_inc(gate_conv if m == 0 else acc_free["dve"], 1)
            split_lo()
            xc.after(2)

        tiles("m2_xbc", conv4, (xc, 2), (C["conv"], 2), (C["step"], 4), splits=True)

        dve.wait_ge(sem("cdec_done"), 1)
        dve.wait_ge(sem("causal_landed"), 16)
        def token_major(grp):
            for c in range(NB):
                dve.wait_ge(sem("xt_done"), 4 * grp + c + 1)
                d8 = dt_t[:, c * 32 + 8 * grp:c * 32 + 8 * grp + 8].rearrange("p (a o) -> p a o", o=1).broadcast_to([P, 8, 64])
                nc.vector.tensor_tensor(as3(xdt[:, c * T:(c + 1) * T], 8), as3(bank(c), 8), d8, MUL).then_inc(sem("xdt_done"), 1)
            for c in range(NB - 1):
                dve.wait_ge(sem("xdt_done"), 4 * grp + c + 1)
                d8 = decay[:, c * 32 + 8 * grp:c * 32 + 8 * grp + 8].rearrange("p (a o) -> p a o", o=1).broadcast_to([P, 8, 64])
                nc.vector.tensor_tensor(as3(xdtd[:, c * T:(c + 1) * T], 8), as3(xdt[:, c * T:(c + 1) * T], 8), d8, MUL).then_inc(sem("xdtd_done"), 1)
        def group_norm(grp):
            dve.wait_ge(sem("gstd_done"), grp + 1)
            chain(nc.vector.reciprocal(rstd[:, :], rstd[:, :]))
            for q_ in range(4):
                n = 4 * grp + q_
                nc.vector.scalar_tensor_tensor(chunk(yg, q_), chunk(yg, q_), v("m2_norm", n), rstd[:, :], MUL, MUL).then_inc(sem("y_normed"), 1)
        def split_y(grp):
            for q_ in range(4):
                n = 4 * grp + q_
                dve.wait_ge(sem("y_hi"), n + 1)
                nc.vector.tensor_tensor(chunk(a_lo, n), chunk(yg, q_), chunk(a_hi, n).bitcast(f32), SUB).then_inc(sem("y_split"), 1)
        def heads(grp):
            for c in range(NB - 1):
                dve.wait_ge(sem("st_done"), 3 * grp + c + 1)
                dst = prev[:, c * T:(c + 1) * T]
                if c == 0:
                    nc.vector.tensor_copy(dst, bank(4)).then_inc(sem("prev_done"), 1)
                else:
                    dve.wait_ge(sem("prev_done"), 3 * grp + c)
                    h8 = cdec[:, c * 32 + 8 * grp:c * 32 + 8 * grp + 8].rearrange("p (a o) -> p a o", o=1).broadcast_to([P, 8, 64])
                    chain(nc.vector.tensor_tensor(as3(ytmp[:, :], 8), as3(prev[:, (c - 1) * T:c * T], 8), h8, MUL))
                    nc.vector.tensor_tensor(dst, ytmp[:, :], bank(4 + c), ADD).then_inc(sem("prev_done"), 1)

            def differ(hh):
                n = 8 * grp + hh
                dve.wait_ge(sem("bc_done"), n + 1)
                if n >= 3:
                    dve.wait_ge(sem("yd_done"), n - 2)
                for c in range(NB):
                    o = slice(c * P, (c + 1) * P)
                    ins = nc.vector.scalar_tensor_tensor(lmat[n % 3][:, o], bank(hh % 2, P, off=c * P), acs_t[:, c * 32 + n:c * 32 + n + 1],
                                                         causal[:, :], SUB, ALU.min)
                ins.then_inc(sem("diff_done"), 1)

            def sum_y(q_):
                pair = 4 * grp + q_
                dve.wait_ge(sem("off_done"), pair + 1)
                dve.wait_ge(sem("ea_done"), 2 * pair + 2)
                chain(nc.vector.tensor_tensor(ytmp[:, P:], bank(4 + q_ % 2, T - P, off=P), ea[:, (q_ % 2) * T + P:(q_ % 2 + 1) * T], MUL))
                dve.wait_ge(sem("yd_done"), 2 * pair + 2)
                if grp:
                    dve.wait_ge(sem("y_split"), 4 * (grp - 1) + q_ + 1)
                chain(nc.vector.scalar_tensor_tensor(chunk(yg, q_), chunk(xbc, pair), v("m2_d", pair), bank(2 + q_ % 2), MUL, ADD))
                yy = yg[:, q_ * T + P:(q_ + 1) * T]
                nc.vector.tensor_tensor(yy, yy, ytmp[:, P:], ADD).then_inc(sem("y_summed"), 1)
                dve.wait_ge(sem("y_summed"), pair + 1)

            differ(0)
            differ(1)
            if grp:
                group_norm(grp - 1)
            dve.wait_ge(sem("cb_copied"), grp + 1)
            for hh in range(8):
                n = 8 * grp + hh
                dve.wait_ge(sem("exp2_done"), n + 1)
                nc.vector.tensor_tensor(lmat[n % 3], lmat[n % 3], cbm[:, :], MUL).then_inc(sem("m_ready"), 1)
                if hh < 6:
                    differ(hh + 2)
                if hh == 1 and grp:
                    split_y(grp - 1)
                if hh % 2 == 0 and hh:
                    sum_y(hh // 2 - 1)
            sum_y(3)
        token_major(0)
        heads(0)
        for grp in range(1, 4):
            token_major(grp)
            heads(grp)
        group_norm(3)
        split_y(3)
        oc = Count()

        def residual(u):
            dve.wait_ge(tile_done, tile_at(g.now()))
            xx = chunk(x, oc.now())
            nc.vector.scalar_tensor_tensor(xx, bank(2 * u), mod[:, bass.ds(oc.now() + (ADA + 16), 1)], xx, MUL, ADD).then_inc(acc_free["dve"], 1)
            oc.after()

        tiles("m2_out", residual, (oc, 1))
        modulation(1, 32, "norm_mlp")
        norm_mod(1, 24)
        if stop == "x7":
            return
        mlp(1)
        norm_rstd()
        for c in range(DC):
            nc.vector.scalar_tensor_tensor(chunk(x, c), chunk(x, c), v("final", c), bank(NORM), MUL, MUL).then_inc(sem("y_ready"), 1)

    @block.gpsimd
    def _(gp):
        C = {k: Count() for k in ("norm", "gelu", "rope")}
        C["ada"] = Count(1)
        C["free_dve"] = Count(2)

        def norm_adds(loads=0):
            n = C["norm"].n
            if n:
                gp.wait_ge(norm_sum, n)
            gp.memset(sqsum[:, :], 0.0).then_inc(sq_added, 1)
            for c in range(DC):
                gp.wait_ge(sq_ready, DC * n + c + 1)
                gp.wait_ge(sq_added, 9 * n + c + 1)
                gp.tensor_tensor(sqsum[:, :], sqsum[:, :], chunk(sq, c % 2), ADD).then_inc(sq_added, 1)
                if c % 2 and c < 2 * loads:
                    ada_load()
            C["norm"].after()

        def ada_load():
            gp.wait_ge(ada_summed, C["ada"].after())
            gp.dma_start(ada_w[:, :], ada[bass.ds(C["ada"].now(1) * P, P), :]).then_inc(ada_landed, 16)

        gp.memset(ones[:, :], 1.0 / D).then_inc(sem("ones_set"), 1)
        gp.memset(ada_acc[:, :], 0.0).then_inc(ada_summed, 1)
        for k, (name, start) in enumerate(START.items()):
            gp.memset(gain[:, k:k + 1], 0.0).then_inc(sem(name), start)
        gp.memset(as3(hp[:, :], DC)[:, :, 0:16], 0.0)
        gp.memset(as3(win[0][:, :], 2)[:, :, 0:16], 0.0)
        gp.memset(as3(win[1][:, :], 2)[:, :, 0:16], 0.0).then_inc(sem("pads_zero"), 1)
        gp.dma_start(ada_w[:, :], ada[0:P, :]).then_inc(ada_landed, 16)
        gp.memset(tv[:, 0:1], 0.0).then_inc(acc_free["act"], 2)
        gp.memset(tv[:, 1:2], 0.0).then_inc(acc_free["dve"], 2)
        norm_adds()
        norm_adds()
        norm_adds()
        if stop == "x1":
            return

        def ffn(layer):
            def product(s, load):
                u = (s + first) % 2
                gp.wait_ge(gelu_done, C["gelu"].after())
                gp.wait_ge(acc_free["dve"], C["free_dve"].after())
                gp.tensor_tensor(chunk(gl, u), chunk(gl, u), chunk(tv, u), MUL).then_inc(prod_done, 1)
                if load:
                    ada_load()

            for half in "ab":
                first = FIRST[f"ffn{layer}_in_{half}"]
                with rounds(gp, FH // 2, (C["gelu"], 2), (C["free_dve"], 2), (C["ada"], 1)):
                    product(0, False)
                    product(1, True)
                product(0, True)
                if half == "a":
                    with rounds(gp, DC, (C["ada"], 1)):
                        ada_load()
            C["free_dve"].after(8)
            norm_adds(4 - layer)
            norm_adds()

        ffn(0)
        if stop == "x2":
            return

        gp.wait_ge(acc_free["dve"], freed["dve"]["kproj"])
        kd3 = as3(kdup[:, :], 4)
        gp.memset(kd3[:, :, 0:P], 0.0)
        gp.memset(v_tok[:, 0:256], 0.0)

        def rope_add(dst, m):
            gp.wait_ge(sem("rope_parts"), C["rope"].after())
            gp.tensor_tensor(dst, chunk(tv, m), chunk(gl, m), ADD).then_inc(sem("rope_done"), 1)

        for m in range(2):
            rope_add(chunk(sq, m), m)
        qc = Count()
        with rounds(gp, 2, (C["rope"], 4), (qc, 4)):
            for m in range(4):
                rope_add(chunk(q, qc.now()), m % 2)
                qc.after()
        norm_adds()
        norm_adds()
        if stop == "x3":
            return
        ffn(1)
        if stop == "x4":
            return

        gp.wait_ge(ada_used, 1 + ADA_TILES)
        gp.wait_ge(acc_free["dve"], freed["dve"]["s5_in"])
        gp.dma_start(b_raw[:, :], s5_b).then_inc(sem("b_landed"), 16)
        gp.wait_ge(h_ready, 40)
        gp.dma_start(c_mat[:, 0:2048], s5_c).then_inc(sem("c_landed"), 16)
        gp.wait_ge(sem("c_landed"), 16)
        gp.tensor_scalar(c_mat[:, 1024:2048], c_mat[:, 1024:2048], -1.0, None, MUL)
        gp.tensor_scalar(c_mat[:, 2048:], c_mat[:, 0:1024], -1.0, None, MUL).then_inc(sem("c_ready"), 1)
        gp.wait_ge(sem("s5_angles"), 1)
        gp.memset(small[:, 18 * 32:20 * 32], 0.0).then_inc(sem("carry"), 2)
        gp.wait_ge(sem("turns_used"), 1)
        S = {"in": Count(), "used": Count(2), "scan": Count(1), "dve": Count(), "y": Count(2), "gp": Count()}

        def add_inputs(j):
            w = w5[j % 2]
            gp.wait_ge(sem("rot_in"), S["in"].after())
            gp.tensor_tensor(w[0][:, :], w[0][:, :], w[1][:, :], ADD).then_inc(sem("v_ready"), 1)
            gp.wait_ge(sem("bu_used"), S["used"].after())
            gp.tensor_tensor(w[2][:, :], w[2][:, :], w[3][:, :], SUB).then_inc(sem("v_ready"), 1)

        def rotate_out(j):
            pp, (gr, gi) = p5[j % 2], g5[j % 2]
            gp.wait_ge(sem("scanned"), S["scan"].after())
            gp.wait_ge(sem("y5_done"), S["y"].now(1))
            S["y"].after()
            gp.tensor_tensor(pp[2][:, :], sin5[:, j * T:(j + 1) * T], gr[:, :], MUL)
            gp.tensor_tensor(pp[3][:, :], cos5[:, j * T:(j + 1) * T], gi[:, :], MUL).then_inc(sem("p_gp"), 1)
            gp.wait_ge(sem("p_dve"), S["dve"].after())
            gp.wait_ge(sem("p_gp"), S["gp"].after())
            for half, op in enumerate((SUB, ADD)):
                ends = [as3(pp[2 * half + k][:, :], 4)[:, :, P - 1:P] for k in range(2)]
                dst = small[:, (18 + half) * 32 + 4 * j:(18 + half) * 32 + 4 * j + 4].rearrange("p (a o) -> p a o", o=1)
                ins = gp.tensor_tensor(dst, *ends, op)
            ins.then_inc(sem("carry"), 1)

        def block5(more):
            for j in range(DC):
                if j < DC - 1 or more:
                    add_inputs((j + 1) % DC)
                rotate_out(j)

        add_inputs(0)
        with rounds(gp, NB - 1, *[(c, DC) for c in S.values()]):
            block5(True)
        block5(False)
        norm_adds()
        if stop == "x5":
            return
        norm_adds()
        if stop == "x6":
            return

        gp.wait_ge(h_ready, 64)
        gp.dma_start(causal[:, :], consts[:, UPPER:UPPER + P]).then_inc(sem("causal_landed"), 16)

        def gate(grp, q_):
            n = 4 * grp + q_
            gp.wait_ge(sem("y_summed"), n + 1)
            gp.tensor_tensor(chunk(yg, q_), chunk(yg, q_), chunk(zt, n), MUL).then_inc(sem("gated"), 1)

        for grp in range(4):
            for q_ in range(4):
                gate(grp, q_)
        norm_adds()
        if stop == "x7":
            return
        norm_adds()

    block.__exit__(None, None, None)


def _col_blocks(w, rows, cols):
    w = w.reshape(w.shape[0] // P, P, w.shape[1] // P, P)
    return w[rows][:, :, cols].transpose(1, 2, 0, 3).reshape(P, -1)


def pack_weights(i):
    w = np.zeros((NT, P, TILE), np.float32)
    at = [0]

    def put(a):
        w[at[0], :, :a.shape[1]] = a
        at[0] += 1

    k8 = list(range(DC))
    pw = i["pool_w"][0].reshape(4, 2, P, 2, P)
    put(pw.transpose(2, 0, 1, 3, 4).reshape(P, -1))

    def ffn(l):
        for half in range(2):
            for j in range(half * FH, (half + 1) * FH):
                put(_col_blocks(i["ffn_w_in"][l], k8, [j, FC + j]))
            for m in range(DC):
                put(_col_blocks(i["ffn_w_out"][l], list(range(half * FH, (half + 1) * FH)), [m]))

    def pairs(mat, cols=None):
        cols = cols or list(range(mat.shape[1] // P))
        for j in range(0, len(cols), 2):
            put(_col_blocks(mat, k8, cols[j:j + 2]))

    def mlp(l):
        for half in range(2):
            pairs(i["mlp_w1_2"][l], list(range(half * MH, (half + 1) * MH)))
            for m in range(DC):
                put(_col_blocks(i["mlp_w2_2"][l], list(range(half * MH, (half + 1) * MH)), [m]))

    ffn(0)
    put(_col_blocks(i["w_kv"], k8, [0, 1]))
    put(i["w_kv"][:, 256:].reshape(DC, P, 256).transpose(1, 0, 2).reshape(P, -1))
    pairs(i["w_q"][0])
    pairs(i["w_o"][0])
    ffn(1)
    pairs(i["s5_w_in_2"][0])
    pairs(i["s5_w_glu_2"][0], [c for j in range(DC) for c in (j, DC + j)])
    mlp(0)
    m2 = i["m2_w_in_2"][0]
    dt_cols = np.zeros((D, P), np.float32)
    dt_cols[:, :NH2] = m2[:, DI + XC * P:]
    put(_col_blocks(dt_cols, k8, [0]))
    pairs(m2[:, :DI + XC * P])
    for m in range(DC):
        put(_col_blocks(i["m2_w_out_2"][0], list(range(ZC)), [m]))
    mlp(1)
    assert at[0] == NT, (at[0], NT)
    return w.reshape(NT * P, TILE)


def pack_vecs(i):
    o = np.zeros((P, NV), np.float32)

    def put(name, a):
        c0, n = VECS[name]
        o[:a.shape[0], c0:c0 + n] = a.reshape(a.shape[0], n)

    feat = lambda a: np.asarray(a, np.float32).reshape(-1, P).T
    for name, key in [("mix_pre", "mix_pre_g"), ("mix_post", "mix_post_g"), ("pool_scale", "pool_scale"),
                      ("kv_norm", "kv_norm_g"), ("ffn_pre", "ffn_pre_g"), ("ffn_post", "ffn_post_g"),
                      ("conv_w", "ffn_conv_w"), ("conv_b", "ffn_conv_b"), ("c", "c_2"), ("ada_b", "ada_b_2"),
                      ("norm_mix", "norm_mix_g_2"), ("norm_mlp", "norm_mlp_g_2"), ("final", "final_norm_g_2"),
                      ("s5_d", "s5_d_2"), ("b_glu", "s5_b_glu_2"), ("m2_conv_w", "m2_conv_w_2"),
                      ("m2_conv_b", "m2_conv_b_2"), ("m2_norm", "m2_norm_g_2"),
                      ("lam_re", "s5_lambda_re_2"), ("lam_im", "s5_lambda_im_2")]:
        put(name, feat(i[key]))
    put("log_dt", feat(np.repeat(i["s5_log_dt_2"][0], 64)))
    put("m2_d", feat(np.repeat(i["m2_d_2"][0], 64)))
    put("dt_bias", i["m2_dt_bias_2"][0][:, None])
    put("a_log", i["m2_a_log_2"][0][:, None])
    put("sinks", np.broadcast_to(i["sinks"][0].reshape(4, 2, 2).transpose(0, 2, 1).reshape(1, 16), (P, 16)))
    freq = 1.0 / (np.float32(10000.0) ** (np.arange(0, 64, 2, dtype=np.float32) / np.float32(64)))
    put("inv_freq", np.tile(freq.astype(np.float32), 4)[:, None])
    put("rope_sign", np.where(np.arange(P) % 64 < 32, -1.0, 1.0)[:, None])
    put("tok", np.broadcast_to(np.arange(1, P + 1, dtype=np.float32)[None], (P, P)))
    return o


def shape_constants():
    p = np.arange(P)
    swap = np.zeros((P, P), np.float32)
    swap[(p // 64) * 64 + (p + 32) % 64, p] = 1.0
    edge = np.ones((4, 16), np.float32)
    for g, w in enumerate((2, 4, 8, 16)):
        edge[g] = w / np.minimum(np.arange(1, 17), w)
    qi, kj = p[:, None], np.arange(256)[None]
    rel = P + qi - kj
    valid = (rel >= 0) & (rel < P)
    masks = [np.where(valid & (n * P + kj - P >= 0), 0.0, NEG) for n in (0, 1)]
    upper = np.where(p[None] >= p[:, None], 0.0, NEG)
    return np.concatenate([np.eye(P), swap, np.broadcast_to(edge.reshape(1, -1), (P, 64))] + masks + [upper],
                          axis=1).astype(np.float32)


def arrays(inputs):
    i = {k: np.asarray(a) for k, a in inputs.items()}
    f = lambda a: np.ascontiguousarray(a, dtype=a.dtype)
    ada = i["ada_w_2"].reshape(2, DC, P, ADA // 2, 2, P).transpose(0, 3, 2, 1, 4, 5).reshape(ADA_TILES * P, TILE)
    b = np.zeros((2, 2, 64, 32, 32), np.float32)
    c = np.zeros((2, 2, 64, 32, 32), np.float32)
    for n, part in enumerate(("re", "im")):
        bb = i[f"s5_b_{part}_2"][0].reshape(32, 2, 64, 16)
        cc = i[f"s5_c_{part}_2"][0].transpose(0, 2, 1).reshape(32, 2, 64, 16)
        for g in range(2):
            b[n, g, :, :, 16 * g:16 * g + 16] = bb[:, g].transpose(1, 0, 2)
            c[n, g, :, :, 16 * g:16 * g + 16] = cc[:, g].transpose(1, 0, 2)
    lay = lambda a: np.ascontiguousarray(a.reshape(2, P, 1024).transpose(1, 0, 2).reshape(P, 2048))
    return {
        "weights": pack_weights(i), "ada": f(ada), "vecs": pack_vecs(i), "consts": shape_constants(),
        "x_in": f(i["x"][0].T.reshape(DC, P, T).transpose(1, 0, 2).reshape(P, DC * T)),
        "pos_in": f(np.broadcast_to(i["positions"][0][None], (P, T)).astype(np.int32)),
        "s5_b": lay(b), "s5_c": lay(c),
    }


def kernel(**inputs):
    import concourse.bacc as bacc
    from concourse.bass_utils import run_bass_kernel_spmd

    nc = bacc.Bacc("TRN2", target_bir_lowering=False, num_devices=1)
    ins = arrays(inputs)
    aps = {k: nc.dram_tensor(f"{k}_dram", a.shape, mybir.dt.from_np(a.dtype), kind="ExternalInput").ap()
           for k, a in ins.items()}
    out = nc.dram_tensor("out_dram", (P, DC * T), mybir.dt.float32, kind="ExternalOutput").ap()
    build(nc, **aps, out=out)
    r = run_bass_kernel_spmd(nc, [{f"{k}_dram": a for k, a in ins.items()}], core_ids=[0])
    y = r.results[0]["out_dram"]
    return np.ascontiguousarray(y.reshape(P, DC, T).transpose(2, 1, 0).reshape(1, T, D))
```
